# Optimizing a Trainium2 kernel written in Bass

```python
import math
import jax, jax.numpy as jnp
from jax import lax
import numpy as np

D_MODEL = 1024
BATCH = 1
SEQ = 512
DEPTH = 2
DEC_BATCH = 8
DEC_SEQ = 8
PAST_LEN = 1024
PAGE_SIZE = 128

HEAD_DIM = 64
N_HEADS_FOX = D_MODEL // (2 * HEAD_DIM)
N_HEADS_DIFF = D_MODEL // (4 * HEAD_DIM)
DIFF_VDIM = 2 * HEAD_DIM
FOX_WIDTH = N_HEADS_FOX * HEAD_DIM
DIFF_QK_WIDTH = N_HEADS_DIFF * 2 * HEAD_DIM
DIFF_V_WIDTH = N_HEADS_DIFF * DIFF_VDIM
L0_KV_WIDTH = FOX_WIDTH + DIFF_QK_WIDTH
N_HEADS_DSA = D_MODEL // HEAD_DIM
N_KV_DSA = N_HEADS_DSA // 4
IDX_HEADS = 4
IDX_DIM = 64
TOPK_MAX = 256
D_FF = ((8 * D_MODEL + 3 * 256 - 1) // (3 * 256)) * 256
ROPE_THETA = 10000.0
Q_BLOCK = 128
LAMBDA_INIT = 0.8 - 0.6 * math.exp(-0.3 * 0)
FORGET_BIAS_CENTER = 2.0
EPS = 1e-6
L0_WIDTHS = (FOX_WIDTH, FOX_WIDTH, FOX_WIDTH, N_HEADS_FOX, DIFF_QK_WIDTH, DIFF_QK_WIDTH, DIFF_V_WIDTH)
L1_WIDTHS = (N_HEADS_DSA * HEAD_DIM, N_KV_DSA * HEAD_DIM, N_KV_DSA * HEAD_DIM, IDX_HEADS * IDX_DIM, IDX_DIM, IDX_HEADS)

kernel_name = 'hybrid_fox_diff_dsa_step'

def rms_norm(x, g):
    xf = x.astype(jnp.float32)
    y = xf * lax.rsqrt(jnp.mean(xf * xf, axis=-1, keepdims=True) + EPS)
    return (y * g.astype(jnp.float32)).astype(x.dtype)

def split_cols(x, widths):
    cuts = [int(c) for c in np.cumsum(widths)[:-1]]
    return jnp.split(x, cuts, axis=-1)

def rope(x, pos):
    d = x.shape[-1]
    half = d // 2
    inv = jnp.power(ROPE_THETA, -jnp.arange(half, dtype=jnp.float32) * (2.0 / d))
    ang = pos.astype(jnp.float32)[:, None] * inv[None, :]
    cos = jnp.cos(ang)[:, None, :]
    sin = jnp.sin(ang)[:, None, :]
    xr = x.reshape(x.shape[:2] + (-1, d)).astype(jnp.float32)
    x1, x2 = xr[..., :half], xr[..., half:]
    out = jnp.concatenate([x1 * cos - x2 * sin, x2 * cos + x1 * sin], axis=-1)
    return out.reshape(x.shape).astype(x.dtype)

def swiglu(x, g, w_gate, w_up, w_down):
    h = rms_norm(x, g)
    return (jax.nn.silu(h @ w_gate) * (h @ w_up)) @ w_down

def project0(h, pos, w_in0, b_f0, qn_fox0, kn_fox0, qn_diff0, kn_diff0):
    B, S, _ = h.shape
    qa, ka, va, fa, qb, kb, vb = split_cols(h @ w_in0, L0_WIDTHS)
    qa = rms_norm(qa.reshape(B, S, N_HEADS_FOX, HEAD_DIM), qn_fox0)
    ka = rms_norm(ka.reshape(B, S, N_HEADS_FOX, HEAD_DIM), kn_fox0)
    va = va.reshape(B, S, N_HEADS_FOX, HEAD_DIM)
    logf = jax.nn.log_sigmoid((fa + b_f0).astype(jnp.float32))
    qb = rope(rms_norm(qb.reshape(B, S, N_HEADS_DIFF, 2, HEAD_DIM), qn_diff0), pos)
    kb = rope(rms_norm(kb.reshape(B, S, N_HEADS_DIFF, 2, HEAD_DIM), kn_diff0), pos)
    vb = vb.reshape(B, S, N_HEADS_DIFF, DIFF_VDIM)
    return qa, ka, va, logf, qb, kb, vb

def pack_rows(a, b):
    B, S = a.shape[:2]
    return jnp.concatenate([a.reshape(B, S, -1), b.reshape(B, S, -1)], axis=-1)

def unpack_k(kf):
    lead = kf.shape[:-1]
    return (kf[..., :FOX_WIDTH].reshape(lead + (N_HEADS_FOX, HEAD_DIM)),
            kf[..., FOX_WIDTH:].reshape(lead + (N_HEADS_DIFF, 2, HEAD_DIM)))

def unpack_v(vf):
    lead = vf.shape[:-1]
    return (vf[..., :FOX_WIDTH].reshape(lead + (N_HEADS_FOX, HEAD_DIM)),
            vf[..., FOX_WIDTH:].reshape(lead + (N_HEADS_DIFF, DIFF_VDIM)))

def fox_diff_attend(qa, qb, cq, q_pos, ka, va, ck, kb, vb, k_pos, lam, subln0):
    B, Q = qa.shape[:2]
    causal = k_pos[None, :] <= q_pos[:, None]
    scale = HEAD_DIM ** -0.5
    sa = jnp.einsum('bqhd,bkhd->bhqk', qa, ka).astype(jnp.float32) * scale
    sa = sa + (jnp.swapaxes(cq, 1, 2)[..., :, None] - jnp.swapaxes(ck, 1, 2)[..., None, :])
    pa = jax.nn.softmax(jnp.where(causal, sa, -jnp.inf), axis=-1)
    oa = jnp.einsum('bhqk,bkhd->bqhd', pa.astype(va.dtype), va)
    sb = jnp.einsum('bqhcd,bkhcd->bhcqk', qb, kb).astype(jnp.float32) * scale
    pb = jax.nn.softmax(jnp.where(causal, sb, -jnp.inf), axis=-1)
    diff = pb[:, :, 0] - lam * pb[:, :, 1]
    ob = jnp.einsum('bhqk,bkhe->bqhe', diff.astype(vb.dtype), vb)
    ob = rms_norm(ob, subln0) * (1.0 - LAMBDA_INIT)
    return jnp.concatenate([oa.reshape(B, Q, -1), ob.reshape(B, Q, -1)], axis=-1)

def layer0_prompt(h, pos, w_in0, b_f0, qn_fox0, kn_fox0, qn_diff0, kn_diff0, lam, subln0):
    B, S, _ = h.shape
    qa, ka, va, logf, qb, kb, vb = project0(h, pos, w_in0, b_f0, qn_fox0, kn_fox0, qn_diff0, kn_diff0)
    c = jnp.cumsum(logf, axis=1)

    def block(i):
        s0 = i * Q_BLOCK
        sl = lambda t: lax.dynamic_slice_in_dim(t, s0, Q_BLOCK, axis=1)
        q_pos = lax.dynamic_slice_in_dim(pos, s0, Q_BLOCK)
        return fox_diff_attend(sl(qa), sl(qb), sl(c), q_pos, ka, va, c, kb, vb, pos, lam, subln0)

    out = lax.map(block, jnp.arange(S // Q_BLOCK))
    out = jnp.swapaxes(out, 0, 1).reshape(B, S, -1)
    return out, pack_rows(ka, kb), pack_rows(va, vb), logf.astype(h.dtype)

def layer0_sample(h, pos, cache_k, cache_v, cache_logf, page_table, w_in0, b_f0, qn_fox0, kn_fox0,
                  qn_diff0, kn_diff0, lam, subln0):
    qa, ka, va, logf, qb, kb, vb = project0(h, pos, w_in0, b_f0, qn_fox0, kn_fox0, qn_diff0, kn_diff0)
    k_new = pack_rows(ka, kb)
    v_new = pack_rows(va, vb)
    past = page_table.shape[1] * PAGE_SIZE
    k_pos = jnp.arange(past + h.shape[1])

    def one(args):
        pt, qa_b, qb_b, k_b, v_b, lf_b = args
        k_all = jnp.concatenate([cache_k[pt].reshape(past, L0_KV_WIDTH), k_b], axis=0)
        v_all = jnp.concatenate([cache_v[pt].reshape(past, L0_KV_WIDTH), v_b], axis=0)
        lf_all = jnp.concatenate([cache_logf[pt].reshape(past, N_HEADS_FOX).astype(jnp.float32), lf_b], axis=0)
        c = jnp.cumsum(lf_all, axis=0)[None]
        ka_all, kb_all = unpack_k(k_all[None])
        va_all, vb_all = unpack_v(v_all[None])
        o = fox_diff_attend(qa_b[None], qb_b[None], c[:, past:], pos, ka_all, va_all, c,
                            kb_all, vb_all, k_pos, lam, subln0)
        return o[0]

    out = lax.map(one, (page_table, qa, qb, k_new, v_new, logf))
    return out, k_new, v_new, logf.astype(h.dtype)

def project1(h, pos, w_in1, qn_dsa1, kn_dsa1):
    B, S, _ = h.shape
    q, k, v, qi, ki, wi = split_cols(h @ w_in1, L1_WIDTHS)
    q = rope(rms_norm(q.reshape(B, S, N_HEADS_DSA, HEAD_DIM), qn_dsa1), pos)
    k = rope(rms_norm(k.reshape(B, S, N_KV_DSA, HEAD_DIM), kn_dsa1), pos)
    v = v.reshape(B, S, N_KV_DSA, HEAD_DIM)
    qi = rope(qi.reshape(B, S, IDX_HEADS, IDX_DIM), pos)
    ki = rope(ki[:, :, None, :], pos)[:, :, 0, :]
    return q, k, v, qi, ki, wi

def dsa_select(qi, wi, q_pos, ki, k_pos, k_sel):
    s = jnp.einsum('bqhd,bkd->bqhk', qi, ki).astype(jnp.float32) * (IDX_DIM ** -0.5)
    score = jnp.einsum('bqhk,bqh->bqk', jax.nn.relu(s), wi.astype(jnp.float32)) * (IDX_HEADS ** -0.5)
    score = jnp.where(k_pos[None, None, :] <= q_pos[None, :, None], score, -jnp.inf)
    _, idx = lax.top_k(score, k_sel)
    valid = idx <= q_pos[None, :, None]
    return idx, valid

def dsa_attend(q, k_sel, v_sel, valid):
    B, Q = q.shape[:2]
    qg = q.reshape(B, Q, N_KV_DSA, N_HEADS_DSA // N_KV_DSA, HEAD_DIM)
    s = jnp.einsum('bqgrd,bqkgd->bqgrk', qg, k_sel).astype(jnp.float32) * (HEAD_DIM ** -0.5)
    p = jax.nn.softmax(jnp.where(valid[:, :, None, None, :], s, -jnp.inf), axis=-1)
    o = jnp.einsum('bqgrk,bqkgd->bqgrd', p.astype(v_sel.dtype), v_sel)
    return o.reshape(B, Q, N_HEADS_DSA * HEAD_DIM)

def layer1_prompt(h, pos, w_in1, qn_dsa1, kn_dsa1):
    B, S, _ = h.shape
    q, k, v, qi, ki, wi = project1(h, pos, w_in1, qn_dsa1, kn_dsa1)
    k_sel = min(TOPK_MAX, S // 4)
    take = jax.vmap(lambda rows, ix: rows[ix])

    def block(i):
        s0 = i * Q_BLOCK
        sl = lambda t: lax.dynamic_slice_in_dim(t, s0, Q_BLOCK, axis=1)
        q_pos = lax.dynamic_slice_in_dim(pos, s0, Q_BLOCK)
        idx, valid = dsa_select(sl(qi), sl(wi), q_pos, ki, pos, k_sel)
        return dsa_attend(sl(q), take(k, idx), take(v, idx), valid)

    out = lax.map(block, jnp.arange(S // Q_BLOCK))
    out = jnp.swapaxes(out, 0, 1).reshape(B, S, -1)
    return out, k, v, ki

def layer1_sample(h, pos, cache_k, cache_v, cache_kidx, page_table, w_in1, qn_dsa1, kn_dsa1):
    T = h.shape[1]
    q, k, v, qi, ki, wi = project1(h, pos, w_in1, qn_dsa1, kn_dsa1)
    past = page_table.shape[1] * PAGE_SIZE
    k_pos = jnp.arange(past + T)
    k_sel = min(TOPK_MAX, (past + T) // 4)

    def one(args):
        pt, q_b, k_b, v_b, qi_b, wi_b, ki_b = args
        ki_all = jnp.concatenate([cache_kidx[pt].reshape(past, IDX_DIM), ki_b], axis=0)
        idx, valid = dsa_select(qi_b[None], wi_b[None], pos, ki_all[None], k_pos, k_sel)
        ix = idx[0]
        from_past = (ix < past)[..., None, None]
        ip = jnp.minimum(ix, past - 1)
        page = pt[ip // PAGE_SIZE]
        off = ip % PAGE_SIZE
        inew = jnp.clip(ix - past, 0, T - 1)
        k_s = jnp.where(from_past, cache_k[page, off], k_b[inew])
        v_s = jnp.where(from_past, cache_v[page, off], v_b[inew])
        return dsa_attend(q_b[None], k_s[None], v_s[None], valid)[0]

    out = lax.map(one, (page_table, q, k, v, qi, wi, ki))
    return out, k, v, ki

def setup_inputs(seed: int = 0) -> dict:
    key = jax.random.key(seed)
    ks = iter(jax.random.split(key, 48))
    f32 = jnp.float32

    def normal(shape):
        return jax.random.normal(next(ks), shape, f32)

    def dense(shape):
        return normal(shape) * (shape[0] ** -0.5)

    def gain(n):
        return 1.0 + 0.01 * normal((n,))

    n_pages = PAST_LEN // PAGE_SIZE
    n_used = DEC_BATCH * n_pages
    n_pool = n_used + (n_used + 3) // 4
    d_in0 = sum(L0_WIDTHS)
    d_in1 = sum(L1_WIDTHS)
    inp = {}
    inp['x_prompt'] = normal((BATCH, SEQ, D_MODEL))
    inp['x_sample'] = normal((DEC_BATCH, DEC_SEQ, D_MODEL))
    inp['cache_l0_k'] = normal((n_pool, PAGE_SIZE, L0_KV_WIDTH))
    inp['cache_l0_v'] = normal((n_pool, PAGE_SIZE, L0_KV_WIDTH))
    inp['cache_l0_logf'] = jax.nn.log_sigmoid(FORGET_BIAS_CENTER + normal((n_pool, PAGE_SIZE, N_HEADS_FOX)))
    inp['cache_l1_k'] = normal((n_pool, PAGE_SIZE, N_KV_DSA, HEAD_DIM))
    inp['cache_l1_v'] = normal((n_pool, PAGE_SIZE, N_KV_DSA, HEAD_DIM))
    inp['cache_l1_kidx'] = normal((n_pool, PAGE_SIZE, IDX_DIM))
    inp['page_table'] = jax.random.permutation(next(ks), n_pool)[:n_used].reshape(DEC_BATCH, n_pages).astype(jnp.int32)
    inp['attn_norm0'] = gain(D_MODEL)
    inp['w_in0'] = dense((D_MODEL, d_in0))
    inp['b_f0'] = FORGET_BIAS_CENTER + 0.1 * normal((N_HEADS_FOX,))
    inp['qn_fox0'] = gain(HEAD_DIM)
    inp['kn_fox0'] = gain(HEAD_DIM)
    inp['qn_diff0'] = gain(HEAD_DIM)
    inp['kn_diff0'] = gain(HEAD_DIM)
    inp['lam_q1_0'] = 0.1 * normal((HEAD_DIM,))
    inp['lam_k1_0'] = 0.1 * normal((HEAD_DIM,))
    inp['lam_q2_0'] = 0.1 * normal((HEAD_DIM,))
    inp['lam_k2_0'] = 0.1 * normal((HEAD_DIM,))
    inp['subln0'] = gain(DIFF_VDIM)
    inp['w_out0'] = dense((D_MODEL, D_MODEL))
    inp['ffn_norm0'] = gain(D_MODEL)
    inp['w_gate0'] = dense((D_MODEL, D_FF))
    inp['w_up0'] = dense((D_MODEL, D_FF))
    inp['w_down0'] = dense((D_FF, D_MODEL))
    inp['attn_norm1'] = gain(D_MODEL)
    inp['w_in1'] = dense((D_MODEL, d_in1))
    inp['qn_dsa1'] = gain(HEAD_DIM)
    inp['kn_dsa1'] = gain(HEAD_DIM)
    inp['w_out1'] = dense((D_MODEL, D_MODEL))
    inp['ffn_norm1'] = gain(D_MODEL)
    inp['w_gate1'] = dense((D_MODEL, D_FF))
    inp['w_up1'] = dense((D_MODEL, D_FF))
    inp['w_down1'] = dense((D_FF, D_MODEL))
    return inp

def reference(x_prompt, x_sample, cache_l0_k, cache_l0_v, cache_l0_logf, cache_l1_k, cache_l1_v,
              cache_l1_kidx, page_table, attn_norm0, w_in0, b_f0, qn_fox0, kn_fox0, qn_diff0, kn_diff0,
              lam_q1_0, lam_k1_0, lam_q2_0, lam_k2_0, subln0, w_out0, ffn_norm0, w_gate0, w_up0, w_down0,
              attn_norm1, w_in1, qn_dsa1, kn_dsa1, w_out1, ffn_norm1, w_gate1, w_up1, w_down1):
    yp, ys = x_prompt, x_sample
    pos_p = jnp.arange(x_prompt.shape[1])
    pos_s = page_table.shape[1] * PAGE_SIZE + jnp.arange(x_sample.shape[1])
    for layer in range(DEPTH):
        if layer % 2 == 0:
            lam = (jnp.exp(jnp.sum(lam_q1_0 * lam_k1_0).astype(jnp.float32))
                   - jnp.exp(jnp.sum(lam_q2_0 * lam_k2_0).astype(jnp.float32)) + LAMBDA_INIT)
            mp, p_l0_k, p_l0_v, p_l0_logf = layer0_prompt(
                rms_norm(yp, attn_norm0), pos_p, w_in0, b_f0, qn_fox0, kn_fox0, qn_diff0, kn_diff0, lam, subln0)
            ms, s_l0_k, s_l0_v, s_l0_logf = layer0_sample(
                rms_norm(ys, attn_norm0), pos_s, cache_l0_k, cache_l0_v, cache_l0_logf, page_table,
                w_in0, b_f0, qn_fox0, kn_fox0, qn_diff0, kn_diff0, lam, subln0)
            yp = yp + mp @ w_out0
            ys = ys + ms @ w_out0
            yp = yp + swiglu(yp, ffn_norm0, w_gate0, w_up0, w_down0)
            ys = ys + swiglu(ys, ffn_norm0, w_gate0, w_up0, w_down0)
        else:
            mp, p_l1_k, p_l1_v, p_l1_kidx = layer1_prompt(rms_norm(yp, attn_norm1), pos_p, w_in1, qn_dsa1, kn_dsa1)
            ms, s_l1_k, s_l1_v, s_l1_kidx = layer1_sample(
                rms_norm(ys, attn_norm1), pos_s, cache_l1_k, cache_l1_v, cache_l1_kidx, page_table,
                w_in1, qn_dsa1, kn_dsa1)
            yp = yp + mp @ w_out1
            ys = ys + ms @ w_out1
            yp = yp + swiglu(yp, ffn_norm1, w_gate1, w_up1, w_down1)
            ys = ys + swiglu(ys, ffn_norm1, w_gate1, w_up1, w_down1)
    return (yp, ys, p_l0_k, p_l0_v, p_l0_logf, p_l1_k, p_l1_v, p_l1_kidx,
            s_l0_k, s_l0_v, s_l0_logf, s_l1_k, s_l1_v, s_l1_kidx)


_drawn_inputs = setup_inputs


def setup_inputs(seed=0):
    import zlib

    import numpy as np

    out = dict(_drawn_inputs(seed))
    spreads = {}
    factors = {'attn_norm0': 3.742,
     'qn_fox0': 8.0,
     'kn_fox0': 7.911,
     'qn_diff0': 5.927,
     'kn_diff0': 6.004,
     'subln0': 5.986,
     'ffn_norm0': 5.233,
     'attn_norm1': 5.399,
     'qn_dsa1': 8.0,
     'kn_dsa1': 16.389,
     'ffn_norm1': 35.253}
    for name, (base, spread) in spreads.items():
        noise = np.random.default_rng([zlib.crc32(name.encode()), seed]).standard_normal(out[name].shape)
        drawn = base * np.exp(spread * noise) if base else spread * noise
        out[name] = __import__('jax').numpy.asarray(drawn.astype(out[name].dtype))
    for name, factor in factors.items():
        out[name] = (out[name] * factor).astype(out[name].dtype)
    return out
```

```python
from contextlib import ExitStack
import math

import numpy as np
import concourse.bass as bass
from concourse import mybir

P = 128
D_MODEL, SEQ, DEC_BATCH, DEC_SEQ = 1024, 512, 8, 8
PAST_LEN, PAGE_SIZE, HEAD_DIM = 1024, 128, 64
N_PAGES = PAST_LEN // PAGE_SIZE
SAMP = DEC_BATCH * DEC_SEQ
TOK = SEQ + SAMP
PT = SEQ // P
NT = PT + 1
KC = D_MODEL // P
D_FF = ((8 * D_MODEL + 3 * 256 - 1) // (3 * 256)) * 256
FC = D_FF // P
HALF = HEAD_DIM // 2
FOX = D_MODEL // (2 * HEAD_DIM)
DIFF = D_MODEL // (4 * HEAD_DIM)
HEADS = 16
KVH = 4
IDXH = 4
KEYS = PAST_LEN + DEC_SEQ
BANK = 512
EPS = 1e-6
SCALE = HEAD_DIM ** -0.5
LAMBDA_INIT = 0.8 - 0.6 * math.exp(-0.3 * 0)
NEG = -1e30
TAKEN = -3e38
K_PROMPT, K_SAMPLE = min(256, SEQ // 4), min(256, KEYS // 4)

ALU = mybir.AluOpType
ACT = mybir.ActivationFunctionType
AX = mybir.AxisListType.X
F32 = mybir.dt.float32
I32 = mybir.dt.int32
ds = bass.ds


def rows_of(t):
    return P if t < PT else SAMP


def bc(ap, axis, n):
    shape = list(ap.shape)
    shape.insert(axis, n)
    return ap.unsqueeze(axis).to_broadcast(shape)


def constant_table():
    cols, at = [], {}

    def put(name, a):
        a = np.asarray(a, np.float32)
        full = np.zeros((P, a.shape[1]), np.float32)
        full[:a.shape[0]] = a
        at[name] = (sum(c.shape[1] for c in cols), a.shape[1])
        cols.append(full)

    i = np.arange(P)
    put("ident", np.eye(P))
    put("causal", np.where(i[None, :] <= i[:, None], 0.0, NEG))
    put("step", np.arange(SEQ)[None, :] >= i[:, None])
    row_head, row_query = i // DEC_SEQ, i % DEC_SEQ
    h8 = np.arange(8)
    put("fox_sel", -(h8[:, None] == row_head[None, :]).astype(float))
    put("query_sel", h8[:, None] == row_query[None, :])
    put("new_mask", np.where(h8[None, :] <= row_query[:, None], 0.0, NEG))
    put("idx_sel", (i[:32, None] % DEC_SEQ) == h8[None, :])
    s = np.arange(SAMP)
    put("page_tri", (s[:, None] // N_PAGES == s[None, :] // N_PAGES) & (s[:, None] < s[None, :]))
    put("tok_tri", (s[:, None] // DEC_SEQ == s[None, :] // DEC_SEQ) & (s[:, None] <= s[None, :]))
    put("same_batch", s[:, None] // DEC_SEQ == s[None, :] // DEC_SEQ)
    second = (row_head >= FOX) & (row_head % 2 == 1)
    put("is_first", ~second[:, None])
    put("is_second", -second[:, None].astype(float))
    put("minus_half", np.full((P, 16), -0.5))
    put("ones", np.ones((P, P)))
    pos = np.concatenate([np.arange(SEQ), np.tile(PAST_LEN + np.arange(DEC_SEQ), DEC_BATCH), np.zeros(SAMP)])
    expo = -np.arange(HALF, dtype=np.float32) * np.float32(2.0 / HEAD_DIM)
    inv = np.power(np.float32(10000.0), expo).astype(np.float32)
    ang = (pos.astype(np.float32)[:, None] * inv[None, :]).astype(np.float64)
    tile = lambda a: a.reshape(NT, P, HALF).transpose(1, 0, 2).reshape(P, NT * HALF)
    put("cos", tile(np.cos(ang)))
    put("sin", tile(np.sin(ang)))
    put("minus_sin", tile(-np.sin(ang)))
    return np.ascontiguousarray(np.concatenate(cols, axis=1)), at


CONST, CONST_AT = constant_table()


class Steps:

    def __init__(self, eng, sem, before=0):
        self.eng, self.sem, self.before, self.n = eng, sem, before, 0

    def ok(self, ins):
        self.n += 1
        return ins.then_inc(self.sem, 1)

    def wait(self):
        self.eng.wait_ge(self.sem, self.before + self.n)


class Kernel:
    pass


class Weights:

    def __init__(self, K, sem):
        self.K, self.tiles, self.issued, self.counts, self.landed = K, [], 0, [0, 0], []
        self.sem_landed = [sem("weights_landed_0"), sem("weights_landed_1")]
        self.used = {}

    def add(self, parts):
        n = len(self.tiles)
        pieces = parts(self.slot(n))
        self.tiles.append(pieces)
        self.counts[n % 2] += 16 * len(pieces)
        self.landed.append(self.counts[n % 2])
        return n

    def slot(self, n):
        return self.K.wslot[:, n % 2, :]

    def load_up_to(self, sp, last):
        while self.issued <= min(last, len(self.tiles) - 1):
            n = self.issued
            if n >= 2:
                sp.wait_ge(*self.used[n - 2])
            for dst, src in self.tiles[n]:
                sp.dma_start(dst, src).then_inc(self.sem_landed[n % 2], 16)
            self.issued += 1

    def arrived(self, eng, n, more=0):
        eng.wait_ge(self.sem_landed[n % 2], self.landed[n] + more)


def column_tile(w, k0, kn, c0, cn):
    def parts(slot):
        view = slot[:, 0:kn * cn].rearrange("p (k n) -> p k n", k=kn)
        return [(view, w[k0 * P:(k0 + kn) * P, c0:c0 + cn].rearrange("(k p) n -> p k n", p=P))]
    return parts


def gate_up_tile(wg, wu, c0):
    def parts(slot):
        view = slot.rearrange("p (a k n) -> p a k n", a=2, k=KC)
        return [(view[:, a], w[:, c0:c0 + 256].rearrange("(k p) n -> p k n", p=P)) for a, w in enumerate((wg, wu))]
    return parts


def load_inputs(nc, K):
    dma, small = K.sem("tokens_landed"), K.sem("small_landed")
    with nc.Block() as block:
        @block.sync
        def _(sp):
            sp.dma_start(K.resid[:, 0:PT, :], K.x_prompt[0].rearrange("(t p) d -> p t d", p=P)).then_inc(dma, 16)
            sp.dma_start(K.resid[0:SAMP, PT, :], K.x_sample.rearrange("b t d -> (b t) d")).then_inc(dma, 16)
            sp.dma_start(K.const[:, :], K.const_in).then_inc(dma, 16)
            K.weights.load_up_to(sp, 1)
            sp.wait_ge(dma, 48)

        @block.scalar
        def _(act):
            pairs = [(K.head_gain[:, i, :], g.partition_broadcast(P)) for i, g in enumerate(K.head_gains)]
            pairs += [(K.subln_row[:, :], K.subln0.partition_broadcast(P)),
                      (K.bias_f[:, :], K.b_f0.partition_broadcast(P)),
                      (K.pages[:, :], K.page_table.rearrange("(a b) n -> a (b n)", a=1)),
                      (K.page_rows[:, :], K.page_table.rearrange("b (n a) -> (b n) a", a=1)),
                      (K.subln_col[:, :], K.subln0.rearrange("(p a) -> p a", a=1))]
            pairs += [(K.lams[:, i, :], g.partition_broadcast(P)) for i, g in enumerate(K.lam_vecs)]
            with nc.allow_non_contiguous_dma(reason="gains by feature: 16 KB once"):
                for i, g in enumerate(K.norm_gains):
                    pairs.append((K.gain_cols[:, i, :], g.rearrange("(c p) -> p c", p=P)))
                for dst, src in pairs:
                    act.dma_start(dst, src).then_inc(small, 16)
            act.wait_ge(small, 16 * len(pairs))


def norm_to_features(nc, K, gain, tag):
    squared, mean_ok, rstd_ok, scaled = (K.sem(f"{tag}_{x}") for x in ("squared", "mean_ok", "rstd_ok", "scaled"))
    turned, out_act, out_dve = (K.sem(f"{tag}_{x}") for x in ("turned", "out_act", "out_dve"))
    with ExitStack() as mem:
        sb = lambda name, shape: mem.enter_context(nc.sbuf_tensor(f"{tag}_{name}", shape, F32))
        square = sb("square", [P, D_MODEL])
        ms = sb("ms", [P, NT])
        rstd = sb("rstd", [P, NT])
        xn = sb("xn", [P, 2, D_MODEL])
        block = mem.enter_context(nc.Block())

        def out_of_psum(half, eng):
            for t in range(NT):
                n = rows_of(t)
                yield t
                eng.wait_ge(turned, 2 * t + half + 1)
                for j in range(4):
                    c = 4 * half + j
                    src = K.ps[:, (2 * t + half) % 4, j * P:j * P + n]
                    dst = K.feat[:, c, t * P:t * P + n]
                    g = K.gain_cols[:, gain, c:c + 1]
                    if half:
                        ins = eng.tensor_scalar(dst, src, g, None, ALU.mult)
                    else:
                        ins = eng.activation(dst, src, ACT.Copy, scale=g)
                ins.then_inc(out_dve if half else out_act, 1)

        @block.scalar
        def _(act):
            for t in range(NT):
                n = rows_of(t)
                if t:
                    act.wait_ge(squared, t)
                act.activation(square[0:n, :], K.resid[0:n, t, :], ACT.Square,
                               accum_out=ms[0:n, t:t + 1]).then_inc(squared, 1)
            for _t in out_of_psum(0, act):
                pass

        @block.gpsimd
        def _(pool):
            for t in range(NT):
                n = rows_of(t)
                pool.wait_ge(mean_ok, t + 1)
                pool.tensor_tensor(rstd[0:n, t:t + 1], ms[0:n, t:t + 1], K.c("minus_half")[0:n, 0:1],
                                   ALU.pow).then_inc(rstd_ok, 1)

        @block.vector
        def _(dve):
            for t in range(NT):
                n = rows_of(t)
                dve.wait_ge(squared, t + 1)
                dve.tensor_scalar(ms[0:n, t:t + 1], ms[0:n, t:t + 1], 1.0 / D_MODEL, EPS, ALU.mult, ALU.add)\
                   .then_inc(mean_ok, 1)
            out = out_of_psum(1, dve)
            for t in range(NT):
                n = rows_of(t)
                dve.wait_ge(rstd_ok, t + 1)
                if t >= 2:
                    dve.wait_ge(turned, 2 * (t - 1))
                dve.tensor_scalar(xn[0:n, t % 2, :], K.resid[0:n, t, :], rstd[0:n, t:t + 1], None, ALU.mult)\
                   .then_inc(scaled, 1)
                if t >= 1:
                    next(out)
            for _t in out:
                pass

        @block.tensor
        def _(pe):
            for t in range(NT):
                n = rows_of(t)
                pe.wait_ge(scaled, t + 1)
                for half, freed in ((0, out_act), (1, out_dve)):
                    if t >= 2:
                        pe.wait_ge(freed, t - 1)
                    for j in range(4):
                        c = 4 * half + j
                        ins = pe.transpose(K.ps[:, (2 * t + half) % 4, j * P:j * P + n],
                                           xn[0:n, t % 2, c * P:(c + 1) * P], K.c("ident")[0:n, 0:n])
                    ins.then_inc(turned, 1)


class Part:

    def __init__(self, tile, width, heads=0, norm=None, rope=False, stores=(), turns=(), copies=(), paired=False):
        self.paired = paired
        self.tile, self.width, self.heads, self.norm, self.rope = tile, width, heads, norm, rope
        self.stores, self.turns, self.copies = stores, turns, copies


class Item:

    def __init__(self, part, t):
        self.p, self.t, self.rows = part, t, rows_of(t)
        self.norm = self.head = self.ready = self.copy = None


def project(nc, K, parts, tag):
    names = ("multiplied", "squared", "mean_ok", "rstd_ok", "gained", "psum_free", "roped", "turned",
             "turned_out", "copied", "chain", "copies_stored")
    S = {n: K.sem(f"{tag}_{n}") for n in names}
    stored = [K.sem(f"{tag}_stored_{i}") for i in range(3)]
    items = [(p, t) for p in parts for t in range(NT)]
    n_norm = n_rope = n_head = n_copy = 0
    info = []
    for p, t in items:
        it = Item(p, t)
        if p.heads:
            it.head = n_head
            n_head += 1
            if p.norm is not None:
                it.norm = n_norm
                n_norm += 1
            if p.rope:
                n_rope += 1
                it.ready = (S["roped"], n_rope)
            else:
                it.ready = (S["gained"], n_norm)
        if p.copies:
            it.copy = n_copy
            n_copy += 1
        info.append(it)
    store_count = [0, 0, 0]
    for it in info:
        it.store_before = None
        if it.head is not None:
            it.store_before = store_count[it.head % 3]
            if it.p.stores:
                store_count[it.head % 3] += 16
    for i, p in enumerate(parts):
        K.weights.used[p.tile] = (S["multiplied"], NT * (i + 1))
    copy_stores = sum(len([c for c in it.p.copies if c[2 if it.t < PT else 3] is not None]) for it in info)
    heads = [it for it in info if it.head is not None]

    with ExitStack() as mem:
        sb = lambda name, shape: mem.enter_context(nc.sbuf_tensor(f"{tag}_{name}", shape, F32))
        square = sb("square", [P, 2, BANK])
        ms = sb("ms", [P, 2, 8])
        rstd = sb("rstd", [P, 2, 8])
        xn = sb("xn", [P, 2, BANK])
        straight = sb("straight", [P, BANK])
        crossed = sb("crossed", [P, BANK])
        res = sb("res", [P, 3, BANK])
        block = mem.enter_context(nc.Block())

        def res_free(eng, it):
            if it.head >= 3:
                eng.wait_ge(S["turned"], it.head - 2)
                if it.store_before:
                    eng.wait_ge(stored[it.head % 3], it.store_before)

        @block.sync
        def _(sp):
            K.weights.load_up_to(sp, parts[-1].tile + 2)

        @block.tensor
        def _(pe):
            def turn(it):
                pe.wait_ge(*it.ready)
                if it.head >= 2:
                    pe.wait_ge(S["turned_out"], it.head - 1)
                for j, (src, _, _) in enumerate(it.p.turns):
                    n = it.rows
                    ins = pe.transpose(K.ps[:, 4 + it.head % 2, j * P:j * P + n], src(res[0:n, it.head % 3, :]),
                                       K.c("ident")[0:n, 0:n])
                ins.then_inc(S["turned"], 1)

            for i, it in enumerate(info):
                n, p = it.rows, it.p
                if it.t == 0:
                    K.weights.arrived(pe, p.tile)
                if i >= 4:
                    pe.wait_ge(S["psum_free"], i - 3)
                w = K.weights.slot(p.tile)[:, 0:KC * p.width].rearrange("p (k n) -> p k n", k=KC)
                for k in range(KC):
                    ins = pe.matmul(K.ps[0:n, i % 4, 0:p.width], K.feat[:, k, it.t * P:it.t * P + n],
                                    w[:, k, :], start=(k == 0), stop=(k == KC - 1))
                ins.then_inc(S["multiplied"], 1)
                if i >= 2 and info[i - 2].head is not None:
                    turn(info[i - 2])
            for it in info[-2:]:
                if it.head is not None:
                    turn(it)

        @block.scalar
        def _(act):
            def turn_out(it):
                act.wait_ge(S["turned"], it.head + 1)
                n = it.rows
                todo = it.p.turns
                for j, (_, dst, scale) in enumerate(todo):
                    src = K.ps[:, 4 + it.head % 2, j * P:j * P + n]
                    ins = act.activation(dst(it.t), src, ACT.Copy, scale=scale)
                ins.then_inc(S["turned_out"], 1)

            def store(it):
                act.wait_ge(*it.ready)
                for sl, dst in it.p.stores:
                    act.dma_start(dst(it.t), res[0:it.rows, it.head % 3, sl]).then_inc(stored[it.head % 3], 16)

            def store_copies(it):
                act.wait_ge(S["copied"], it.copy + 1)
                for c in it.p.copies:
                    dram = c[2 if it.t < PT else 3]
                    if dram is not None:
                        act.dma_start(dram(it.t), c[1](it.t)).then_inc(S["copies_stored"], 16)

            def after(i):
                if i >= 1:
                    it = info[i - 1]
                    if it.p.stores:
                        store(it)
                    if it.copy is not None:
                        store_copies(it)
                if i >= 2 and info[i - 2].head is not None:
                    turn_out(info[i - 2])

            for i, it in enumerate(info):
                if it.norm is not None:
                    act.wait_ge(S["multiplied"], i + 1)
                    if it.norm >= 2:
                        act.wait_ge(S["mean_ok"], it.norm - 1)
                    act.activation(square[0:it.rows, it.norm % 2, 0:it.p.heads], K.ps[0:it.rows, i % 4, 0:it.p.heads],
                                   ACT.Square).then_inc(S["squared"], 1)
                after(i)
            after(len(info))
            if info[-1].head is not None:
                turn_out(info[-1])
            for s, n in zip(stored, store_count):
                if n:
                    act.wait_ge(s, n)
            if copy_stores:
                act.wait_ge(S["copies_stored"], 16 * copy_stores)

        @block.gpsimd
        def _(pool):
            for it in heads:
                if it.norm is None:
                    continue
                n, m, nh = it.rows, it.norm, it.p.heads // HEAD_DIM
                pool.wait_ge(S["mean_ok"], m + 1)
                pool.tensor_tensor(rstd[0:n, m % 2, 0:nh], ms[0:n, m % 2, 0:nh], K.c("minus_half")[0:n, 0:nh],
                                   ALU.pow).then_inc(S["rstd_ok"], 1)
                pool.wait_ge(S["psum_free"], info.index(it) + 1)
                view = xn[0:n, m % 2, 0:it.p.heads].rearrange("p (h d) -> p h d", d=HEAD_DIM)
                gain = bc(K.head_gain[0:n, it.p.norm, :], 1, nh)
                if it.p.rope:
                    dst = view
                else:
                    res_free(pool, it)
                    dst = res[0:n, it.head % 3, 0:it.p.heads].rearrange("p (h d) -> p h d", d=HEAD_DIM)
                pool.tensor_tensor(dst, view, gain, ALU.mult).then_inc(S["gained"], 1)

        @block.vector
        def _(dve):
            s = Steps(dve, S["chain"])
            for i, it in enumerate(info):
                n, p, t = it.rows, it.p, it.t
                ps = K.ps[0:n, i % 4, :]
                nh = p.heads // HEAD_DIM
                if it.norm is not None:
                    m = it.norm
                    dve.wait_ge(S["squared"], m + 1)
                    if m >= 2:
                        dve.wait_ge(S["rstd_ok"], m - 1)
                    s.ok(dve.tensor_reduce(ms[0:n, m % 2, 0:nh],
                                           square[0:n, m % 2, 0:p.heads].rearrange("p (h d) -> p h d", d=HEAD_DIM),
                                           AX, ALU.add))
                    s.wait()
                    dve.tensor_scalar(ms[0:n, m % 2, 0:nh], ms[0:n, m % 2, 0:nh], 1.0 / HEAD_DIM, EPS,
                                      ALU.mult, ALU.add).then_inc(S["mean_ok"], 1)
                else:
                    dve.wait_ge(S["multiplied"], i + 1)
                if p.copies:
                    for k, (sl, dst, _, _, how) in enumerate(p.copies):
                        ins = how(dve, dst(t), ps[:, sl], s) if how else dve.tensor_copy(dst(t), ps[:, sl])
                        if k < len(p.copies) - 1:
                            s.ok(ins)
                    ins.then_inc(S["copied"], 1)
                src = None
                if it.norm is not None:
                    dve.wait_ge(S["rstd_ok"], m + 1)
                    if m >= 2:
                        dve.wait_ge(S["gained"], m - 1)
                    if p.rope and m >= 2:
                        s.wait()
                    src = xn[0:n, m % 2, 0:p.heads].rearrange("p (h d) -> p h d", d=HEAD_DIM)
                    dve.tensor_tensor(src, ps[:, 0:p.heads].rearrange("p (h d) -> p h d", d=HEAD_DIM),
                                      bc(rstd[0:n, m % 2, 0:nh], 2, HEAD_DIM), ALU.mult).then_inc(S["psum_free"], 1)
                    if p.rope:
                        dve.wait_ge(S["gained"], m + 1)
                elif p.heads:
                    src = ps[:, 0:p.heads].rearrange("p (h d) -> p h d", d=HEAD_DIM)
                if p.rope:
                    four = src.rearrange("p h (a d) -> p h a d", a=2)
                    st = straight[0:n, 0:p.heads].rearrange("p (h a d) -> p h a d", a=2, d=HALF)
                    cr = crossed[0:n, 0:p.heads].rearrange("p (h a d) -> p h a d", a=2, d=HALF)
                    cos, sin, msin = (K.c(x)[0:n, t * HALF:(t + 1) * HALF] for x in ("cos", "sin", "minus_sin"))
                    s.wait()
                    for a in range(2):
                        s.ok(dve.tensor_tensor(st[:, :, a, :], four[:, :, a, :], bc(cos, 1, nh), ALU.mult))
                    s.ok(dve.tensor_tensor(cr[:, :, 0, :], four[:, :, 1, :], bc(msin, 1, nh), ALU.mult))
                    ins = dve.tensor_tensor(cr[:, :, 1, :], four[:, :, 0, :], bc(sin, 1, nh), ALU.mult)
                    if it.norm is None:
                        ins.then_inc(S["psum_free"], 1)
                        dve.wait_ge(S["psum_free"], i + 1)
                    else:
                        s.ok(ins)
                    s.wait()
                    res_free(dve, it)
                    if p.heads == 5 * HEAD_DIM:
                        s.ok(dve.tensor_tensor(res[0:n, it.head % 3, p.heads:p.heads + HEAD_DIM],
                                               straight[0:n, p.heads - HEAD_DIM:p.heads],
                                               crossed[0:n, p.heads - HEAD_DIM:p.heads], ALU.add))
                        s.wait()
                    dst, a, b = res[0:n, it.head % 3, 0:p.heads], straight[0:n, 0:p.heads], crossed[0:n, 0:p.heads]
                    if p.paired:
                        dst = dst.rearrange("p (r a d) -> p a r d", a=2, d=HEAD_DIM)
                        a, b = (x.rearrange("p (a r d) -> p a r d", a=2, d=HEAD_DIM) for x in (a, b))
                    dve.tensor_tensor(dst, a, b, ALU.add).then_inc(S["roped"], 1)
                    dve.wait_ge(*it.ready)
                elif not p.heads:
                    dve.wait_ge(S["copied"], it.copy + 1)
                    dve.sem_inc(S["psum_free"], 1)


def forget_sums(nc, K):
    S = {n: K.sem("sums_" + n) for n in ("chain", "scanned", "summed", "out", "scratch", "broadcast", "lam_sum", "lam_exp")}
    S["pages_in"] = nc.alloc_semaphore(name="sums_pages_in")
    with ExitStack() as mem:
        sb = lambda name, shape: mem.enter_context(nc.sbuf_tensor("sums_" + name, shape, F32))
        page_logf = sb("page_logf", [SAMP, PAGE_SIZE * FOX])
        page_cum = sb("page_cum", [SAMP, FOX, PAGE_SIZE])
        zero = sb("zero", [SAMP, PAGE_SIZE])
        total = sb("total", [SAMP, FOX])
        carry = sb("carry", [SAMP, FOX])
        prompt_row = sb("prompt_row", [FOX, SEQ])
        new_row = sb("new_row", [FOX, SAMP])
        prod = sb("prod", [P, HEAD_DIM])
        lam_sum = sb("lam_sum", [P, 2])
        lam_exp = sb("lam_exp", [P, 2])
        block = mem.enter_context(nc.Block())
        CP, CARRY, NEW = K.ps[0:FOX, 0, :], K.ps[0:SAMP, 1, 0:FOX], K.ps[0:FOX, 2, 0:SAMP]
        scr = K.fox_rows

        @block.gpsimd
        def _(pool):
            pool.indirect_dma_start(page_logf[:, :], None, K.cache_l0_logf.rearrange("n k h -> n (k h)"),
                                    bass.IndirectOffsetOnAxis(ap=K.page_rows[:, 0:1], axis=0)).then_inc(S["pages_in"], 16)

        @block.tensor
        def _(pe):
            for t in range(PT):
                ins = pe.matmul(CP[:, t * P:SEQ], K.logf[:, t, :], K.c("step")[:, 0:SEQ - t * P],
                                start=(t == 0), stop=(t == PT - 1))
            ins.then_inc(S["summed"], 1)
            pe.wait_ge(S["scanned"], 1)
            pe.matmul(CARRY, K.c("page_tri")[0:SAMP, :], total[:, :], start=True, stop=True).then_inc(S["summed"], 1)
            pe.matmul(NEW, K.logf[0:SAMP, PT, :], K.c("tok_tri")[0:SAMP, :], start=True, stop=False)
            pe.matmul(NEW, total[:, :], K.c("same_batch")[0:SAMP, :], start=False, stop=True).then_inc(S["summed"], 1)

        @block.scalar
        def _(act):
            act.wait_ge(S["lam_sum"], 2)
            act.activation(lam_exp[:, :], lam_sum[:, :], ACT.Exp).then_inc(S["lam_exp"], 1)

        @block.vector
        def _(dve):
            s = Steps(dve, S["chain"])
            s.ok(dve.memset(zero[:, :], 0.0))
            for i in range(2):
                if i:
                    dve.wait_ge(S["lam_sum"], 1)
                dve.tensor_tensor_reduce(prod[:, :], K.lams[:, 2 * i, :], K.lams[:, 2 * i + 1, :], 1.0, 0.0,
                                         ALU.mult, ALU.add, lam_sum[:, i:i + 1]).then_inc(S["lam_sum"], 1)
            dve.wait_ge(S["summed"], 1)
            dve.tensor_scalar(prompt_row[:, :], CP, -1.0, None, ALU.mult).then_inc(S["out"], 1)
            dve.wait_ge(S["pages_in"], 16)
            s.wait()
            by_head = page_logf[:, :].rearrange("p (k h) -> p h k", h=FOX)
            for h in range(FOX):
                s.ok(dve.tensor_tensor_scan(page_cum[:, h, :], by_head[:, h, :], zero[:, :], 0.0, ALU.add, ALU.add))
            s.wait()
            dve.tensor_copy(total[:, :], page_cum[:, :, PAGE_SIZE - 1]).then_inc(S["scanned"], 1)
            dve.wait_ge(S["summed"], 2)
            s.ok(dve.tensor_copy(carry[:, :], CARRY))
            s.wait()
            dve.wait_ge(S["scanned"], 1)
            dve.tensor_tensor(page_cum[:, :, :], page_cum[:, :, :], bc(carry[:, :], 2, PAGE_SIZE), ALU.add)\
               .then_inc(S["out"], 1)
            dve.wait_ge(S["summed"], 3)
            dve.tensor_copy(new_row[:, :], NEW).then_inc(S["out"], 1)
            dve.wait_ge(S["lam_exp"], 1)
            s.ok(dve.tensor_scalar(K.lam[:, :], lam_exp[:, 0:1], lam_exp[:, 1:2], LAMBDA_INIT, ALU.subtract, ALU.add))
            s.wait()
            s.ok(dve.tensor_scalar(K.coef[:, :], K.c("is_second"), K.lam[:, 0:1], K.c("is_first"),
                                   ALU.mult, ALU.add))
            s.ok(dve.tensor_scalar(K.minus_lam[:, :], K.lam[:, :], -1.0, None, ALU.mult))
            s.ok(dve.tensor_scalar(K.subln_col8[:, :], K.subln_col[:, :], 1.0 - LAMBDA_INIT, None, ALU.mult))
            s.ok(dve.tensor_scalar(K.subln_row8[:, :], K.subln_row[:, :], 1.0 - LAMBDA_INIT, None, ALU.mult))
            s.wait()

        @block.sync
        def _(sp):
            sp.wait_ge(S["out"], 1)
            sp.dma_start(K.prompt_rows, prompt_row[:, :]).then_inc(S["scratch"], 16)
            sp.wait_ge(S["scratch"], 16)
            sp.dma_start(K.minus_c[:, :, :], K.prompt_rows.partition_broadcast(P)).then_inc(S["broadcast"], 16)
            sp.wait_ge(S["out"], 2)
            for b in range(DEC_BATCH):
                dst = scr[b, :, 0:PAST_LEN].rearrange("h (j k) -> j h k", j=N_PAGES)
                sp.dma_start(dst, page_cum[b * N_PAGES:(b + 1) * N_PAGES, :, :]).then_inc(S["scratch"], 16)
            sp.wait_ge(S["out"], 3)
            sp.dma_start(scr[:, :, PAST_LEN:KEYS].rearrange("b h t -> h b t"),
                         new_row[:, :].rearrange("h (b t) -> h b t", b=DEC_BATCH)).then_inc(S["scratch"], 16)
            sp.wait_ge(S["scratch"], 16 * (2 + DEC_BATCH))
            sp.wait_ge(S["broadcast"], 16)


def prompt_attention(nc, K, tag, q_at, k_at, v_at, bias_at, diag, out_at, second):
    names = ("scored", "shifted", "exped", "turned", "turned_out", "weighed", "out", "chain")
    S = {n: K.sem(f"{tag}_{n}") for n in names}
    units = [(h, qt) for h in range(HEADS) for qt in range(PT)]
    n = len(units)
    with ExitStack() as mem:
        sb = lambda name, shape: mem.enter_context(nc.sbuf_tensor(f"{tag}_{name}", shape, F32))
        scores = sb("scores", [P, 3, SEQ])
        probs = sb("probs", [P, 3, SEQ])
        probs_t = sb("probs_t", [P, 3, SEQ])
        top, minus, total, scale, scale2 = (sb(x, [P, n]) for x in ("top", "minus", "total", "scale", "scale2"))
        block = mem.enter_context(nc.Block())

        @block.tensor
        def _(pe):
            for u in range(n + 3):
                if u < n:
                    h, qt = units[u]
                    if u >= 3:
                        pe.wait_ge(S["exped"], u - 2)
                    w = (qt + 1) * P
                    pe.matmul(K.ps[:, u % 3, 0:w], q_at(h, qt), k_at(h)[:, 0:w], start=True, stop=True)\
                      .then_inc(S["scored"], 1)
                if 2 <= u < n + 2:
                    v = u - 2
                    pe.wait_ge(S["exped"], v + 1)
                    if v >= 3:
                        pe.wait_ge(S["turned_out"], v - 2)
                    for j in range(units[v][1] + 1):
                        ins = pe.transpose(K.ps[:, 3 + v % 3, j * P:(j + 1) * P], probs[:, v % 3, j * P:(j + 1) * P],
                                           K.c("ident"))
                    ins.then_inc(S["turned"], 1)
                if u >= 3:
                    v = u - 3
                    h, qt = units[v]
                    pe.wait_ge(S["turned_out"], v + 1)
                    if v >= 2:
                        pe.wait_ge(S["out"], v - 1)
                    for j in range(qt + 1):
                        val = v_at(h, j)
                        ins = pe.matmul(K.ps[:, 6 + v % 2, 0:val.shape[1]], probs_t[:, v % 3, j * P:(j + 1) * P], val,
                                        start=(j == 0), stop=(j == qt))
                    ins.then_inc(S["weighed"], 1)

        @block.scalar
        def _(act):
            for u in range(n + 2):
                if u < n:
                    h, qt = units[u]
                    w = (qt + 1) * P
                    act.wait_ge(S["shifted"], u + 1)
                    if u >= 3:
                        act.wait_ge(S["turned"], u - 2)
                    src = scores[:, u % 3, 0:w] if bias_at(h, qt) is not None else K.ps[:, u % 3, 0:w]
                    act.activation(probs[:, u % 3, 0:w], src, ACT.Exp, bias=minus[:, u:u + 1],
                                   accum_out=total[:, u:u + 1]).then_inc(S["exped"], 1)
                if u >= 2:
                    v = u - 2
                    w = (units[v][1] + 1) * P
                    act.wait_ge(S["turned"], v + 1)
                    if v >= 3:
                        act.wait_ge(S["weighed"], v - 2)
                    act.activation(probs_t[:, v % 3, 0:w], K.ps[:, 3 + v % 3, 0:w], ACT.Copy).then_inc(S["turned_out"], 1)

        @block.vector
        def _(dve):
            s = Steps(dve, S["chain"])
            for u in range(n + 3):
                if u < n:
                    h, qt = units[u]
                    w = (qt + 1) * P
                    ps = K.ps[:, u % 3, 0:w]
                    dve.wait_ge(S["scored"], u + 1)
                    if diag:
                        s.ok(dve.tensor_tensor(ps[:, qt * P:w], ps[:, qt * P:w], K.c("causal"), ALU.add))
                        s.wait()
                    bias = bias_at(h, qt)
                    if bias is not None:
                        if u >= 3:
                            dve.wait_ge(S["exped"], u - 2)
                        s.ok(dve.tensor_tensor_reduce(scores[:, u % 3, 0:w], ps, bias, 1.0, -3e38, ALU.add, ALU.max,
                                                      top[:, u:u + 1]))
                        s.wait()
                        dve.tensor_scalar(minus[:, u:u + 1], top[:, u:u + 1], -1.0, None, ALU.mult)\
                           .then_inc(S["shifted"], 1)
                    else:
                        dve.tensor_reduce(minus[:, u:u + 1], ps, AX, ALU.max, negate=True).then_inc(S["shifted"], 1)
                if u >= 3:
                    v = u - 3
                    h, qt = units[v]
                    dve.wait_ge(S["exped"], v + 1)
                    s.ok(dve.reciprocal(scale[:, v:v + 1], total[:, v:v + 1]))
                    s.wait()
                    dst = out_at(h, qt)
                    acc = K.ps[:, 6 + v % 2, 0:dst.shape[1]]
                    if second(h):
                        s.ok(dve.tensor_scalar(scale2[:, v:v + 1], scale[:, v:v + 1], K.minus_lam[:, 0:1], None,
                                               ALU.mult))
                        s.wait()
                        dve.wait_ge(S["weighed"], v + 1)
                        dve.wait_ge(S["out"], v + 1 - PT)
                        dve.scalar_tensor_tensor(out=dst, in0=acc, scalar=scale2[:, v:v + 1], in1=dst,
                                                 op0=ALU.mult, op1=ALU.add).then_inc(S["out"], 1)
                    else:
                        dve.wait_ge(S["weighed"], v + 1)
                        dve.tensor_scalar(dst, acc, scale[:, v:v + 1], None, ALU.mult).then_inc(S["out"], 1)


def turn_attention(nc, K, att, tag, subln):
    S = {n: K.sem(f"{tag}_{n}") for n in ("squared", "mean_ok", "rstd_ok", "normed", "chain", "turned", "out_act", "out_dve")}
    with ExitStack() as mem:
        sb = lambda name, shape: mem.enter_context(nc.sbuf_tensor(f"{tag}_{name}", shape, F32))
        if subln:
            square = sb("square", [P, 2, DIFF * P])
            ms = sb("ms", [P, PT, DIFF])
            rstd = sb("rstd", [P, PT, DIFF])
        block = mem.enter_context(nc.Block())

        @block.tensor
        def _(pe):
            for t in range(PT):
                for half, freed in ((0, S["out_act"]), (1, S["out_dve"])):
                    if subln and half:
                        pe.wait_ge(S["normed"], t + 1)
                    if t >= 2:
                        pe.wait_ge(freed, t - 1)
                    for j in range(4):
                        c = 4 * half + j
                        ins = pe.transpose(K.ps[:, 2 * (t % 2) + half, j * P:(j + 1) * P], att[:, t, c * P:(c + 1) * P],
                                           K.c("ident"))
                    ins.then_inc(S["turned"], 1)

        @block.scalar
        def _(act):
            if subln:
                for t in range(PT):
                    if t >= 2:
                        act.wait_ge(S["mean_ok"], t - 1)
                    act.activation(square[:, t % 2, :], att[:, t, BANK:], ACT.Square).then_inc(S["squared"], 1)
            for t in range(PT):
                act.wait_ge(S["turned"], 2 * t + 1)
                act.activation(K.feat[:, 0:4, t * P:(t + 1) * P],
                               K.ps[:, 2 * (t % 2), :].rearrange("p (c n) -> p c n", c=4), ACT.Copy)\
                   .then_inc(S["out_act"], 1)

        @block.gpsimd
        def _(pool):
            if subln:
                for t in range(PT):
                    pool.wait_ge(S["mean_ok"], t + 1)
                    pool.tensor_tensor(rstd[:, t, :], ms[:, t, :], K.c("minus_half")[:, 0:DIFF], ALU.pow)\
                        .then_inc(S["rstd_ok"], 1)

        @block.vector
        def _(dve):
            s = Steps(dve, S["chain"])
            if subln:
                for t in range(PT):
                    dve.wait_ge(S["squared"], t + 1)
                    s.ok(dve.tensor_reduce(ms[:, t, :], square[:, t % 2, :].rearrange("p (h d) -> p h d", h=DIFF),
                                           AX, ALU.add))
                    s.wait()
                    dve.tensor_scalar(ms[:, t, :], ms[:, t, :], 1.0 / P, EPS, ALU.mult, ALU.add).then_inc(S["mean_ok"], 1)
                for t in range(PT):
                    view = att[:, t, BANK:].rearrange("p (h d) -> p h d", h=DIFF)
                    dve.wait_ge(S["rstd_ok"], t + 1)
                    s.ok(dve.tensor_tensor(view, view, bc(rstd[:, t, :], 2, P), ALU.mult))
                    s.wait()
                    dve.tensor_tensor(view, view, bc(K.subln_row8[:, :], 1, DIFF), ALU.mult).then_inc(S["normed"], 1)
            for t in range(PT):
                dve.wait_ge(S["turned"], 2 * t + 2)
                dve.tensor_copy(K.feat[:, 4:8, t * P:(t + 1) * P],
                                K.ps[:, 2 * (t % 2) + 1, :].rearrange("p (c n) -> p c n", c=4)).then_inc(S["out_dve"], 1)


def sample_attention(nc, K, tag, cache_k, cache_v, new_v, row_bias, bias_sel, width, chunks, fill_q, new_k, new_mask,
                     coef, out):
    names = ("q_ok", "turned_act", "turned_dve", "kt_act", "kt_dve", "scored", "new_out", "shifted",
             "exped", "scaled", "pt_turned", "pt_act", "pt_dve", "weighed", "o_copied", "o_turned", "chain", "chain_act",
             "new_v_in", "bias_in")
    S = {n: K.sem(f"{tag}_{n}") for n in names}
    k_in = [K.sem(f"{tag}_k_in_{j}") for j in range(N_PAGES)]
    v_in = [K.sem(f"{tag}_v_in_{j}") for j in range(N_PAGES)]
    per_bank = BANK // P // chunks if chunks <= 4 else 0
    units = [((j,), range(4 * a, 4 * a + 4)) for j in range(N_PAGES) for a in range(chunks // 4)] if chunks >= 4 else \
            [(range(j, j + per_bank), range(chunks)) for j in range(0, N_PAGES, per_bank)]
    half_units = len(units) // 2
    rows4 = [slice(32 * i, 32 * i + 32) for i in range(4)]
    group_chunks = [(2 * i, 2 * i + 1) if chunks == KC else (i // 2,) for i in range(4)]
    vw = width // 4
    with ExitStack() as mem:
        sb = lambda name, shape: mem.enter_context(nc.sbuf_tensor(f"{tag}_{name}", shape, F32))
        kslot = sb("kslot", [P, N_PAGES, width])
        vslot = sb("vslot", [P, N_PAGES, width])
        kt = sb("kt", [P, 2, chunks, BANK])
        qz = sb("qz", [P, chunks, P])
        vnew = sb("vnew", [DEC_SEQ, width])
        bias = sb("bias", [DEC_SEQ, KEYS])
        knew = sb("knew", [P, chunks, DEC_SEQ])
        snew = sb("snew", [P, DEC_SEQ])
        probs = sb("probs", [P, KEYS])
        pt = sb("pt", [P, N_PAGES, P])
        ptn = sb("ptn", [DEC_SEQ, P])
        st = sb("st", [P, 8])
        o_sb = sb("o_sb", [P, max(vw, P)])
        block = mem.enter_context(nc.Block())
        SC, NEWS, NEWT, O = K.ps[:, 2:4, :], K.ps[:, 4, 0:DEC_SEQ], K.ps[0:DEC_SEQ, 4, P:2 * P], K.ps[:, 7, 0:vw]
        OT = K.ps[:, 4, 2 * P:4 * P].rearrange("p (x n) -> p x n", x=2)

        @block.sync
        def _(sp):
            with sp.Fori(0, DEC_BATCH) as b:
                ids = [sp.value_load(K.pages[0:1, ds(b * N_PAGES + j, 1)], min_val=0, max_val=cache_k.shape[0] - 1)
                       for j in range(N_PAGES)]
                for j in range(N_PAGES):
                    i = [n for n, (pages, _) in enumerate(units) if j in pages][-1]
                    sp.wait_ge(S["turned_dve"] if i % 2 else S["turned_act"], b * half_units + i // 2 + 1)
                    sp.dma_start(kslot[:, j, :], cache_k[ds(ids[j], 1), :, :].rearrange("a k d -> (a k) d"))\
                      .then_inc(k_in[j], 16)
                sp.wait_ge(S["scored"], b * 3 + 1)
                sp.dma_start(bias[:, :], row_bias(b)).then_inc(S["bias_in"], 16)
                sp.wait_ge(S["weighed"], b + 1)
                sp.dma_start(vnew[:, :], new_v(b)).then_inc(S["new_v_in"], 16)
                for j in range(N_PAGES):
                    sp.dma_start(vslot[:, j, :], cache_v[ds(ids[j], 1), :, :].rearrange("a k d -> (a k) d"))\
                      .then_inc(v_in[j], 16)

        @block.tensor
        def _(pe):
            pe.sem_inc(S["turned_act"], half_units)
            pe.sem_inc(S["turned_dve"], half_units)
            pe.sem_inc(S["weighed"], 1)
            pe.sem_inc(S["scored"], 1)
            with pe.Fori(0, DEC_BATCH) as b:
                def scores(g):
                    pe.wait_ge(S["kt_act"], (b * 2 + g + 1) * (half_units // 2) + 1)
                    pe.wait_ge(S["kt_dve"], (b * 2 + g + 1) * (half_units // 2) + 1)
                    score_groups(SC[:, g, :], bias[:, g * BANK:(g + 1) * BANK], lambda c: kt[:, g, c, :])

                def score_groups(dst, bias_row, keys_at):
                    pe.matmul(dst, bias_sel, bias_row, start=True, stop=True)
                    for x in range(len(group_chunks[0])):
                        for i in range(4):
                            c = group_chunks[i][x]
                            ins = pe.matmul(dst[rows4[i], :], qz[:, c, rows4[i]], keys_at(c), start=False,
                                            stop=True, skip_group_check=True)
                    ins.then_inc(S["scored"], 1)
                pe.wait_ge(S["q_ok"], b + 1)
                pe.wait_ge(S["bias_in"], b * 16 + 16)
                for i, (pages, cs) in enumerate(units):
                    for j in pages:
                        pe.wait_ge(k_in[j], b * 16 + 16)
                    pe.wait_ge(S["kt_dve"] if i % 2 else S["kt_act"], b * half_units + i // 2 + 1)
                    for x, (j, c) in enumerate((j, c) for c in cs for j in pages):
                        ins = pe.transpose(K.ps[:, i % 2, x * P:(x + 1) * P], kslot[:, j, c * P:(c + 1) * P],
                                           K.c("ident"))
                    ins.then_inc(S["turned_dve"] if i % 2 else S["turned_act"], 1)
                    if i == half_units:
                        scores(0)
                scores(1)
                score_groups(NEWS, bias[:, PAST_LEN:KEYS], lambda c: knew[:, c, :])
                pe.wait_ge(S["scaled"], b + 1)
                for g in range(2):
                    for j in range(4):
                        ins = pe.transpose(K.ps[:, 5 + g, j * P:(j + 1) * P],
                                           probs[:, (4 * g + j) * P:(4 * g + j + 1) * P], K.c("ident"))
                    if g == 1:
                        ins = pe.transpose(NEWT, probs[:, PAST_LEN:KEYS], K.c("ident"))
                    ins.then_inc(S["pt_turned"], 1)
                pe.wait_ge(S["new_v_in"], b * 16 + 16)
                pe.wait_ge(S["o_copied"], b + 1)
                pe.wait_ge(S["pt_act"], b + 1)
                pe.wait_ge(S["pt_dve"], b + 1)
                for j in range(N_PAGES):
                    pe.wait_ge(v_in[j], b * 16 + 16)
                    for i in range(4):
                        pe.matmul(O[rows4[i], :], pt[:, j, rows4[i]], vslot[:, j, i * vw:(i + 1) * vw],
                                  start=(j == 0), stop=False)
                for i in range(4):
                    ins = pe.matmul(O[rows4[i], :], ptn[:, rows4[i]], vnew[:, i * vw:(i + 1) * vw],
                                    start=False, stop=True)
                ins.then_inc(S["weighed"], 1)
                pe.wait_ge(S["o_copied"], b + 2)
                for x in range(0, vw, P):
                    ins = pe.transpose(OT[:, x // P, :], o_sb[:, x:x + P], K.c("ident"))
                ins.then_inc(S["o_turned"], 1)

        def kt_out(eng, i, b):
            pages, cs = units[i]
            g = pages[0] // 4
            eng.wait_ge(S["turned_dve"] if i % 2 else S["turned_act"], (b + 1) * half_units + i // 2 + 1)
            j0 = pages[0] % 4
            dst = kt[:, g, cs[0]:cs[-1] + 1, j0 * P:(j0 + len(pages)) * P]
            src = K.ps[:, i % 2, :].rearrange("p (c n) -> p c n", c=len(cs))
            if i % 2:
                eng.tensor_copy(dst, src).then_inc(S["kt_dve"], 1)
            else:
                eng.activation(dst, src, ACT.Copy).then_inc(S["kt_act"], 1)

        @block.scalar
        def _(act):
            act.sem_inc(S["kt_act"], 1)
            with act.Fori(0, DEC_BATCH) as b:
                act.wait_ge(S["scored"], b * 3 + 1)
                for i in range(0, len(units), 2):
                    kt_out(act, i, b)
                act.wait_ge(S["shifted"], b + 1)
                act.activation(probs[:, 0:PAST_LEN].rearrange("p (g k) -> p g k", g=2), SC, ACT.Exp, bias=st[:, 3:4],
                               accum_out=st[:, 4:5]).then_inc(S["exped"], 1)
                act.activation(probs[:, PAST_LEN:KEYS], snew[:, :], ACT.Exp, bias=st[:, 3:4],
                               accum_out=st[:, 5:6]).then_inc(S["exped"], 1)
                act.wait_ge(S["pt_turned"], b * 2 + 1)
                act.activation(pt[:, 0:4, :], K.ps[:, 5, :].rearrange("p (j n) -> p j n", j=4), ACT.Copy)\
                   .then_inc(S["pt_act"], 1)

        @block.vector
        def _(dve):
            s0 = Steps(dve, S["chain"])
            s0.ok(dve.memset(qz[:, :, :], 0.0))
            dve.memset(o_sb[:, :], 0.0)
            s0.wait()
            dve.sem_inc(S["kt_dve"], 1)
            dve.sem_inc(S["o_copied"], 1)
            STEPS = 6 + (0 if coef is None else 1)
            with dve.Fori(0, DEC_BATCH) as b:
                s = Steps(dve, S["chain"], b * STEPS + 1)
                dve.wait_ge(S["scored"], b * 3 + 1)
                dve.tensor_copy(knew[:, :, :], new_k[:, :, ds(b * DEC_SEQ, DEC_SEQ)])
                fill_q(dve, qz, b, S["q_ok"])
                for i in range(1, len(units), 2):
                    kt_out(dve, i, b)
                dve.wait_ge(S["scored"], b * 3 + 4)
                if new_mask is None:
                    s.ok(dve.tensor_copy(snew[:, :], NEWS))
                else:
                    s.ok(dve.tensor_tensor(snew[:, :], NEWS, new_mask, ALU.add))
                s.ok(dve.tensor_reduce(st[:, 0:1], SC, mybir.AxisListType.XY, ALU.max))
                s.wait()
                s.ok(dve.tensor_reduce(st[:, 1:2], snew[:, :], AX, ALU.max))
                s.wait()
                dve.tensor_scalar(st[:, 3:4], st[:, 0:1], st[:, 1:2], -1.0, ALU.max, ALU.mult).then_inc(S["shifted"], 1)
                dve.wait_ge(S["exped"], b * 2 + 2)
                s.ok(dve.tensor_scalar(st[:, 6:7], st[:, 4:5], st[:, 5:6], None, ALU.add))
                s.wait()
                s.ok(dve.reciprocal(st[:, 7:8], st[:, 6:7]))
                s.wait()
                if coef is not None:
                    s.ok(dve.tensor_scalar(st[:, 2:3], st[:, 7:8], coef, None, ALU.mult))
                    s.wait()
                r = st[:, 7:8] if coef is None else st[:, 2:3]
                dve.tensor_scalar(probs[:, :], probs[:, :], r, None, ALU.mult).then_inc(S["scaled"], 1)
                dve.wait_ge(S["pt_turned"], b * 2 + 2)
                s.ok(dve.tensor_copy(ptn[:, :], NEWT))
                assert s.n == STEPS
                dve.tensor_copy(pt[:, 4:8, :], K.ps[:, 6, :].rearrange("p (j n) -> p j n", j=4))\
                   .then_inc(S["pt_dve"], 1)
                s.wait()
                dve.wait_ge(S["weighed"], b + 2)
                dve.tensor_copy(o_sb[:, 0:vw], O).then_inc(S["o_copied"], 1)
                dve.wait_ge(S["o_turned"], b + 1)
                out(dve, OT, b)


def sample_subln(nc, K):
    S = {n: K.sem("subln_" + n) for n in ("squared", "summed", "mean_ok", "rstd_ok", "chain")}
    with ExitStack() as mem:
        square = mem.enter_context(nc.sbuf_tensor("subln_square", [P, DIFF, SAMP], F32))
        ms = mem.enter_context(nc.sbuf_tensor("subln_ms", [P, DIFF, SAMP], F32))
        root, inv, fix = (mem.enter_context(nc.sbuf_tensor(f"subln_{x}", [P, DIFF, SAMP], F32))
                          for x in ("root", "inv", "fix"))
        block = mem.enter_context(nc.Block())
        view = K.feat[:, 4:8, SEQ:TOK]

        @block.scalar
        def _(act):
            act.activation(square[:, :, :], view, ACT.Square).then_inc(S["squared"], 1)
            act.wait_ge(S["mean_ok"], 1)
            act.activation(root[:, :, :], ms[:, :, :], ACT.Sqrt).then_inc(S["rstd_ok"], 1)

        @block.tensor
        def _(pe):
            pe.wait_ge(S["squared"], 1)
            pe.matmul(K.ps[:, 0, 0:DIFF * SAMP], K.c("ones"), square[:, :, :].rearrange("p h n -> p (h n)"),
                      start=True, stop=True).then_inc(S["summed"], 1)

        @block.vector
        def _(dve):
            s = Steps(dve, S["chain"])
            dve.wait_ge(S["summed"], 1)
            dve.tensor_scalar(ms[:, :, :], K.ps[:, 0, 0:DIFF * SAMP].rearrange("p (h n) -> p h n", h=DIFF),
                              1.0 / P, EPS, ALU.mult, ALU.add).then_inc(S["mean_ok"], 1)
            dve.wait_ge(S["rstd_ok"], 1)
            s.ok(dve.reciprocal(inv[:, :, :], root[:, :, :]))
            s.wait()
            s.ok(dve.tensor_tensor(fix[:, :, :], inv[:, :, :], inv[:, :, :], ALU.mult))
            s.wait()
            dve.wait_ge(S["mean_ok"], 1)
            s.ok(dve.tensor_tensor(fix[:, :, :], fix[:, :, :], ms[:, :, :], ALU.mult))
            s.wait()
            s.ok(dve.tensor_scalar(fix[:, :, :], fix[:, :, :], -0.5, 1.5, ALU.mult, ALU.add))
            s.wait()
            s.ok(dve.tensor_tensor(fix[:, :, :], fix[:, :, :], inv[:, :, :], ALU.mult))
            s.wait()
            s.ok(dve.scalar_tensor_tensor(out=view, in0=view, scalar=K.subln_col8[:, 0:1], in1=fix[:, :, :],
                                          op0=ALU.mult, op1=ALU.mult))
            s.wait()


def add_product(nc, K, tag, lhs_at, tiles):
    multiplied, added, passed = (K.sem(f"{tag}_{x}") for x in ("multiplied", "added", "passed"))
    n_passed = 0
    for half in range(2):
        for tile, _ in tiles[half][:-1]:
            n_passed += 1
            K.weights.used[tile] = (passed, n_passed)
        K.weights.used[tiles[half][-1][0]] = (multiplied, NT * (half + 1))
    with nc.Block() as block:
        @block.sync
        def _(sp):
            K.weights.load_up_to(sp, tiles[-1][-1][0] + 2)

        @block.tensor
        def _(pe):
            for half in range(2):
                first, last = tiles[half][0][1][0], tiles[half][-1][1][-1]
                for tile, chunks in tiles[half]:
                    K.weights.arrived(pe, tile)
                    w = K.weights.slot(tile)[:, 0:len(chunks) * BANK].rearrange("p (k n) -> p k n", n=BANK)
                    for t in range(NT):
                        n, item = rows_of(t), half * NT + t
                        if item >= 8 and chunks[0] == first:
                            pe.wait_ge(added, item - 7)
                        for i, c in enumerate(chunks):
                            ins = pe.matmul(K.ps[0:n, item % 8, :], lhs_at(c, t), w[:, i, :],
                                            start=(c == first), stop=(c == last))
                        if chunks[-1] == last:
                            ins.then_inc(multiplied, 1)
                    if chunks[-1] != last:
                        ins.then_inc(passed, 1)

        @block.vector
        def _(dve):
            for item in range(2 * NT):
                half, t = divmod(item, NT)
                n = rows_of(t)
                dst = K.resid[0:n, t, half * BANK:(half + 1) * BANK]
                dve.wait_ge(multiplied, item + 1)
                dve.tensor_tensor(dst, dst, K.ps[0:n, item % 8, :], ALU.add).then_inc(added, 1)
            dve.wait_ge(added, 2 * NT)


def gate_up(nc, K, tag, act_t, first_tile):
    S = {n: K.sem(f"{tag}_{n}") for n in ("multiplied", "silu_ok", "chunk_ok")}
    H = TOK // 2
    n_tiles = FC // 2
    for i in range(n_tiles):
        K.weights.used[first_tile + i] = (S["multiplied"], 2 * (i + 1))
    with ExitStack() as mem:
        silu = mem.enter_context(nc.sbuf_tensor(f"{tag}_silu", [P, 2, 2, H], F32))
        block = mem.enter_context(nc.Block())

        @block.sync
        def _(sp):
            K.weights.load_up_to(sp, first_tile + n_tiles + 1)

        @block.tensor
        def _(pe):
            def tile(i, a):
                n = first_tile + a
                K.weights.arrived(pe, n, i * 32)
                w = K.weights.slot(n).rearrange("p (a k n) -> p a k n", a=2, k=KC)
                for x in range(2):
                    pe.wait_ge(S["chunk_ok"], i * 4 + 2 * a + x + 1)
                    for g in range(2):
                        for hf in range(2):
                            for k in range(KC):
                                ins = pe.matmul(K.ps[:, 4 * x + 2 * g + hf, 0:H], w[:, g, k, x * P:(x + 1) * P],
                                                K.feat[:, k, hf * H:(hf + 1) * H], start=(k == 0), stop=(k == KC - 1))
                    ins.then_inc(S["multiplied"], 1)
            with pe.Fori(0, n_tiles // 2) as i:
                tile(i, 0)
                tile(i, 1)
            tile(n_tiles // 2, 0)

        @block.scalar
        def _(act):
            def chunk(i, x):
                act.wait_ge(S["multiplied"], i * 2 + x + 1)
                act.wait_ge(S["chunk_ok"], i * 2 + x + 1)
                act.activation(silu[:, x, :, :], K.ps[:, 4 * x:4 * x + 2, 0:H], ACT.Silu).then_inc(S["silu_ok"], 1)
            with act.Fori(0, FC // 2) as i:
                chunk(i, 0)
                chunk(i, 1)

        @block.vector
        def _(dve):
            dve.sem_inc(S["chunk_ok"], 2)
            with dve.Fori(0, FC // 2) as i:
                for x in range(2):
                    dve.wait_ge(S["silu_ok"], i * 2 + x + 1)
                    dst = act_t[:, ds((i * 2 + x) * TOK, TOK)].rearrange("p (f n) -> p f n", f=2)
                    dve.tensor_tensor(dst, silu[:, x, :, :], K.ps[:, 4 * x + 2:4 * x + 4, 0:H], ALU.mult)\
                       .then_inc(S["chunk_ok"], 1)


def select_keys(nc, K):
    names = ("kidx_turned", "kt_ok", "p_scored", "p_relu", "p_ok", "s_scored", "s_relu", "s_mixed", "s_out",
             "row_stored", "rows_in", "masked", "chain", "weights_in", "weights_out", "q_ok", "mask_stored")
    S = {n: K.sem("select_" + n) for n in names}
    kidx_in = [K.sem(f"select_kidx_in_{i}") for i in range(2)]
    row_stored = [K.sem(f"select_row_stored_{i}") for i in range(2)]
    with ExitStack() as mem:
        sb = lambda name, shape: mem.enter_context(nc.sbuf_tensor("select_" + name, shape, F32))
        relu = sb("relu", [P, 2, SEQ])
        pages = sb("pages", [P, 2, N_PAGES, HEAD_DIM])
        kt = sb("kt", [P, 2, 4, P])
        qs = sb("qs", [P, DEC_BATCH, IDXH, DEC_SEQ])
        wt = sb("wt", [IDXH * DEC_SEQ, DEC_BATCH])
        mix = sb("mix", [IDXH * DEC_SEQ, DEC_BATCH, DEC_SEQ])
        srelu = sb("srelu", [IDXH * DEC_SEQ, KEYS])
        srow = sb("srow", [DEC_SEQ, 2, KEYS])
        sample = sb("sample", [SAMP, KEYS])
        prompt = sb("prompt", [P, 3, SEQ])
        best = sb("best", [P, 4, 8])
        block = mem.enter_context(nc.Block())
        NEWS, NEWO = K.ps[0:32, 3, 0:DEC_SEQ], K.ps[0:DEC_SEQ, 3, 64:64 + DEC_SEQ]
        p_units = [(qt, h) for qt in range(1, PT) for h in range(IDXH)]
        B = range(DEC_BATCH)

        @block.sync
        def _(sp):
            for b in B:
                if b >= 2:
                    sp.wait_ge(S["kidx_turned"], b - 1)
                for j in range(N_PAGES):
                    n = b * N_PAGES + j
                    pid = sp.value_load(K.pages[0:1, n:n + 1], min_val=0, max_val=K.cache_l1_kidx.shape[0] - 1)
                    sp.dma_start(pages[:, b % 2, j, :], K.cache_l1_kidx[ds(pid, 1), :, :]
                                 .rearrange("a k d -> (a k) d")).then_inc(kidx_in[b % 2], 16)
                if b >= 2:
                    sp.wait_ge(S["s_out"], b - 1)
                    sp.dma_start(K.idx_rows[b - 2], srow[:, b % 2, :]).then_inc(row_stored[b % 2], 16)
            for b in B[-2:]:
                sp.wait_ge(S["s_out"], b + 1)
                sp.dma_start(K.idx_rows[b], srow[:, b % 2, :]).then_inc(row_stored[b % 2], 16)
            for x in row_stored:
                sp.wait_ge(x, 16 * DEC_BATCH // 2)
            sp.dma_start(sample[:, :], K.idx_rows.rearrange("b q k -> (b q) k")).then_inc(S["rows_in"], 16)
            sp.wait_ge(S["masked"], 1)
            sp.dma_start(K.mask_rows.rearrange("b q k -> (b q) k"), sample[:, :]).then_inc(S["mask_stored"], 16)
            sp.wait_ge(S["mask_stored"], 16)

        @block.tensor
        def _(pe):
            for u, (qt, h) in enumerate(p_units):
                if u >= 2:
                    pe.wait_ge(S["p_relu"], u - 1)
                lo = (h % 2) * HEAD_DIM
                w = (qt + 1) * P
                pe.matmul(K.ps[:, 6 + u % 2, 0:w], K.qi[lo:lo + HEAD_DIM, h // 2, qt * P:w], K.ki[lo:lo + HEAD_DIM, 0:w],
                          start=True, stop=True).then_inc(S["p_scored"], 1)
            for b in B:
                pe.wait_ge(kidx_in[b % 2], 16 * N_PAGES * (b // 2 + 1))
                if b >= 1:
                    pe.wait_ge(S["kt_ok"], b)
                for j in range(0, N_PAGES, 2):
                    ins = pe.transpose(K.ps[:, 0, j // 2 * P:(j // 2 + 1) * P],
                                       pages[:, b % 2, j:j + 2, :].rearrange("p a d -> p (a d)"), K.c("ident"))
                ins.then_inc(S["kidx_turned"], 1)
                pe.wait_ge(S["kt_ok"], b + 1)
                pe.wait_ge(S["q_ok"], 1)
                if b >= 1:
                    pe.wait_ge(S["s_relu"], 2 * b)
                for j in range(N_PAGES):
                    lo = (j % 2) * HEAD_DIM
                    pe.matmul(K.ps[0:32, 1 + j % 2, j // 2 * P:(j // 2 + 1) * P],
                              qs[lo:lo + HEAD_DIM, b, :, :].rearrange("p h q -> p (h q)"),
                              kt[lo:lo + HEAD_DIM, b % 2, j // 2, :], start=True, stop=True)
                if b >= 1:
                    pe.wait_ge(S["s_out"], b)
                pe.matmul(NEWS, qs[0:HEAD_DIM, b, :, :].rearrange("p h q -> p (h q)"),
                          K.ki[0:HEAD_DIM, SEQ + b * DEC_SEQ:SEQ + (b + 1) * DEC_SEQ], start=True, stop=True)\
                  .then_inc(S["s_scored"], 1)
                pe.wait_ge(S["s_relu"], 2 * b + 2)
                for dst, lo, hi in ((K.ps[0:DEC_SEQ, 4, :], 0, BANK), (K.ps[0:DEC_SEQ, 5, :], BANK, PAST_LEN),
                                    (NEWO, PAST_LEN, KEYS)):
                    ins = pe.matmul(dst, mix[:, b, :], srelu[:, lo:hi], start=True, stop=True)
                ins.then_inc(S["s_mixed"], 1)

        @block.scalar
        def _(act):
            act.dma_start(K.idx_weights, K.wi[0:SAMP, PT, :]).then_inc(S["weights_out"], 16)
            act.wait_ge(S["weights_out"], 16)
            with nc.allow_non_contiguous_dma(reason="256 words"):
                for h in range(IDXH):
                    act.dma_start(wt[h * DEC_SEQ:(h + 1) * DEC_SEQ, :],
                                   K.idx_weights[:, h:h + 1].rearrange("(b q) a -> q (b a)", b=DEC_BATCH))\
                        .then_inc(S["weights_in"], 16)
            for u, (qt, h) in enumerate(p_units):
                w = (qt + 1) * P
                act.wait_ge(S["p_scored"], u + 1)
                if u >= 2:
                    act.wait_ge(S["p_ok"], u - 1)
                act.activation(relu[:, u % 2, 0:w], K.ps[:, 6 + u % 2, 0:w], ACT.Relu).then_inc(S["p_relu"], 1)
            for b in B:
                act.wait_ge(S["kidx_turned"], b + 1)
                if b >= 2:
                    act.wait_ge(S["s_scored"], b - 1)
                act.activation(kt[:, b % 2, :, :], K.ps[:, 0, :].rearrange("p (j n) -> p j n", j=4), ACT.Copy)\
                   .then_inc(S["kt_ok"], 1)
                act.wait_ge(S["s_scored"], b + 1)
                if b >= 1:
                    act.wait_ge(S["s_mixed"], b)
                act.activation(srelu[:, 0:PAST_LEN].rearrange("p (j a k) -> p a j k", a=2, k=P),
                               K.ps[0:32, 1:3, :].rearrange("p a (j k) -> p a j k", k=P), ACT.Relu)\
                   .then_inc(S["s_relu"], 1)
                act.activation(srelu[:, PAST_LEN:KEYS], NEWS, ACT.Relu).then_inc(S["s_relu"], 1)

        @block.vector
        def _(dve):
            s = Steps(dve, S["chain"])
            for half in range(2):
                for par in range(2):
                    src = K.qi[par * HEAD_DIM:(par + 1) * HEAD_DIM, :, SEQ:TOK].rearrange(
                        "p c (b q) -> p b c q", b=DEC_BATCH)
                    dst = qs[half * HEAD_DIM:(half + 1) * HEAD_DIM, :, par:IDXH:2, :]
                    s.ok(dve.tensor_copy(dst, src))
            dve.wait_ge(S["weights_in"], 16 * IDXH)
            s.ok(dve.tensor_tensor(mix[:, :, :], bc(K.c("idx_sel")[0:32, :], 1, DEC_BATCH),
                                   bc(wt[:, :], 2, DEC_SEQ), ALU.mult))
            s.wait()
            dve.sem_inc(S["q_ok"], 1)
            for u, (qt, h) in enumerate(p_units):
                w = (qt + 1) * P
                dst, src, wh = prompt[:, qt - 1, 0:w], relu[:, u % 2, 0:w], K.wi[:, qt, h:h + 1]
                dve.wait_ge(S["p_relu"], u + 1)
                if h == 0:
                    dve.tensor_scalar(dst, src, wh, None, ALU.mult).then_inc(S["p_ok"], 1)
                else:
                    dve.wait_ge(S["p_ok"], u)
                    dve.scalar_tensor_tensor(out=dst, in0=src, scalar=wh, in1=dst, op0=ALU.mult, op1=ALU.add)\
                       .then_inc(S["p_ok"], 1)
                if h == IDXH - 1:
                    dve.wait_ge(S["p_ok"], u + 1)
                    s.ok(dve.tensor_tensor(dst[:, qt * P:w], dst[:, qt * P:w], K.c("causal"), ALU.add))
            for b in B:
                dve.wait_ge(S["s_mixed"], b + 1)
                if b >= 2:
                    dve.wait_ge(row_stored[b % 2], 16 * (b // 2))
                s.ok(dve.tensor_copy(srow[:, b % 2, 0:PAST_LEN].rearrange("p (g k) -> p g k", g=2),
                                     K.ps[0:DEC_SEQ, 4:6, :]))
                s.ok(dve.tensor_tensor(srow[:, b % 2, PAST_LEN:KEYS], NEWO, K.c("new_mask")[0:DEC_SEQ, :], ALU.add))
                s.wait()
                dve.sem_inc(S["s_out"], 1)

            def rounds(views, bests, k):
                for _ in range(k // 8):
                    for v, b8 in zip(views, bests):
                        s.ok(dve.max(b8, v))
                    s.wait()
                    for v, b8 in zip(views, bests):
                        s.ok(dve.match_replace(v, b8, v, TAKEN))
                    s.wait()

            def to_mask(dst, view):
                return dve.tensor_scalar(dst, view, TAKEN * 0.5, NEG, ALU.is_gt, ALU.mult)

            views = [prompt[:, qt - 1, 0:(qt + 1) * P] for qt in range(1, PT)]
            rounds(views, [best[:, i, :] for i in range(3)], K_PROMPT)
            s.ok(dve.tensor_copy(K.mask[:, 0, 0:P], K.c("causal")))
            for i, v in enumerate(views):
                s.ok(to_mask(K.mask[:, i + 1, 0:(i + 2) * P], v))
            dve.wait_ge(S["rows_in"], 16)
            rounds([sample[:, :]], [best[0:SAMP, 3, :]], K_SAMPLE)
            to_mask(sample[:, :], sample[:, :]).then_inc(S["masked"], 1)
            s.wait()


def store_results(nc, K):
    done = K.sem("results_stored")
    with nc.Block() as block:
        @block.sync
        def _(sp):
            sp.dma_start(K.y_prompt[0].rearrange("(t p) d -> p t d", p=P), K.resid[:, 0:PT, :]).then_inc(done, 16)
            sp.dma_start(K.y_sample.rearrange("b t d -> (b t) d"), K.resid[0:SAMP, PT, :]).then_inc(done, 16)
            sp.wait_ge(done, 32)


def two_layers(nc, K):
    W = K.weights = Weights(K, lambda name: nc.alloc_semaphore(name=name))
    cuts0 = dict(qa=0, ka=512, va=1024, fa=1536, qb=1544, kb=2056, vb=2568)
    l0 = {n: W.add(column_tile(K.w_in0, 0, KC, c, 8 if n == "fa" else 512)) for n, c in cuts0.items()}

    def products(w_out, wg, wu, wd):
        out = [[(W.add(column_tile(w_out, 0, KC, h * BANK, BANK)), range(KC))] for h in range(2)]
        gu = [W.add(gate_up_tile(wg, wu, i * 256)) for i in range(FC // 2)]
        down = [[(W.add(column_tile(wd, k, min(8, FC - k), h * BANK, BANK)), range(k, min(k + 8, FC)))
                 for k in range(0, FC, 8)] for h in range(2)]
        return out, gu[0], down

    out0, gu0, down0 = products(K.w_out0, K.w_gate0, K.w_up0, K.w_down0)
    l1 = {n: W.add(column_tile(K.w_in1, 0, KC, c, w)) for n, c, w in
          (("idx", 1536, 324), ("kv", 1024, 512), ("q0", 0, 512), ("q1", 512, 512))}
    out1, gu1, down1 = products(K.w_out1, K.w_gate1, K.w_up1, K.w_down1)

    load_inputs(nc, K)

    def tok_rows(prompt, sample, c0, c1):
        def at(t):
            return prompt[t * P:(t + 1) * P, c0:c1] if t < PT else sample[:, c0:c1]
        return at

    def plain(j):
        return lambda r: r[:, j * P:(j + 1) * P]

    def to(prompt, sample, c):
        return lambda t: prompt[:, c, t * P:(t + 1) * P] if t < PT else sample[:, c, :]

    def ffn(tag, gain, gu, down):
        norm_to_features(nc, K, gain, tag + "n")
        with nc.sbuf_tensor(tag + "_act", [P, FC * TOK], F32) as act_t:
            gate_up(nc, K, tag + "g", act_t, gu)
            add_product(nc, K, tag + "d", lambda c, t: act_t[:, c * TOK + t * P:c * TOK + t * P + rows_of(t)], down)

    norm_to_features(nc, K, 0, "n0")
    with ExitStack() as layer:
        sb = lambda mem, name, shape: mem.enter_context(nc.sbuf_tensor(name, shape, F32))
        qs, ks = sb(layer, "qs0", [P, KC, SAMP]), sb(layer, "ks0", [P, KC, SAMP])
        vs = sb(layer, "vs0", [SAMP, D_MODEL])
        K.logf = sb(layer, "logf", [P, NT, FOX])
        with ExitStack() as pr:
            att = sb(pr, "att0", [P, PT, D_MODEL])
            qp, kp = sb(pr, "qp0", [P, KC, SEQ]), sb(pr, "kp0", [P, KC, SEQ])
            vp = sb(pr, "vp0", [P, PT, D_MODEL])
            K.minus_c = sb(pr, "minus_c", [P, FOX, SEQ])

            def q_part(name, norm, rope, c):
                return Part(l0[name], 512, 512, norm, rope,
                            turns=[(plain(j), to(qp, qs, c + j), SCALE) for j in range(4)])

            def k_part(name, norm, rope, c):
                return Part(l0[name], 512, 512, norm, rope,
                            stores=[(slice(0, 512), tok_rows(K.p_l0_k, K.s_l0_k, c * P, c * P + 512))],
                            turns=[(plain(j), to(kp, ks, c + j), 1.0) for j in range(4)])

            def v_part(name, c0):
                rows = tok_rows(K.p_l0_v, K.s_l0_v, c0, c0 + 512)
                return Part(l0[name], 512, copies=[(
                    slice(0, 512), lambda t: vp[:, t, c0:c0 + 512] if t < PT else vs[:, c0:c0 + 512],
                    rows, rows, None)])

            f_rows = tok_rows(K.p_l0_logf, K.s_l0_logf, 0, FOX)

            def log_sigmoid_in(dve, dst, src, s):
                return dve.tensor_tensor(dst, src, K.bias_f[0:src.shape[0], :], ALU.add)

            parts = [q_part("qa", 0, False, 0), k_part("ka", 1, False, 0), v_part("va", 0),
                     Part(l0["fa"], FOX, copies=[(slice(0, FOX), lambda t: K.logf[0:rows_of(t), t, :], None, None,
                                                  log_sigmoid_in)]),
                     q_part("qb", 2, True, 4), k_part("kb", 3, True, 4), v_part("vb", 512)]
            project(nc, K, parts, "p0")
            log_sigmoid(nc, K, f_rows)
            forget_sums(nc, K)

            def lo(h):
                return slice((h % 2) * HEAD_DIM, (h % 2 + 1) * HEAD_DIM)

            def v_cols(h):
                return slice(h * HEAD_DIM, (h + 1) * HEAD_DIM) if h < FOX else \
                    slice(512 + (h - FOX) // 2 * P, 512 + ((h - FOX) // 2 + 1) * P)
            prompt_attention(
                nc, K, "a0", q_at=lambda h, qt: qp[lo(h), h // 2, qt * P:(qt + 1) * P], k_at=lambda h: kp[lo(h), h // 2, :],
                v_at=lambda h, j: vp[:, j, v_cols(h)],
                bias_at=lambda h, qt: K.minus_c[:, h, 0:(qt + 1) * P] if h < FOX else None, diag=True,
                out_at=lambda h, qt: att[:, qt, v_cols(h)], second=lambda h: h >= FOX and h % 2 == 1)
            turn_attention(nc, K, att, "t0", True)

        def fill_q0(dve, qz, b, ok):
            flat = qz[:, :, :].rearrange("p c n -> p (c n)")
            for half in range(2):
                rows = slice(half * HEAD_DIM, (half + 1) * HEAD_DIM)
                for c in range(KC):
                    col = c * P + 16 * c + 8 * half
                    ins = dve.tensor_copy(flat[rows, col:col + DEC_SEQ], qs[rows, c, ds(b * DEC_SEQ, DEC_SEQ)])
            ins.then_inc(ok, 1)

        def out0_fn(dve, OT, b):
            now = ds(SEQ + b * DEC_SEQ, DEC_SEQ)
            for x in range(2):
                o = OT[:, x, :].rearrange("p (i x a q) -> p i x a q", i=4, x=2, a=2)[:, :, x]
                for half in range(2):
                    rows = slice(half * HEAD_DIM, (half + 1) * HEAD_DIM)
                    dve.tensor_copy(K.feat[rows, x:4:2, now], o[rows, 0:2, half, :])
                dve.tensor_reduce(K.feat[:, 4 + x:8:2, now], o[:, 2:4].rearrange("p i a q -> p i q a"), AX, ALU.add)

        sample_attention(
            nc, K, "s0", K.cache_l0_k, K.cache_l0_v, lambda b: K.s_l0_v[ds(b * DEC_SEQ, DEC_SEQ), :],
            lambda b: K.fox_rows[ds(b, 1), :, :].rearrange("a h k -> (a h) k"), K.c("fox_sel")[0:FOX, :], D_MODEL, KC, fill_q0,
            ks, K.c("new_mask"), K.coef[:, 0:1], out0_fn)
        sample_subln(nc, K)
    add_product(nc, K, "o0", lambda c, t: K.feat[:, c, t * P:t * P + rows_of(t)], out0)
    ffn("f0", 1, gu0, down0)

    renew_semaphores(nc, K)

    norm_to_features(nc, K, 2, "n1")
    with ExitStack() as layer:
        sb = lambda mem, name, shape: mem.enter_context(nc.sbuf_tensor(name, shape, F32))
        qs, ks = sb(layer, "qs1", [P, KC, SAMP]), sb(layer, "ks1", [P, 2, SAMP])
        vs = sb(layer, "vs1", [SAMP, 256])
        with ExitStack() as pr:
            att = sb(pr, "att1", [P, PT, D_MODEL])
            qp, kp = sb(pr, "qp1", [P, KC, SEQ]), sb(pr, "kp1", [P, 2, SEQ])
            vp = sb(pr, "vp1", [P, PT, 256])
            K.mask = sb(pr, "mask", [P, PT, SEQ])
            K.qi = sb(pr, "qi", [P, 2, TOK])
            K.ki = sb(pr, "ki", [P, TOK])
            K.wi = sb(pr, "wi", [P, NT, IDXH])
            span = lambda t: slice(t * P, t * P + rows_of(t))
            idx_rows = tok_rows(K.p_l1_kidx, K.s_l1_kidx, 0, HEAD_DIM)
            parts = [Part(l1["idx"], 324, 320, None, True,
                          stores=[(slice(256, 320), idx_rows)],
                          turns=[(plain(0), lambda t: K.qi[:, 0, span(t)], 1.0),
                                 (plain(1), lambda t: K.qi[:, 1, span(t)], 1.0),
                                 (plain(2), lambda t: K.ki[:, span(t)], 1.0)],
                          copies=[(slice(320, 324), lambda t: K.wi[0:rows_of(t), t, :], None, None,
                                   lambda dve, dst, src, s: dve.tensor_scalar(dst, src, SCALE * IDXH ** -0.5, None,
                                                                              ALU.mult))]),
                     Part(l1["kv"], 512, 256, 5, True,
                          stores=[(slice(0, 256), tok_rows(K.p_l1_k, K.s_l1_k, 0, 256))],
                          turns=[(plain(j), to(kp, ks, j), 1.0) for j in range(2)],
                          copies=[(slice(256, 512), lambda t: vp[:, t, :] if t < PT else vs[:, :],
                                   tok_rows(K.p_l1_v, K.s_l1_v, 0, 256), tok_rows(K.p_l1_v, K.s_l1_v, 0, 256), None)])]

            for g in range(2):
                parts.append(Part(l1[f"q{g}"], 512, 512, 4, True, paired=True,
                                  turns=[(plain(r), to(qp, qs, 4 * g + r), SCALE) for r in range(4)]))
            project(nc, K, parts, "p1")
            select_keys(nc, K)

            def kv_half(h):
                a = h // 4 % 2
                return slice(a * HEAD_DIM, (a + 1) * HEAD_DIM)
            prompt_attention(
                nc, K, "a1", q_at=lambda h, qt: qp[kv_half(h), 4 * (h // 8) + h % 4, qt * P:(qt + 1) * P],
                k_at=lambda h: kp[kv_half(h), h // 8, :],
                v_at=lambda h, j: vp[:, j, h // 4 * HEAD_DIM:(h // 4 + 1) * HEAD_DIM],
                bias_at=lambda h, qt: K.mask[:, qt, 0:(qt + 1) * P], diag=False,
                out_at=lambda h, qt: att[:, qt, h * HEAD_DIM:(h + 1) * HEAD_DIM], second=lambda h: False)
            turn_attention(nc, K, att, "t1", False)

        def fill_q1(dve, qz, b, ok):
            for half in range(2):
                rows = slice(half * HEAD_DIM, (half + 1) * HEAD_DIM)
                for g in range(2):
                    col = (8 * g + 4 * half) * DEC_SEQ
                    dst = qz[rows, g, col:col + 4 * DEC_SEQ].rearrange("p (r q) -> p r q", r=4)
                    ins = dve.tensor_copy(dst, qs[rows, 4 * g:4 * g + 4, ds(b * DEC_SEQ, DEC_SEQ)])
            ins.then_inc(ok, 1)

        def out1_fn(dve, OT, b):
            o = OT[0:HEAD_DIM, 0, :].rearrange("p (c a q) -> p c a q", c=KC, a=2)
            for half in range(2):
                dve.tensor_copy(K.feat[half * HEAD_DIM:(half + 1) * HEAD_DIM, :, ds(SEQ + b * DEC_SEQ, DEC_SEQ)],
                                o[:, :, half, :])

        sample_attention(
            nc, K, "s1", K.cache_l1_k.rearrange("n k g d -> n k (g d)"), K.cache_l1_v.rearrange("n k g d -> n k (g d)"),
            lambda b: K.s_l1_v[ds(b * DEC_SEQ, DEC_SEQ), :],
            lambda b: K.mask_rows[ds(b, 1), :, :].rearrange("a q k -> (a q) k"), K.c("query_sel")[0:DEC_SEQ, :], 256, 2, fill_q1,
            ks, None, None, out1_fn)
    add_product(nc, K, "o1", lambda c, t: K.feat[:, c, t * P:t * P + rows_of(t)], out1)
    ffn("f1", 3, gu1, down1)
    store_results(nc, K)


def renew_semaphores(nc, K):
    numbers = sorted(h.num for h in K.phase_sems)
    runs = []
    for n in numbers:
        if runs and runs[-1][1] == n:
            runs[-1][1] = n + 1
        else:
            runs.append([n, n + 1])
    with nc.Block() as block:
        @block.gpsimd
        def _(pool):
            for lo, hi in runs:
                pool.sem_clear(range(lo, hi))
    for h in K.phase_sems:
        nc.release_semaphore(h)
    K.phase_sems = []


def log_sigmoid(nc, K, rows):
    S = {n: K.sem("logsig_" + n) for n in ("act", "dve", "stored")}
    with ExitStack() as mem:
        low = mem.enter_context(nc.sbuf_tensor("logsig_low", [P, NT, FOX], F32))
        e = mem.enter_context(nc.sbuf_tensor("logsig_e", [P, NT, FOX], F32))
        block = mem.enter_context(nc.Block())
        parts = [lambda x: x[:, 0:PT, :], lambda x: x[0:SAMP, PT, :]]

        @block.scalar
        def _(act):
            for i, (f, src) in enumerate(((ACT.Abs, K.logf), (ACT.Exp, e), (ACT.Ln, e))):
                if i:
                    act.wait_ge(S["act"], 2 * i)
                if i == 2:
                    act.wait_ge(S["dve"], 4)
                for p in parts:
                    act.activation(p(e), p(src), f, scale=-1.0 if f == ACT.Exp else 1.0).then_inc(S["act"], 1)

        @block.vector
        def _(dve):
            for p in parts:
                dve.tensor_scalar(p(low), p(K.logf), 0.0, None, ALU.min).then_inc(S["dve"], 1)
            dve.wait_ge(S["act"], 4)
            for p in parts:
                dve.tensor_scalar(p(e), p(e), 1.0, None, ALU.add).then_inc(S["dve"], 1)
            dve.wait_ge(S["dve"], 2)
            dve.wait_ge(S["act"], 6)
            for p in parts:
                dve.tensor_tensor(p(K.logf), p(low), p(e), ALU.subtract).then_inc(S["dve"], 1)

        @block.sync
        def _(sp):
            sp.wait_ge(S["dve"], 6)
            for t in range(NT):
                sp.dma_start(rows(t), K.logf[0:rows_of(t), t, :]).then_inc(S["stored"], 16)
            sp.wait_ge(S["stored"], 16 * NT)


def build(nc, ins, outs, const_in):
    with ExitStack() as ctx:
        sb = lambda name, shape, dt=F32: ctx.enter_context(nc.sbuf_tensor(name, shape, dt))
        K = Kernel()
        K.x_prompt, K.x_sample, K.cache_l0_k = ins["x_prompt"], ins["x_sample"], ins["cache_l0_k"]
        K.cache_l0_v, K.cache_l0_logf, K.cache_l1_k = ins["cache_l0_v"], ins["cache_l0_logf"], ins["cache_l1_k"]
        K.cache_l1_v, K.cache_l1_kidx, K.page_table = ins["cache_l1_v"], ins["cache_l1_kidx"], ins["page_table"]
        K.b_f0, K.subln0, K.w_in0 = ins["b_f0"], ins["subln0"], ins["w_in0"]
        K.w_out0, K.w_gate0, K.w_up0 = ins["w_out0"], ins["w_gate0"], ins["w_up0"]
        K.w_down0, K.w_in1, K.w_out1 = ins["w_down0"], ins["w_in1"], ins["w_out1"]
        K.w_gate1, K.w_up1, K.w_down1 = ins["w_gate1"], ins["w_up1"], ins["w_down1"]
        flat = lambda x: x.rearrange("b t d -> (b t) d")
        heads_flat = lambda x: x.rearrange("b t g d -> (b t) (g d)")
        K.y_prompt, K.y_sample = outs["y_prompt"], outs["y_sample"]
        K.p_l0_k, K.p_l0_v, K.p_l0_logf = flat(outs["p_l0_k"]), flat(outs["p_l0_v"]), flat(outs["p_l0_logf"])
        K.p_l1_kidx, K.s_l0_k, K.s_l0_v = flat(outs["p_l1_kidx"]), flat(outs["s_l0_k"]), flat(outs["s_l0_v"])
        K.s_l0_logf, K.s_l1_kidx = flat(outs["s_l0_logf"]), flat(outs["s_l1_kidx"])
        K.p_l1_k, K.p_l1_v, K.s_l1_k = heads_flat(outs["p_l1_k"]), heads_flat(outs["p_l1_v"]), heads_flat(outs["s_l1_k"])
        K.s_l1_v = heads_flat(outs["s_l1_v"])
        K.phase_sems = []

        def sem(name):
            handle = nc.alloc_semaphore(name=name)
            K.phase_sems.append(handle)
            return handle
        K.sem = sem
        K.const_in = const_in
        K.head_gains = [ins[n] for n in ("qn_fox0", "kn_fox0", "qn_diff0", "kn_diff0", "qn_dsa1", "kn_dsa1")]
        K.norm_gains = [ins[n] for n in ("attn_norm0", "ffn_norm0", "attn_norm1", "ffn_norm1")]
        K.lam_vecs = [ins[n] for n in ("lam_q1_0", "lam_k1_0", "lam_q2_0", "lam_k2_0")]
        scratch = lambda name, shape: nc.dram_tensor(name, shape, F32, kind="Internal").ap()
        K.prompt_rows = scratch("prompt_rows", (FOX, SEQ))
        K.fox_rows = scratch("fox_rows", (DEC_BATCH, FOX, KEYS))
        K.idx_rows = scratch("idx_rows", (DEC_BATCH, DEC_SEQ, KEYS))
        K.mask_rows = scratch("mask_rows", (DEC_BATCH, DEC_SEQ, KEYS))
        K.idx_weights = scratch("idx_weights", (SAMP, IDXH))
        K.ps = ctx.enter_context(nc.psum_tensor("ps", [P, 8, BANK], F32))
        K.resid = sb("resid", [P, NT, D_MODEL])
        K.feat = sb("feat", [P, KC, TOK])
        K.wslot = sb("wslot", [P, 2, KC * BANK])
        K.const = sb("const", [P, const_in.shape[1]])
        K.c = lambda name: K.const[:, CONST_AT[name][0]:CONST_AT[name][0] + CONST_AT[name][1]]
        K.gain_cols = sb("gain_cols", [P, 4, KC])
        K.head_gain = sb("head_gain", [P, 6, HEAD_DIM])
        K.subln_row, K.subln_col = sb("subln_row", [P, P]), sb("subln_col", [P, 1])
        K.subln_row8, K.subln_col8 = sb("subln_row8", [P, P]), sb("subln_col8", [P, 1])
        K.bias_f = sb("bias_f", [P, FOX])
        K.pages = sb("pages", [1, DEC_BATCH * N_PAGES], I32)
        K.page_rows = sb("page_rows", [DEC_BATCH * N_PAGES, 1], I32)
        K.lams = sb("lams", [P, 4, HEAD_DIM])
        K.lam, K.minus_lam, K.coef = sb("lam", [P, 1]), sb("minus_lam", [P, 1]), sb("coef", [P, 1])
        two_layers(nc, K)


_INS = ['x_prompt', 'x_sample', 'cache_l0_k', 'cache_l0_v', 'cache_l0_logf', 'cache_l1_k', 'cache_l1_v',
        'cache_l1_kidx', 'page_table', 'attn_norm0', 'w_in0', 'b_f0', 'qn_fox0', 'kn_fox0', 'qn_diff0', 'kn_diff0',
        'lam_q1_0', 'lam_k1_0', 'lam_q2_0', 'lam_k2_0', 'subln0', 'w_out0', 'ffn_norm0', 'w_gate0', 'w_up0', 'w_down0',
        'attn_norm1', 'w_in1', 'qn_dsa1', 'kn_dsa1', 'w_out1', 'ffn_norm1', 'w_gate1', 'w_up1', 'w_down1']
_OUTS = {'y_prompt': (1, SEQ, D_MODEL), 'y_sample': (DEC_BATCH, DEC_SEQ, D_MODEL),
         'p_l0_k': (1, SEQ, 1024), 'p_l0_v': (1, SEQ, 1024), 'p_l0_logf': (1, SEQ, FOX),
         'p_l1_k': (1, SEQ, KVH, HEAD_DIM), 'p_l1_v': (1, SEQ, KVH, HEAD_DIM), 'p_l1_kidx': (1, SEQ, HEAD_DIM),
         's_l0_k': (DEC_BATCH, DEC_SEQ, 1024), 's_l0_v': (DEC_BATCH, DEC_SEQ, 1024),
         's_l0_logf': (DEC_BATCH, DEC_SEQ, FOX), 's_l1_k': (DEC_BATCH, DEC_SEQ, KVH, HEAD_DIM),
         's_l1_v': (DEC_BATCH, DEC_SEQ, KVH, HEAD_DIM), 's_l1_kidx': (DEC_BATCH, DEC_SEQ, HEAD_DIM)}


def kernel(**inputs):
    import numpy as _np
    import concourse.bacc as _bacc
    from concourse import mybir as _mybir
    from concourse.bass_utils import run_bass_kernel_spmd as _run

    nc = _bacc.Bacc("TRN2", target_bir_lowering=False, num_devices=1)
    arrays, ins, outs = {"in_const_dram": CONST}, {}, {}
    for name in _INS:
        a = _np.ascontiguousarray(inputs[name])
        arrays[f"in_{name}_dram"] = a
        ins[name] = nc.dram_tensor(f"in_{name}_dram", a.shape, _mybir.dt.from_np(a.dtype), kind="ExternalInput").ap()
    const_in = nc.dram_tensor("in_const_dram", CONST.shape, _mybir.dt.float32, kind="ExternalInput").ap()
    for name, shape in _OUTS.items():
        outs[name] = nc.dram_tensor(f"out_{name}_dram", shape, _mybir.dt.float32, kind="ExternalOutput").ap()
    build(nc, ins, outs, const_in)
    r = _run(nc, [arrays], core_ids=[0])
    return tuple(r.results[0][f"out_{name}_dram"] for name in _OUTS)
```

```python
from contextlib import ExitStack
import math

import numpy as np
import concourse.bass as bass
from concourse import mybir

P = 128
D_MODEL, SEQ, DEC_BATCH, DEC_SEQ = 1024, 512, 8, 8
PAST_LEN, PAGE_SIZE, HEAD_DIM = 1024, 128, 64
N_PAGES = PAST_LEN // PAGE_SIZE
SAMP = DEC_BATCH * DEC_SEQ
TOK = SEQ + SAMP
PT = SEQ // P
NT = PT + 1
KC = D_MODEL // P
D_FF = ((8 * D_MODEL + 3 * 256 - 1) // (3 * 256)) * 256
FC = D_FF // P
HALF = HEAD_DIM // 2
FOX = D_MODEL // (2 * HEAD_DIM)
DIFF = D_MODEL // (4 * HEAD_DIM)
HEADS = 16
KVH = 4
IDXH = 4
KEYS = PAST_LEN + DEC_SEQ
BANK = 512
EPS = 1e-6
SCALE = HEAD_DIM ** -0.5
LAMBDA_INIT = 0.8 - 0.6 * math.exp(-0.3 * 0)
NEG = -1e30
TAKEN = -3e38
K_PROMPT, K_SAMPLE = min(256, SEQ // 4), min(256, KEYS // 4)

ALU = mybir.AluOpType
ACT = mybir.ActivationFunctionType
AX = mybir.AxisListType.X
F32 = mybir.dt.float32
F32R = mybir.dt.float32r
I32 = mybir.dt.int32
ds = bass.ds


def rows_of(t):
    return P if t < PT else SAMP


def bc(ap, axis, n):
    shape = list(ap.shape)
    shape.insert(axis, n)
    return ap.unsqueeze(axis).to_broadcast(shape)


def constant_table():
    cols, at = [], {}

    def put(name, a):
        a = np.asarray(a, np.float32)
        full = np.zeros((P, a.shape[1]), np.float32)
        full[:a.shape[0]] = a
        at[name] = (sum(c.shape[1] for c in cols), a.shape[1])
        cols.append(full)

    i = np.arange(P)
    put("ident", np.eye(P))
    put("causal", np.where(i[None, :] <= i[:, None], 0.0, NEG))
    put("step", np.arange(SEQ)[None, :] >= i[:, None])
    row_head, row_query = i // DEC_SEQ, i % DEC_SEQ
    h8 = np.arange(8)
    put("fox_sel", -(h8[:, None] == row_head[None, :]).astype(float))
    put("query_sel", h8[:, None] == row_query[None, :])
    put("new_mask", np.where(h8[None, :] <= row_query[:, None], 0.0, NEG))
    put("idx_sel", (i[:32, None] % DEC_SEQ) == h8[None, :])
    s = np.arange(SAMP)
    put("page_tri", (s[:, None] // N_PAGES == s[None, :] // N_PAGES) & (s[:, None] < s[None, :]))
    put("tok_tri", (s[:, None] // DEC_SEQ == s[None, :] // DEC_SEQ) & (s[:, None] <= s[None, :]))
    put("same_batch", s[:, None] // DEC_SEQ == s[None, :] // DEC_SEQ)
    second = (row_head >= FOX) & (row_head % 2 == 1)
    put("is_first", ~second[:, None])
    put("is_second", -second[:, None].astype(float))
    put("minus_half", np.full((P, 16), -0.5))
    put("ones", np.ones((P, P)))
    pos = np.concatenate([np.arange(SEQ), np.tile(PAST_LEN + np.arange(DEC_SEQ), DEC_BATCH), np.zeros(SAMP)])
    expo = -np.arange(HALF, dtype=np.float32) * np.float32(2.0 / HEAD_DIM)
    inv = np.power(np.float32(10000.0), expo).astype(np.float32)
    ang = (pos.astype(np.float32)[:, None] * inv[None, :]).astype(np.float64)
    tile = lambda a: a.reshape(NT, P, HALF).transpose(1, 0, 2).reshape(P, NT * HALF)
    put("cos", tile(np.cos(ang)))
    put("sin", tile(np.sin(ang)))
    put("minus_sin", tile(-np.sin(ang)))
    return np.ascontiguousarray(np.concatenate(cols, axis=1)), at


CONST, CONST_AT = constant_table()


class Steps:

    def __init__(self, eng, sem, before=0):
        self.eng, self.sem, self.before, self.n = eng, sem, before, 0

    def ok(self, ins):
        self.n += 1
        return ins.then_inc(self.sem, 1)

    def wait(self):
        self.eng.wait_ge(self.sem, self.before + self.n)


class Kernel:
    pass


class Weights:

    SIZE = 4 * BANK

    def __init__(self, K, sem):
        self.K, self.tiles, self.issued, self.counts, self.landed = K, [], 0, [0, 0], []
        self.sem_landed = [sem("weights_landed_0"), sem("weights_landed_1")]
        self.split_hi, self.split_lo = sem("weights_split_hi"), sem("weights_split_lo")
        self.used = {}

    def add(self, parts):
        n = len(self.tiles)
        pieces = parts(self.K.w_raw[:, n % 2, :])
        self.tiles.append(pieces)
        self.counts[n % 2] += 16 * len(pieces)
        self.landed.append(self.counts[n % 2])
        return n

    def load_up_to(self, sp, last):
        while self.issued <= min(last, len(self.tiles) - 1):
            n = self.issued
            if n >= 2:
                sp.wait_ge(self.split_lo, n - 1)
            for dst, src in self.tiles[n]:
                sp.dma_start(dst, src).then_inc(self.sem_landed[n % 2], 16)
            self.issued += 1

    def hi(self, act, n, landed_more=0):
        if n < len(self.tiles):
            act.wait_ge(self.sem_landed[n % 2], self.landed[n] + landed_more)
            act.activation(self.K.w_hi[:, n % 2, :], self.K.w_raw[:, n % 2, :], ACT.Copy).then_inc(self.split_hi, 1)

    def lo(self, dve, n, count_more=0):
        if n < len(self.tiles):
            dve.wait_ge(self.split_hi, n + 1 + count_more)
            dve.tensor_tensor(self.K.w_lo[:, n % 2, :], self.K.w_raw[:, n % 2, :],
                              self.K.w_hi[:, n % 2, :].bitcast(F32), ALU.subtract).then_inc(self.split_lo, 1)

    def split_after(self, eng, n, half):
        if n + 2 < len(self.tiles):
            eng.wait_ge(*self.used[n])
            half(eng, n + 2)

    def parts_of(self, n):
        return self.K.w_hi[:, n % 2, :], self.K.w_lo[:, n % 2, :]

    def ready(self, eng, n, more=0):
        eng.wait_ge(self.split_lo, n + 1 + more)


def three_passes(pe, out, lhs, rhs, start, stop):
    pe.matmul(out, lhs[0], rhs[1], start=start, stop=False)
    pe.matmul(out, lhs[1], rhs[0], start=False, stop=False)
    return pe.matmul(out, lhs[0], rhs[0], start=False, stop=stop)


def column_tile(w, k0, kn, c0, cn):
    def parts(slot):
        view = slot[:, 0:kn * cn].rearrange("p (k n) -> p k n", k=kn)
        return [(view, w[k0 * P:(k0 + kn) * P, c0:c0 + cn].rearrange("(k p) n -> p k n", p=P))]
    return parts


def gate_up_tile(wg, wu, c0):
    def parts(slot):
        view = slot.rearrange("p (a k n) -> p a k n", a=2, k=KC)
        return [(view[:, a], w[:, c0:c0 + P].rearrange("(k p) n -> p k n", p=P)) for a, w in enumerate((wg, wu))]
    return parts


def load_inputs(nc, K):
    dma, small = K.sem("tokens_landed"), K.sem("small_landed")
    with nc.Block() as block:
        @block.sync
        def _(sp):
            sp.dma_start(K.resid[:, 0:PT, :], K.x_prompt[0].rearrange("(t p) d -> p t d", p=P)).then_inc(dma, 16)
            sp.dma_start(K.resid[0:SAMP, PT, :], K.x_sample.rearrange("b t d -> (b t) d")).then_inc(dma, 16)
            sp.dma_start(K.const[:, :], K.const_in).then_inc(dma, 16)
            K.weights.load_up_to(sp, 3)
            sp.wait_ge(dma, 48)

        @block.scalar
        def _(act):
            pairs = [(K.head_gain[:, i, :], g.partition_broadcast(P)) for i, g in enumerate(K.head_gains)]
            pairs += [(K.subln_row[:, :], K.subln0.partition_broadcast(P)),
                      (K.bias_f[:, :], K.b_f0.partition_broadcast(P)),
                      (K.pages[:, :], K.page_table.rearrange("(a b) n -> a (b n)", a=1)),
                      (K.page_rows[:, :], K.page_table.rearrange("b (n a) -> (b n) a", a=1)),
                      (K.subln_col[:, :], K.subln0.rearrange("(p a) -> p a", a=1))]
            pairs += [(K.lams[:, i, :], g.partition_broadcast(P)) for i, g in enumerate(K.lam_vecs)]
            with nc.allow_non_contiguous_dma(reason="gains by feature: 16 KB once"):
                for i, g in enumerate(K.norm_gains):
                    pairs.append((K.gain_cols[:, i, :], g.rearrange("(c p) -> p c", p=P)))
                for dst, src in pairs:
                    act.dma_start(dst, src).then_inc(small, 16)
            for n in range(2):
                K.weights.hi(act, n)
            act.wait_ge(small, 16 * len(pairs))

        @block.vector
        def _(dve):
            for n in range(2):
                K.weights.lo(dve, n)


def norm_to_features(nc, K, gain, tag):
    squared, mean_ok, rstd_ok, scaled = (K.sem(f"{tag}_{x}") for x in ("squared", "mean_ok", "rstd_ok", "scaled"))
    turned, out_act, out_dve = (K.sem(f"{tag}_{x}") for x in ("turned", "out_act", "out_dve"))
    with ExitStack() as mem:
        sb = lambda name, shape: mem.enter_context(nc.sbuf_tensor(f"{tag}_{name}", shape, F32))
        square = sb("square", [P, D_MODEL])
        ms = sb("ms", [P, NT])
        rstd = sb("rstd", [P, NT])
        xn = sb("xn", [P, 2, D_MODEL])
        block = mem.enter_context(nc.Block())

        def out_of_psum(eng):
            for t in range(NT):
                n = rows_of(t)
                yield t
                for half in range(2):
                    u = 2 * t + half
                    eng.wait_ge(turned, u + 1)
                    if eng is nc.vector:
                        eng.wait_ge(out_act, u + 1)
                    for j in range(4):
                        c = 4 * half + j
                        src = K.ps[:, u % 4, j * P:j * P + n]
                        hi, lo = (x[:, c, t * P:t * P + n] for x in (K.feat_hi, K.feat_lo))
                        g = K.gain_cols[:, gain, c:c + 1]
                        if eng is nc.vector:
                            ins = eng.scalar_tensor_tensor(out=lo, in0=src, scalar=g, in1=hi.bitcast(F32),
                                                           op0=ALU.mult, op1=ALU.subtract)
                        else:
                            ins = eng.activation(hi, src, ACT.Copy, scale=g)
                    ins.then_inc(out_dve if eng is nc.vector else out_act, 1)

        @block.scalar
        def _(act):
            for t in range(NT):
                n = rows_of(t)
                if t:
                    act.wait_ge(squared, t)
                act.activation(square[0:n, :], K.resid[0:n, t, :], ACT.Square,
                               accum_out=ms[0:n, t:t + 1]).then_inc(squared, 1)
            for _t in out_of_psum(act):
                pass

        @block.gpsimd
        def _(pool):
            for t in range(NT):
                n = rows_of(t)
                pool.wait_ge(mean_ok, t + 1)
                pool.tensor_tensor(rstd[0:n, t:t + 1], ms[0:n, t:t + 1], K.c("minus_half")[0:n, 0:1],
                                   ALU.pow).then_inc(rstd_ok, 1)

        @block.vector
        def _(dve):
            for t in range(NT):
                n = rows_of(t)
                dve.wait_ge(squared, t + 1)
                dve.tensor_scalar(ms[0:n, t:t + 1], ms[0:n, t:t + 1], 1.0 / D_MODEL, EPS, ALU.mult, ALU.add)\
                   .then_inc(mean_ok, 1)
            out = out_of_psum(dve)
            for t in range(NT):
                n = rows_of(t)
                dve.wait_ge(rstd_ok, t + 1)
                if t >= 2:
                    dve.wait_ge(turned, 2 * (t - 1))
                dve.tensor_scalar(xn[0:n, t % 2, :], K.resid[0:n, t, :], rstd[0:n, t:t + 1], None, ALU.mult)\
                   .then_inc(scaled, 1)
                if t >= 1:
                    next(out)
            for _t in out:
                pass

        @block.tensor
        def _(pe):
            for t in range(NT):
                n = rows_of(t)
                pe.wait_ge(scaled, t + 1)
                for half in range(2):
                    if t >= 2:
                        pe.wait_ge(out_dve, 2 * t + half - 3)
                    for j in range(4):
                        c = 4 * half + j
                        ins = pe.transpose(K.ps[:, (2 * t + half) % 4, j * P:j * P + n],
                                           xn[0:n, t % 2, c * P:(c + 1) * P], K.c("ident")[0:n, 0:n])
                    ins.then_inc(turned, 1)


class Part:

    def __init__(self, tiles, width, heads=0, norm=None, rope=False, stores=(), turns=(), copies=(), paired=False):
        self.paired = paired
        self.tiles, self.width, self.heads, self.norm, self.rope = tiles, width, heads, norm, rope
        self.stores, self.turns, self.copies = stores, turns, copies


class Item:

    def __init__(self, part, t):
        self.p, self.t, self.rows = part, t, rows_of(t)
        self.norm = self.head = self.ready = self.copy = None


def project(nc, K, parts, tag):
    names = ("multiplied", "squared", "mean_ok", "rstd_ok", "gained", "psum_free", "roped", "turned",
             "turned_out", "copied", "chain", "copies_stored", "passed")
    S = {n: K.sem(f"{tag}_{n}") for n in names}
    stored = [K.sem(f"{tag}_stored_{i}") for i in range(3)]
    items = [(p, t) for p in parts for t in range(NT)]
    n_norm = n_rope = n_head = n_copy = 0
    info = []
    for p, t in items:
        it = Item(p, t)
        if p.heads:
            it.head = n_head
            n_head += 1
            if p.norm is not None:
                it.norm = n_norm
                n_norm += 1
            if p.rope:
                n_rope += 1
                it.ready = (S["roped"], n_rope)
            else:
                it.ready = (S["gained"], n_norm)
        if p.copies:
            it.copy = n_copy
            n_copy += 1
        info.append(it)
    store_count = [0, 0, 0]
    for it in info:
        it.store_before = None
        if it.head is not None:
            it.store_before = store_count[it.head % 3]
            if it.p.stores:
                store_count[it.head % 3] += 16
    W = K.weights
    n_passed = 0
    for i, p in enumerate(parts):
        for n, _ in p.tiles[:-1]:
            n_passed += 1
            W.used[n] = (S["passed"], n_passed)
        W.used[p.tiles[-1][0]] = (S["multiplied"], NT * (i + 1))

    def splits(eng, half, i):
        p, t = items[i]
        for n, _ in p.tiles[:-1] if t == 0 else p.tiles[-1:] if t == NT - 1 else ():
            W.split_after(eng, n, half)
    copy_stores = sum(len([c for c in it.p.copies if c[2 if it.t < PT else 3] is not None]) for it in info)
    heads = [it for it in info if it.head is not None]

    with ExitStack() as mem:
        sb = lambda name, shape: mem.enter_context(nc.sbuf_tensor(f"{tag}_{name}", shape, F32))
        square = sb("square", [P, 2, BANK])
        ms = sb("ms", [P, 2, 8])
        rstd = sb("rstd", [P, 2, 8])
        xn = sb("xn", [P, 2, BANK])
        straight = sb("straight", [P, BANK])
        crossed = sb("crossed", [P, BANK])
        res = sb("res", [P, 3, BANK])
        block = mem.enter_context(nc.Block())

        def res_free(eng, it):
            if it.head >= 3:
                eng.wait_ge(S["turned"], it.head - 2)
                if it.store_before:
                    eng.wait_ge(stored[it.head % 3], it.store_before)

        @block.sync
        def _(sp):
            W.load_up_to(sp, parts[-1].tiles[-1][0] + 2)

        @block.tensor
        def _(pe):
            def turn(it):
                pe.wait_ge(*it.ready)
                if it.head >= 2:
                    pe.wait_ge(S["turned_out"], it.head - 1)
                for j, (src, _, _) in enumerate(it.p.turns):
                    n = it.rows
                    ins = pe.transpose(K.ps[:, 6 + it.head % 2, j * P:j * P + n], src(res[0:n, it.head % 3, :]),
                                       K.c("ident")[0:n, 0:n])
                ins.then_inc(S["turned"], 1)

            MAIN = 6
            for b, p in enumerate(parts):
                block_items = info[b * NT:(b + 1) * NT]
                for a, (tile, chunks) in enumerate(p.tiles):
                    W.ready(pe, tile)
                    hi, lo = (x[:, 0:len(chunks) * p.width].rearrange("p (k n) -> p k n", n=p.width)
                              for x in W.parts_of(tile))
                    last = a == len(p.tiles) - 1
                    for t, it in enumerate(block_items):
                        i, n = b * NT + t, it.rows
                        if a == 0 and i >= MAIN:
                            pe.wait_ge(S["psum_free"], i - MAIN + 1)
                        for k, c in enumerate(chunks):
                            cols = slice(t * P, t * P + n)
                            ins = three_passes(pe, K.ps[0:n, i % MAIN, 0:p.width],
                                               (K.feat_hi[:, c, cols], K.feat_lo[:, c, cols]), (hi[:, k, :], lo[:, k, :]),
                                               c == 0, c == KC - 1)
                        if last:
                            ins.then_inc(S["multiplied"], 1)
                        elif t == NT - 1:
                            ins.then_inc(S["passed"], 1)
                        if ((a == 0 and t < 2) or (last and t >= 2)) and i >= 2 and info[i - 2].head is not None:
                            turn(info[i - 2])
            for it in info[-2:]:
                if it.head is not None:
                    turn(it)

        @block.scalar
        def _(act):
            def turn_out(it):
                act.wait_ge(S["turned"], it.head + 1)
                n = it.rows
                todo = it.p.turns
                for j, (_, dst, scale) in enumerate(todo):
                    src = K.ps[:, 6 + it.head % 2, j * P:j * P + n]
                    ins = act.activation(dst(it.t), src, ACT.Copy, scale=scale)
                ins.then_inc(S["turned_out"], 1)

            def store(it):
                act.wait_ge(*it.ready)
                for sl, dst in it.p.stores:
                    act.dma_start(dst(it.t), res[0:it.rows, it.head % 3, sl]).then_inc(stored[it.head % 3], 16)

            def store_copies(it):
                act.wait_ge(S["copied"], it.copy + 1)
                for c in it.p.copies:
                    dram = c[2 if it.t < PT else 3]
                    if dram is not None:
                        act.dma_start(dram(it.t), c[1](it.t)).then_inc(S["copies_stored"], 16)

            def after(i):
                if i >= 1:
                    it = info[i - 1]
                    if it.p.stores:
                        store(it)
                    if it.copy is not None:
                        store_copies(it)
                if i >= 2 and info[i - 2].head is not None:
                    turn_out(info[i - 2])

            for i, it in enumerate(info):
                splits(act, W.hi, i)
                if it.norm is not None:
                    act.wait_ge(S["multiplied"], i + 1)
                    if it.norm >= 2:
                        act.wait_ge(S["mean_ok"], it.norm - 1)
                    act.activation(square[0:it.rows, it.norm % 2, 0:it.p.heads], K.ps[0:it.rows, i % 6, 0:it.p.heads],
                                   ACT.Square).then_inc(S["squared"], 1)
                after(i)
            after(len(info))
            if info[-1].head is not None:
                turn_out(info[-1])
            for s, n in zip(stored, store_count):
                if n:
                    act.wait_ge(s, n)
            if copy_stores:
                act.wait_ge(S["copies_stored"], 16 * copy_stores)

        @block.gpsimd
        def _(pool):
            for it in heads:
                if it.norm is None:
                    continue
                n, m, nh = it.rows, it.norm, it.p.heads // HEAD_DIM
                pool.wait_ge(S["mean_ok"], m + 1)
                pool.tensor_tensor(rstd[0:n, m % 2, 0:nh], ms[0:n, m % 2, 0:nh], K.c("minus_half")[0:n, 0:nh],
                                   ALU.pow).then_inc(S["rstd_ok"], 1)
                pool.wait_ge(S["psum_free"], info.index(it) + 1)
                view = xn[0:n, m % 2, 0:it.p.heads].rearrange("p (h d) -> p h d", d=HEAD_DIM)
                gain = bc(K.head_gain[0:n, it.p.norm, :], 1, nh)
                if it.p.rope:
                    dst = view
                else:
                    res_free(pool, it)
                    dst = res[0:n, it.head % 3, 0:it.p.heads].rearrange("p (h d) -> p h d", d=HEAD_DIM)
                pool.tensor_tensor(dst, view, gain, ALU.mult).then_inc(S["gained"], 1)

        @block.vector
        def _(dve):
            s = Steps(dve, S["chain"])
            for i, it in enumerate(info):
                splits(dve, W.lo, i)
                n, p, t = it.rows, it.p, it.t
                ps = K.ps[0:n, i % 6, :]
                nh = p.heads // HEAD_DIM
                if it.norm is not None:
                    m = it.norm
                    dve.wait_ge(S["squared"], m + 1)
                    if m >= 2:
                        dve.wait_ge(S["rstd_ok"], m - 1)
                    s.ok(dve.tensor_reduce(ms[0:n, m % 2, 0:nh],
                                           square[0:n, m % 2, 0:p.heads].rearrange("p (h d) -> p h d", d=HEAD_DIM),
                                           AX, ALU.add))
                    s.wait()
                    dve.tensor_scalar(ms[0:n, m % 2, 0:nh], ms[0:n, m % 2, 0:nh], 1.0 / HEAD_DIM, EPS,
                                      ALU.mult, ALU.add).then_inc(S["mean_ok"], 1)
                else:
                    dve.wait_ge(S["multiplied"], i + 1)
                if p.copies:
                    for k, (sl, dst, _, _, how) in enumerate(p.copies):
                        ins = how(dve, dst(t), ps[:, sl], s) if how else dve.tensor_copy(dst(t), ps[:, sl])
                        if k < len(p.copies) - 1:
                            s.ok(ins)
                    ins.then_inc(S["copied"], 1)
                src = None
                if it.norm is not None:
                    dve.wait_ge(S["rstd_ok"], m + 1)
                    if m >= 2:
                        dve.wait_ge(S["gained"], m - 1)
                    if p.rope and m >= 2:
                        s.wait()
                    src = xn[0:n, m % 2, 0:p.heads].rearrange("p (h d) -> p h d", d=HEAD_DIM)
                    dve.tensor_tensor(src, ps[:, 0:p.heads].rearrange("p (h d) -> p h d", d=HEAD_DIM),
                                      bc(rstd[0:n, m % 2, 0:nh], 2, HEAD_DIM), ALU.mult).then_inc(S["psum_free"], 1)
                    if p.rope:
                        dve.wait_ge(S["gained"], m + 1)
                elif p.heads:
                    src = ps[:, 0:p.heads].rearrange("p (h d) -> p h d", d=HEAD_DIM)
                if p.rope:
                    four = src.rearrange("p h (a d) -> p h a d", a=2)
                    st = straight[0:n, 0:p.heads].rearrange("p (h a d) -> p h a d", a=2, d=HALF)
                    cr = crossed[0:n, 0:p.heads].rearrange("p (h a d) -> p h a d", a=2, d=HALF)
                    cos, sin, msin = (K.c(x)[0:n, t * HALF:(t + 1) * HALF] for x in ("cos", "sin", "minus_sin"))
                    s.wait()
                    for a in range(2):
                        s.ok(dve.tensor_tensor(st[:, :, a, :], four[:, :, a, :], bc(cos, 1, nh), ALU.mult))
                    s.ok(dve.tensor_tensor(cr[:, :, 0, :], four[:, :, 1, :], bc(msin, 1, nh), ALU.mult))
                    ins = dve.tensor_tensor(cr[:, :, 1, :], four[:, :, 0, :], bc(sin, 1, nh), ALU.mult)
                    if it.norm is None:
                        ins.then_inc(S["psum_free"], 1)
                        dve.wait_ge(S["psum_free"], i + 1)
                    else:
                        s.ok(ins)
                    s.wait()
                    res_free(dve, it)
                    if p.heads == 5 * HEAD_DIM:
                        s.ok(dve.tensor_tensor(res[0:n, it.head % 3, p.heads:p.heads + HEAD_DIM],
                                               straight[0:n, p.heads - HEAD_DIM:p.heads],
                                               crossed[0:n, p.heads - HEAD_DIM:p.heads], ALU.add))
                        s.wait()
                    dst, a, b = res[0:n, it.head % 3, 0:p.heads], straight[0:n, 0:p.heads], crossed[0:n, 0:p.heads]
                    if p.paired:
                        dst = dst.rearrange("p (r a d) -> p a r d", a=2, d=HEAD_DIM)
                        a, b = (x.rearrange("p (a r d) -> p a r d", a=2, d=HEAD_DIM) for x in (a, b))
                    dve.tensor_tensor(dst, a, b, ALU.add).then_inc(S["roped"], 1)
                    dve.wait_ge(*it.ready)
                elif not p.heads:
                    dve.wait_ge(S["copied"], it.copy + 1)
                    dve.sem_inc(S["psum_free"], 1)


def forget_sums(nc, K):
    S = {n: K.sem("sums_" + n) for n in ("chain", "scanned", "summed", "out", "scratch", "broadcast", "lam_sum", "lam_exp")}
    S["pages_in"] = nc.alloc_semaphore(name="sums_pages_in")
    with ExitStack() as mem:
        sb = lambda name, shape: mem.enter_context(nc.sbuf_tensor("sums_" + name, shape, F32))
        page_logf = sb("page_logf", [SAMP, PAGE_SIZE * FOX])
        page_cum = sb("page_cum", [SAMP, FOX, PAGE_SIZE])
        zero = sb("zero", [SAMP, PAGE_SIZE])
        total = sb("total", [SAMP, FOX])
        carry = sb("carry", [SAMP, FOX])
        prompt_row = sb("prompt_row", [FOX, SEQ])
        new_row = sb("new_row", [FOX, SAMP])
        prod = sb("prod", [P, HEAD_DIM])
        lam_sum = sb("lam_sum", [P, 2])
        lam_exp = sb("lam_exp", [P, 2])
        block = mem.enter_context(nc.Block())
        CP, CARRY, NEW = K.ps[0:FOX, 0, :], K.ps[0:SAMP, 1, 0:FOX], K.ps[0:FOX, 2, 0:SAMP]
        scr = K.fox_rows

        @block.gpsimd
        def _(pool):
            pool.indirect_dma_start(page_logf[:, :], None, K.cache_l0_logf.rearrange("n k h -> n (k h)"),
                                    bass.IndirectOffsetOnAxis(ap=K.page_rows[:, 0:1], axis=0)).then_inc(S["pages_in"], 16)

        @block.tensor
        def _(pe):
            for t in range(PT):
                ins = pe.matmul(CP[:, t * P:SEQ], K.logf[:, t, :], K.c("step")[:, 0:SEQ - t * P],
                                start=(t == 0), stop=(t == PT - 1))
            ins.then_inc(S["summed"], 1)
            pe.wait_ge(S["scanned"], 1)
            pe.matmul(CARRY, K.c("page_tri")[0:SAMP, :], total[:, :], start=True, stop=True).then_inc(S["summed"], 1)
            pe.matmul(NEW, K.logf[0:SAMP, PT, :], K.c("tok_tri")[0:SAMP, :], start=True, stop=False)
            pe.matmul(NEW, total[:, :], K.c("same_batch")[0:SAMP, :], start=False, stop=True).then_inc(S["summed"], 1)

        @block.scalar
        def _(act):
            act.wait_ge(S["lam_sum"], 2)
            act.activation(lam_exp[:, :], lam_sum[:, :], ACT.Exp).then_inc(S["lam_exp"], 1)

        @block.vector
        def _(dve):
            s = Steps(dve, S["chain"])
            s.ok(dve.memset(zero[:, :], 0.0))
            for i in range(2):
                if i:
                    dve.wait_ge(S["lam_sum"], 1)
                dve.tensor_tensor_reduce(prod[:, :], K.lams[:, 2 * i, :], K.lams[:, 2 * i + 1, :], 1.0, 0.0,
                                         ALU.mult, ALU.add, lam_sum[:, i:i + 1]).then_inc(S["lam_sum"], 1)
            dve.wait_ge(S["summed"], 1)
            dve.tensor_scalar(prompt_row[:, :], CP, -1.0, None, ALU.mult).then_inc(S["out"], 1)
            dve.wait_ge(S["pages_in"], 16)
            s.wait()
            by_head = page_logf[:, :].rearrange("p (k h) -> p h k", h=FOX)
            for h in range(FOX):
                s.ok(dve.tensor_tensor_scan(page_cum[:, h, :], by_head[:, h, :], zero[:, :], 0.0, ALU.add, ALU.add))
            s.wait()
            dve.tensor_copy(total[:, :], page_cum[:, :, PAGE_SIZE - 1]).then_inc(S["scanned"], 1)
            dve.wait_ge(S["summed"], 2)
            s.ok(dve.tensor_copy(carry[:, :], CARRY))
            s.wait()
            dve.wait_ge(S["scanned"], 1)
            dve.tensor_tensor(page_cum[:, :, :], page_cum[:, :, :], bc(carry[:, :], 2, PAGE_SIZE), ALU.add)\
               .then_inc(S["out"], 1)
            dve.wait_ge(S["summed"], 3)
            dve.tensor_copy(new_row[:, :], NEW).then_inc(S["out"], 1)
            dve.wait_ge(S["lam_exp"], 1)
            s.ok(dve.tensor_scalar(K.lam[:, :], lam_exp[:, 0:1], lam_exp[:, 1:2], LAMBDA_INIT, ALU.subtract, ALU.add))
            s.wait()
            s.ok(dve.tensor_scalar(K.coef[:, :], K.c("is_second"), K.lam[:, 0:1], K.c("is_first"),
                                   ALU.mult, ALU.add))
            s.ok(dve.tensor_scalar(K.minus_lam[:, :], K.lam[:, :], -1.0, None, ALU.mult))
            s.ok(dve.tensor_scalar(K.subln_col8[:, :], K.subln_col[:, :], 1.0 - LAMBDA_INIT, None, ALU.mult))
            s.ok(dve.tensor_scalar(K.subln_row8[:, :], K.subln_row[:, :], 1.0 - LAMBDA_INIT, None, ALU.mult))
            s.wait()

        @block.sync
        def _(sp):
            sp.wait_ge(S["out"], 1)
            sp.dma_start(K.prompt_rows, prompt_row[:, :]).then_inc(S["scratch"], 16)
            sp.wait_ge(S["scratch"], 16)
            sp.dma_start(K.minus_c[:, :, :], K.prompt_rows.partition_broadcast(P)).then_inc(S["broadcast"], 16)
            sp.wait_ge(S["out"], 2)
            for b in range(DEC_BATCH):
                dst = scr[b, :, 0:PAST_LEN].rearrange("h (j k) -> j h k", j=N_PAGES)
                sp.dma_start(dst, page_cum[b * N_PAGES:(b + 1) * N_PAGES, :, :]).then_inc(S["scratch"], 16)
            sp.wait_ge(S["out"], 3)
            sp.dma_start(scr[:, :, PAST_LEN:KEYS].rearrange("b h t -> h b t"),
                         new_row[:, :].rearrange("h (b t) -> h b t", b=DEC_BATCH)).then_inc(S["scratch"], 16)
            sp.wait_ge(S["scratch"], 16 * (2 + DEC_BATCH))
            sp.wait_ge(S["broadcast"], 16)


def prompt_attention(nc, K, tag, q_at, k_at, v_at, bias_at, diag, out_at, second):
    names = ("scored", "shifted", "exped", "turned", "turned_out", "weighed", "out", "chain")
    S = {n: K.sem(f"{tag}_{n}") for n in names}
    units = [(h, qt) for h in range(HEADS) for qt in range(PT)]
    n = len(units)
    with ExitStack() as mem:
        sb = lambda name, shape: mem.enter_context(nc.sbuf_tensor(f"{tag}_{name}", shape, F32))
        scores = sb("scores", [P, 3, SEQ])
        probs = sb("probs", [P, 3, SEQ])
        probs_t = sb("probs_t", [P, 3, SEQ])
        top, minus, total, scale, scale2 = (sb(x, [P, n]) for x in ("top", "minus", "total", "scale", "scale2"))
        block = mem.enter_context(nc.Block())

        @block.tensor
        def _(pe):
            for u in range(n + 3):
                if u < n:
                    h, qt = units[u]
                    if u >= 3:
                        pe.wait_ge(S["exped"], u - 2)
                    w = (qt + 1) * P
                    pe.matmul(K.ps[:, u % 3, 0:w], q_at(h, qt), k_at(h)[:, 0:w], start=True, stop=True)\
                      .then_inc(S["scored"], 1)
                if 2 <= u < n + 2:
                    v = u - 2
                    pe.wait_ge(S["exped"], v + 1)
                    if v >= 3:
                        pe.wait_ge(S["turned_out"], v - 2)
                    for j in range(units[v][1] + 1):
                        ins = pe.transpose(K.ps[:, 3 + v % 3, j * P:(j + 1) * P], probs[:, v % 3, j * P:(j + 1) * P],
                                           K.c("ident"))
                    ins.then_inc(S["turned"], 1)
                if u >= 3:
                    v = u - 3
                    h, qt = units[v]
                    pe.wait_ge(S["turned_out"], v + 1)
                    if v >= 2:
                        pe.wait_ge(S["out"], v - 1)
                    for j in range(qt + 1):
                        val = v_at(h, j)
                        ins = pe.matmul(K.ps[:, 6 + v % 2, 0:val.shape[1]], probs_t[:, v % 3, j * P:(j + 1) * P], val,
                                        start=(j == 0), stop=(j == qt))
                    ins.then_inc(S["weighed"], 1)

        @block.scalar
        def _(act):
            for u in range(n + 2):
                if u < n:
                    h, qt = units[u]
                    w = (qt + 1) * P
                    act.wait_ge(S["shifted"], u + 1)
                    if u >= 3:
                        act.wait_ge(S["turned"], u - 2)
                    src = scores[:, u % 3, 0:w] if bias_at(h, qt) is not None else K.ps[:, u % 3, 0:w]
                    act.activation(probs[:, u % 3, 0:w], src, ACT.Exp, bias=minus[:, u:u + 1],
                                   accum_out=total[:, u:u + 1]).then_inc(S["exped"], 1)
                if u >= 2:
                    v = u - 2
                    w = (units[v][1] + 1) * P
                    act.wait_ge(S["turned"], v + 1)
                    if v >= 3:
                        act.wait_ge(S["weighed"], v - 2)
                    act.activation(probs_t[:, v % 3, 0:w], K.ps[:, 3 + v % 3, 0:w], ACT.Copy).then_inc(S["turned_out"], 1)

        @block.vector
        def _(dve):
            s = Steps(dve, S["chain"])
            for u in range(n + 3):
                if u < n:
                    h, qt = units[u]
                    w = (qt + 1) * P
                    ps = K.ps[:, u % 3, 0:w]
                    dve.wait_ge(S["scored"], u + 1)
                    if diag:
                        s.ok(dve.tensor_tensor(ps[:, qt * P:w], ps[:, qt * P:w], K.c("causal"), ALU.add))
                        s.wait()
                    bias = bias_at(h, qt)
                    if bias is not None:
                        if u >= 3:
                            dve.wait_ge(S["exped"], u - 2)
                        s.ok(dve.tensor_tensor_reduce(scores[:, u % 3, 0:w], ps, bias, 1.0, -3e38, ALU.add, ALU.max,
                                                      top[:, u:u + 1]))
                        s.wait()
                        dve.tensor_scalar(minus[:, u:u + 1], top[:, u:u + 1], -1.0, None, ALU.mult)\
                           .then_inc(S["shifted"], 1)
                    else:
                        dve.tensor_reduce(minus[:, u:u + 1], ps, AX, ALU.max, negate=True).then_inc(S["shifted"], 1)
                if u >= 3:
                    v = u - 3
                    h, qt = units[v]
                    dve.wait_ge(S["exped"], v + 1)
                    s.ok(dve.reciprocal(scale[:, v:v + 1], total[:, v:v + 1]))
                    s.wait()
                    dst = out_at(h, qt)
                    acc = K.ps[:, 6 + v % 2, 0:dst.shape[1]]
                    if second(h):
                        s.ok(dve.tensor_scalar(scale2[:, v:v + 1], scale[:, v:v + 1], K.minus_lam[:, 0:1], None,
                                               ALU.mult))
                        s.wait()
                        dve.wait_ge(S["weighed"], v + 1)
                        dve.wait_ge(S["out"], v + 1 - PT)
                        dve.scalar_tensor_tensor(out=dst, in0=acc, scalar=scale2[:, v:v + 1], in1=dst,
                                                 op0=ALU.mult, op1=ALU.add).then_inc(S["out"], 1)
                    else:
                        dve.wait_ge(S["weighed"], v + 1)
                        dve.tensor_scalar(dst, acc, scale[:, v:v + 1], None, ALU.mult).then_inc(S["out"], 1)


def turn_attention(nc, K, att, tag, subln):
    S = {n: K.sem(f"{tag}_{n}") for n in ("squared", "mean_ok", "rstd_ok", "normed", "chain", "turned", "out_act", "out_dve")}
    with ExitStack() as mem:
        sb = lambda name, shape: mem.enter_context(nc.sbuf_tensor(f"{tag}_{name}", shape, F32))
        if subln:
            square = sb("square", [P, 2, DIFF * P])
            ms = sb("ms", [P, PT, DIFF])
            rstd = sb("rstd", [P, PT, DIFF])
        block = mem.enter_context(nc.Block())

        def feat_part(feat, u):
            return feat[:, 4 * (u % 2):4 * (u % 2) + 4, u // 2 * P:(u // 2 + 1) * P]

        @block.tensor
        def _(pe):
            for t in range(PT):
                for half in range(2):
                    if subln and half:
                        pe.wait_ge(S["normed"], t + 1)
                    for j in range(4):
                        c = 4 * half + j
                        ins = pe.transpose(K.ps[:, 2 * t + half, j * P:(j + 1) * P], att[:, t, c * P:(c + 1) * P],
                                           K.c("ident"))
                    ins.then_inc(S["turned"], 1)

        @block.scalar
        def _(act):
            if subln:
                for t in range(PT):
                    if t >= 2:
                        act.wait_ge(S["mean_ok"], t - 1)
                    act.activation(square[:, t % 2, :], att[:, t, BANK:], ACT.Square).then_inc(S["squared"], 1)
            for u in range(2 * PT):
                act.wait_ge(S["turned"], u + 1)
                act.activation(feat_part(K.feat_hi, u), K.ps[:, u, :].rearrange("p (c n) -> p c n", c=4), ACT.Copy)\
                   .then_inc(S["out_act"], 1)

        @block.gpsimd
        def _(pool):
            if subln:
                for t in range(PT):
                    pool.wait_ge(S["mean_ok"], t + 1)
                    pool.tensor_tensor(rstd[:, t, :], ms[:, t, :], K.c("minus_half")[:, 0:DIFF], ALU.pow)\
                        .then_inc(S["rstd_ok"], 1)

        @block.vector
        def _(dve):
            s = Steps(dve, S["chain"])
            if subln:
                for t in range(PT):
                    dve.wait_ge(S["squared"], t + 1)
                    s.ok(dve.tensor_reduce(ms[:, t, :], square[:, t % 2, :].rearrange("p (h d) -> p h d", h=DIFF),
                                           AX, ALU.add))
                    s.wait()
                    dve.tensor_scalar(ms[:, t, :], ms[:, t, :], 1.0 / P, EPS, ALU.mult, ALU.add).then_inc(S["mean_ok"], 1)
                for t in range(PT):
                    view = att[:, t, BANK:].rearrange("p (h d) -> p h d", h=DIFF)
                    dve.wait_ge(S["rstd_ok"], t + 1)
                    s.ok(dve.tensor_tensor(view, view, bc(rstd[:, t, :], 2, P), ALU.mult))
                    s.wait()
                    dve.tensor_tensor(view, view, bc(K.subln_row8[:, :], 1, DIFF), ALU.mult).then_inc(S["normed"], 1)
            dve.wait_ge(S["turned"], 2 * PT)
            for u in range(2 * PT):
                dve.wait_ge(S["out_act"], u + 1)
                dve.tensor_tensor(feat_part(K.feat_lo, u), K.ps[:, u, :].rearrange("p (c n) -> p c n", c=4),
                                  feat_part(K.feat_hi, u).bitcast(F32), ALU.subtract).then_inc(S["out_dve"], 1)


def sample_attention(nc, K, tag, cache_k, cache_v, new_v, row_bias, bias_sel, width, chunks, fill_q, new_k, new_mask,
                     coef, out):
    names = ("q_ok", "turned_act", "turned_dve", "kt_act", "kt_dve", "scored", "new_out", "shifted",
             "exped", "scaled", "pt_turned", "pt_act", "pt_dve", "weighed", "o_copied", "o_turned", "chain", "chain_act",
             "new_v_in", "bias_in")
    S = {n: K.sem(f"{tag}_{n}") for n in names}
    k_in = [K.sem(f"{tag}_k_in_{j}") for j in range(N_PAGES)]
    v_in = [K.sem(f"{tag}_v_in_{j}") for j in range(N_PAGES)]
    per_bank = BANK // P // chunks if chunks <= 4 else 0
    units = [((j,), range(4 * a, 4 * a + 4)) for j in range(N_PAGES) for a in range(chunks // 4)] if chunks >= 4 else \
            [(range(j, j + per_bank), range(chunks)) for j in range(0, N_PAGES, per_bank)]
    half_units = len(units) // 2
    rows4 = [slice(32 * i, 32 * i + 32) for i in range(4)]
    group_chunks = [(2 * i, 2 * i + 1) if chunks == KC else (i // 2,) for i in range(4)]
    vw = width // 4
    with ExitStack() as mem:
        sb = lambda name, shape: mem.enter_context(nc.sbuf_tensor(f"{tag}_{name}", shape, F32))
        kslot = sb("kslot", [P, N_PAGES, width])
        vslot = sb("vslot", [P, N_PAGES, width])
        kt = [half.rearrange("p (c n) -> p c n", n=BANK)[:, 0:chunks, :] for half in (K.kt0[:, :], K.w_raw.rearrange("p a n -> p (a n)"))]
        qz = sb("qz", [P, chunks, P])
        vnew = sb("vnew", [DEC_SEQ, width])
        bias = sb("bias", [DEC_SEQ, KEYS])
        knew = sb("knew", [P, chunks, DEC_SEQ])
        snew = sb("snew", [P, DEC_SEQ])
        probs = sb("probs", [P, KEYS])
        pt = sb("pt", [P, N_PAGES, P])
        ptn = sb("ptn", [DEC_SEQ, P])
        st = sb("st", [P, 8])
        o_sb = sb("o_sb", [P, max(vw, P)])
        block = mem.enter_context(nc.Block())
        SC, NEWS, NEWT, O = K.ps[:, 2:4, :], K.ps[:, 4, 0:DEC_SEQ], K.ps[0:DEC_SEQ, 4, P:2 * P], K.ps[:, 7, 0:vw]
        OT = K.ps[:, 4, 2 * P:4 * P].rearrange("p (x n) -> p x n", x=2)

        n = len(units)
        cuts = (0, 7, 10, 12, 16) if n == 16 else (0, 2, 3, 3, 4)
        assert len(cuts) == 5 and cuts[4] == n and cuts[3] < n
        stretch = [range(cuts[x], cuts[x + 1]) for x in range(4)]
        LAST = DEC_BATCH - 1

        @block.sync
        def _(sp):
            def page_ids(b):
                return [sp.value_load(K.pages[0:1, ds(b * N_PAGES + j, 1)], min_val=0, max_val=cache_k.shape[0] - 1)
                        for j in range(N_PAGES)]

            def load_k(b, ids, pages_of):
                for j in pages_of:
                    i = [n for n, (pages, _) in enumerate(units) if j in pages][-1]
                    sp.wait_ge(S["turned_dve"] if i % 2 else S["turned_act"], b * half_units + i // 2 + 1)
                    sp.dma_start(kslot[:, j, :], cache_k[ds(ids[j], 1), :, :].rearrange("a k d -> (a k) d"))\
                      .then_inc(k_in[j], 16)

            def load_bias(b):
                sp.wait_ge(S["scored"], b * 3 + 1)
                sp.dma_start(bias[:, :], row_bias(b)).then_inc(S["bias_in"], 16)

            def load_v(b, ids):
                sp.wait_ge(S["weighed"], b + 1)
                sp.dma_start(vnew[:, :], new_v(b)).then_inc(S["new_v_in"], 16)
                for j in range(N_PAGES):
                    sp.dma_start(vslot[:, j, :], cache_v[ds(ids[j], 1), :, :].rearrange("a k d -> (a k) d"))\
                      .then_inc(v_in[j], 16)
            load_k(0, page_ids(0), range(N_PAGES))
            load_bias(0)
            with sp.Fori(0, LAST) as b:
                ids, next_ids = page_ids(b), page_ids(b + 1)
                load_k(b + 1, next_ids, range(N_PAGES // 2))
                load_v(b, ids)
                load_k(b + 1, next_ids, range(N_PAGES // 2, N_PAGES))
                load_bias(b + 1)
            load_v(LAST, page_ids(LAST))

        @block.tensor
        def _(pe):
            def turn_k(b, which):
                for i in which:
                    pages, cs = units[i]
                    for j in pages:
                        pe.wait_ge(k_in[j], b * 16 + 16)
                    pe.wait_ge(S["kt_dve"] if i % 2 else S["kt_act"], b * half_units + i // 2 + 1)
                    for x, (j, c) in enumerate((j, c) for c in cs for j in pages):
                        ins = pe.transpose(K.ps[:, i % 2, x * P:(x + 1) * P], kslot[:, j, c * P:(c + 1) * P],
                                           K.c("ident"))
                    ins.then_inc(S["turned_dve"] if i % 2 else S["turned_act"], 1)

            def score_groups(dst, bias_row, keys_at):
                pe.matmul(dst, bias_sel, bias_row, start=True, stop=True)
                for x in range(len(group_chunks[0])):
                    for i in range(4):
                        c = group_chunks[i][x]
                        ins = pe.matmul(dst[rows4[i], :], qz[:, c, rows4[i]], keys_at(c), start=False,
                                        stop=True, skip_group_check=True)
                ins.then_inc(S["scored"], 1)

            def scores(b):
                pe.wait_ge(S["q_ok"], b + 1)
                pe.wait_ge(S["bias_in"], b * 16 + 16)
                for g in range(2):
                    pe.wait_ge(S["kt_act"], (b * 2 + g + 1) * (half_units // 2) + 1)
                    pe.wait_ge(S["kt_dve"], (b * 2 + g + 1) * (half_units // 2) + 1)
                    score_groups(SC[:, g, :], bias[:, g * BANK:(g + 1) * BANK], lambda c: kt[g][:, c, :])
                score_groups(NEWS, bias[:, PAST_LEN:KEYS], lambda c: knew[:, c, :])

            def turn_probs(b):
                pe.wait_ge(S["scaled"], b + 1)
                for g in range(2):
                    for j in range(4):
                        ins = pe.transpose(K.ps[:, 5 + g, j * P:(j + 1) * P],
                                           probs[:, (4 * g + j) * P:(4 * g + j + 1) * P], K.c("ident"))
                    if g == 1:
                        ins = pe.transpose(NEWT, probs[:, PAST_LEN:KEYS], K.c("ident"))
                    ins.then_inc(S["pt_turned"], 1)

            def weigh(b):
                pe.wait_ge(S["new_v_in"], b * 16 + 16)
                pe.wait_ge(S["o_copied"], b + 1)
                pe.wait_ge(S["pt_act"], b + 1)
                pe.wait_ge(S["pt_dve"], b + 1)
                for j in range(N_PAGES):
                    pe.wait_ge(v_in[j], b * 16 + 16)
                    for i in range(4):
                        pe.matmul(O[rows4[i], :], pt[:, j, rows4[i]], vslot[:, j, i * vw:(i + 1) * vw],
                                  start=(j == 0), stop=False)
                for i in range(4):
                    ins = pe.matmul(O[rows4[i], :], ptn[:, rows4[i]], vnew[:, i * vw:(i + 1) * vw],
                                    start=False, stop=True)
                ins.then_inc(S["weighed"], 1)

            def turn_o(b):
                pe.wait_ge(S["o_copied"], b + 2)
                for x in range(0, vw, P):
                    ins = pe.transpose(OT[:, x // P, :], o_sb[:, x:x + P], K.c("ident"))
                ins.then_inc(S["o_turned"], 1)

            pe.sem_inc(S["turned_act"], half_units)
            pe.sem_inc(S["turned_dve"], half_units)
            pe.sem_inc(S["weighed"], 1)
            pe.sem_inc(S["scored"], 1)
            turn_k(0, range(len(units)))
            scores(0)
            with pe.Fori(0, LAST) as b:
                turn_k(b + 1, stretch[0])
                turn_probs(b)
                turn_k(b + 1, stretch[1])
                weigh(b)
                turn_k(b + 1, stretch[2])
                turn_o(b)
                turn_k(b + 1, stretch[3])
                scores(b + 1)
            turn_probs(LAST)
            weigh(LAST)
            turn_o(LAST)

        def kt_out(eng, i, b):
            pages, cs = units[i]
            g = pages[0] // 4
            eng.wait_ge(S["turned_dve"] if i % 2 else S["turned_act"], (b + 1) * half_units + i // 2 + 1)
            j0 = pages[0] % 4
            dst = kt[g][:, cs[0]:cs[-1] + 1, j0 * P:(j0 + len(pages)) * P]
            src = K.ps[:, i % 2, :].rearrange("p (c n) -> p c n", c=len(cs))
            if i % 2:
                eng.tensor_copy(dst, src).then_inc(S["kt_dve"], 1)
            else:
                eng.activation(dst, src, ACT.Copy).then_inc(S["kt_act"], 1)

        @block.scalar
        def _(act):
            act.sem_inc(S["kt_act"], 1)

            def keys(b, which):
                for i in which:
                    if i % 2 == 0:
                        kt_out(act, i, b)

            def exps(b):
                act.wait_ge(S["shifted"], b + 1)
                act.activation(probs[:, 0:PAST_LEN].rearrange("p (g k) -> p g k", g=2), SC, ACT.Exp, bias=st[:, 3:4],
                               accum_out=st[:, 4:5]).then_inc(S["exped"], 1)
                act.activation(probs[:, PAST_LEN:KEYS], snew[:, :], ACT.Exp, bias=st[:, 3:4],
                               accum_out=st[:, 5:6]).then_inc(S["exped"], 1)

            def probs_out(b):
                act.wait_ge(S["pt_turned"], b * 2 + 1)
                act.activation(pt[:, 0:4, :], K.ps[:, 5, :].rearrange("p (j n) -> p j n", j=4), ACT.Copy)\
                   .then_inc(S["pt_act"], 1)
            keys(0, range(len(units)))
            with act.Fori(0, LAST) as b:
                act.wait_ge(S["scored"], b * 3 + 4)
                keys(b + 1, stretch[0][:2])
                exps(b)
                keys(b + 1, stretch[0][2:])
                probs_out(b)
                for x in (1, 2, 3):
                    keys(b + 1, stretch[x])
            exps(LAST)
            probs_out(LAST)

        @block.vector
        def _(dve):
            s0 = Steps(dve, S["chain"])
            s0.ok(dve.memset(qz[:, :, :], 0.0))
            dve.memset(o_sb[:, :], 0.0)
            s0.wait()
            dve.sem_inc(S["kt_dve"], 1)
            dve.sem_inc(S["o_copied"], 1)
            STEPS = 6 + (0 if coef is None else 1)

            def queries(b):
                dve.tensor_copy(knew[:, :, :], new_k[:, :, ds(b * DEC_SEQ, DEC_SEQ)])
                fill_q(dve, qz, b, S["q_ok"])

            def keys(b, which):
                for i in which:
                    if i % 2:
                        kt_out(dve, i, b)

            def shift(b, s):
                dve.wait_ge(S["scored"], b * 3 + 4)
                if new_mask is None:
                    s.ok(dve.tensor_copy(snew[:, :], NEWS))
                else:
                    s.ok(dve.tensor_tensor(snew[:, :], NEWS, new_mask, ALU.add))
                s.ok(dve.tensor_reduce(st[:, 0:1], SC, mybir.AxisListType.XY, ALU.max))
                s.wait()
                s.ok(dve.tensor_reduce(st[:, 1:2], snew[:, :], AX, ALU.max))
                s.wait()
                dve.tensor_scalar(st[:, 3:4], st[:, 0:1], st[:, 1:2], -1.0, ALU.max, ALU.mult).then_inc(S["shifted"], 1)

            def scale(b, s):
                dve.wait_ge(S["exped"], b * 2 + 2)
                s.ok(dve.tensor_scalar(st[:, 6:7], st[:, 4:5], st[:, 5:6], None, ALU.add))
                s.wait()
                s.ok(dve.reciprocal(st[:, 7:8], st[:, 6:7]))
                s.wait()
                if coef is not None:
                    s.ok(dve.tensor_scalar(st[:, 2:3], st[:, 7:8], coef, None, ALU.mult))
                    s.wait()
                r = st[:, 7:8] if coef is None else st[:, 2:3]
                dve.tensor_scalar(probs[:, :], probs[:, :], r, None, ALU.mult).then_inc(S["scaled"], 1)

            def probs_out(b, s):
                dve.wait_ge(S["pt_turned"], b * 2 + 2)
                s.ok(dve.tensor_copy(ptn[:, :], NEWT))
                assert s.n == STEPS
                dve.tensor_copy(pt[:, 4:8, :], K.ps[:, 6, :].rearrange("p (j n) -> p j n", j=4))\
                   .then_inc(S["pt_dve"], 1)
                s.wait()

            def o_out(b):
                dve.wait_ge(S["weighed"], b + 2)
                dve.tensor_copy(o_sb[:, 0:vw], O).then_inc(S["o_copied"], 1)

            def finish(b):
                dve.wait_ge(S["o_turned"], b + 1)
                out(dve, OT, b)
            queries(0)
            keys(0, range(len(units)))
            with dve.Fori(0, LAST) as b:
                s = Steps(dve, S["chain"], b * STEPS + 1)
                shift(b, s)
                keys(b + 1, stretch[0][:4])
                scale(b, s)
                keys(b + 1, stretch[0][4:])
                probs_out(b, s)
                queries(b + 1)
                keys(b + 1, stretch[1])
                o_out(b)
                keys(b + 1, stretch[2])
                finish(b)
                keys(b + 1, stretch[3])
            s = Steps(dve, S["chain"], LAST * STEPS + 1)
            shift(LAST, s)
            scale(LAST, s)
            probs_out(LAST, s)
            o_out(LAST)
            finish(LAST)


def sample_subln(nc, K):
    S = {n: K.sem("subln_" + n) for n in ("squared", "summed", "mean_ok", "rstd_ok", "chain")}
    with ExitStack() as mem:
        square = mem.enter_context(nc.sbuf_tensor("subln_square", [P, DIFF, SAMP], F32))
        ms = mem.enter_context(nc.sbuf_tensor("subln_ms", [P, DIFF, SAMP], F32))
        root, inv, fix = (mem.enter_context(nc.sbuf_tensor(f"subln_{x}", [P, DIFF, SAMP], F32))
                          for x in ("root", "inv", "fix"))
        block = mem.enter_context(nc.Block())
        view = K.feat_s[:, 4:8, :]

        @block.scalar
        def _(act):
            act.activation(square[:, :, :], view, ACT.Square).then_inc(S["squared"], 1)
            act.wait_ge(S["mean_ok"], 1)
            act.activation(root[:, :, :], ms[:, :, :], ACT.Sqrt).then_inc(S["rstd_ok"], 1)

        @block.tensor
        def _(pe):
            pe.wait_ge(S["squared"], 1)
            pe.matmul(K.ps[:, 0, 0:DIFF * SAMP], K.c("ones"), square[:, :, :].rearrange("p h n -> p (h n)"),
                      start=True, stop=True).then_inc(S["summed"], 1)

        @block.vector
        def _(dve):
            s = Steps(dve, S["chain"])
            dve.wait_ge(S["summed"], 1)
            dve.tensor_scalar(ms[:, :, :], K.ps[:, 0, 0:DIFF * SAMP].rearrange("p (h n) -> p h n", h=DIFF),
                              1.0 / P, EPS, ALU.mult, ALU.add).then_inc(S["mean_ok"], 1)
            dve.wait_ge(S["rstd_ok"], 1)
            s.ok(dve.reciprocal(inv[:, :, :], root[:, :, :]))
            s.wait()
            s.ok(dve.tensor_tensor(fix[:, :, :], inv[:, :, :], inv[:, :, :], ALU.mult))
            s.wait()
            dve.wait_ge(S["mean_ok"], 1)
            s.ok(dve.tensor_tensor(fix[:, :, :], fix[:, :, :], ms[:, :, :], ALU.mult))
            s.wait()
            s.ok(dve.tensor_scalar(fix[:, :, :], fix[:, :, :], -0.5, 1.5, ALU.mult, ALU.add))
            s.wait()
            s.ok(dve.tensor_tensor(fix[:, :, :], fix[:, :, :], inv[:, :, :], ALU.mult))
            s.wait()
            s.ok(dve.scalar_tensor_tensor(out=view, in0=view, scalar=K.subln_col8[:, 0:1], in1=fix[:, :, :],
                                          op0=ALU.mult, op1=ALU.mult))
            s.wait()


def split_sample(nc, K, tag):
    hi_ok, lo_ok = K.sem(tag + "_hi_ok"), K.sem(tag + "_lo_ok")
    with nc.Block() as block:
        @block.vector
        def _(dve):
            dve.tensor_copy(K.feat_hi[:, :, SEQ:TOK], K.feat_s[:, :, :]).then_inc(hi_ok, 1)
            dve.wait_ge(hi_ok, 1)
            dve.tensor_tensor(K.feat_lo[:, :, SEQ:TOK], K.feat_s[:, :, :], K.feat_hi[:, :, SEQ:TOK].bitcast(F32),
                              ALU.subtract).then_inc(lo_ok, 1)
            dve.wait_ge(lo_ok, 1)


def add_product(nc, K, tag, lhs_at, tiles):
    W = K.weights
    multiplied, added, passed = (K.sem(f"{tag}_{x}") for x in ("multiplied", "added", "passed"))
    n_passed = 0
    for half in range(2):
        for tile, _ in tiles[half][:-1]:
            n_passed += 1
            W.used[tile] = (passed, n_passed)
        W.used[tiles[half][-1][0]] = (multiplied, NT * (half + 1))
    with nc.Block() as block:
        @block.sync
        def _(sp):
            W.load_up_to(sp, tiles[-1][-1][0] + 4)

        @block.tensor
        def _(pe):
            for half in range(2):
                first, last = tiles[half][0][1][0], tiles[half][-1][1][-1]
                for tile, chunks in tiles[half]:
                    W.ready(pe, tile)
                    hi, lo = (x[:, 0:len(chunks) * BANK].rearrange("p (k n) -> p k n", n=BANK)
                              for x in W.parts_of(tile))
                    for t in range(NT):
                        n, item = rows_of(t), half * NT + t
                        if item >= 8 and chunks[0] == first:
                            pe.wait_ge(added, item - 7)
                        for i, c in enumerate(chunks):
                            ins = three_passes(pe, K.ps[0:n, item % 8, :], lhs_at(c, t), (hi[:, i, :], lo[:, i, :]),
                                               c == first, c == last)
                        if chunks[-1] == last:
                            ins.then_inc(multiplied, 1)
                    if chunks[-1] != last:
                        ins.then_inc(passed, 1)

        @block.scalar
        def _(act):
            for half in range(2):
                for tile, _ in tiles[half]:
                    W.split_after(act, tile, W.hi)

        @block.vector
        def _(dve):
            for half in range(2):
                for tile, _ in tiles[half][:-1]:
                    W.split_after(dve, tile, W.lo)
                for t in range(NT):
                    item, n = half * NT + t, rows_of(t)
                    dst = K.resid[0:n, t, half * BANK:(half + 1) * BANK]
                    dve.wait_ge(multiplied, item + 1)
                    if t == NT - 1:
                        W.split_after(dve, tiles[half][-1][0], W.lo)
                    dve.tensor_tensor(dst, dst, K.ps[0:n, item % 8, :], ALU.add).then_inc(added, 1)
            dve.wait_ge(added, 2 * NT)


def gate_up(nc, K, tag, act_hi, act_lo, first, n_chunks):
    S = {n: K.sem(f"{tag}_{n}") for n in ("multiplied", "silu_ok", "up_ok", "hi_ok", "chunk_ok")}
    W = K.weights
    H = TOK // 2
    LOOPS = (n_chunks - 3) // 2
    assert n_chunks == 2 * LOOPS + 3
    for n in range(n_chunks):
        W.used[first + n] = (S["multiplied"], n + 1)
    with ExitStack() as mem:
        silu = mem.enter_context(nc.sbuf_tensor(f"{tag}_silu", [P, 2, 2, H], F32))
        prod = mem.enter_context(nc.sbuf_tensor(f"{tag}_prod", [P, 2, 2, H], F32))
        block = mem.enter_context(nc.Block())

        def every_chunk(eng, step):
            with eng.Fori(0, LOOPS) as i:
                for x in range(2):
                    step(i * 2 + x, x, i)
            for n in range(2 * LOOPS, n_chunks):
                step(n, n % 2, None)

        def at(buf, n):
            start = ds(n * TOK, TOK) if not isinstance(n, int) else slice(n * TOK, (n + 1) * TOK)
            return buf[:, start].rearrange("p (f n) -> p f n", f=2)

        @block.sync
        def _(sp):
            W.load_up_to(sp, first + n_chunks + 3)

        @block.tensor
        def _(pe):
            def step(n, x, i):
                tile = first + x
                W.ready(pe, first, n)
                hi, lo = (v.rearrange("p (a k n) -> p a k n", a=2, k=KC) for v in W.parts_of(tile))
                pe.wait_ge(S["up_ok"], n + 1)
                for g in range(2):
                    for hf in range(2):
                        for k in range(KC):
                            cols = slice(hf * H, (hf + 1) * H)
                            ins = three_passes(pe, K.ps[:, 4 * x + 2 * g + hf, 0:H],
                                               (hi[:, g, k, :], lo[:, g, k, :]),
                                               (K.feat_hi[:, k, cols], K.feat_lo[:, k, cols]), k == 0, k == KC - 1)
                ins.then_inc(S["multiplied"], 1)
            every_chunk(pe, step)

        @block.scalar
        def _(act):
            def step(n, x, i):
                act.wait_ge(S["multiplied"], n + 1)
                act.wait_ge(S["up_ok"], n + 1)
                act.activation(silu[:, x, :, :], K.ps[:, 4 * x:4 * x + 2, 0:H], ACT.Silu).then_inc(S["silu_ok"], 1)
                if i is None:
                    W.hi(act, first + n + 2)
                else:
                    W.hi(act, first + x + 2, i * 32)
                act.wait_ge(S["up_ok"], n + 3)
                act.activation(at(act_hi, n), prod[:, x, :, :], ACT.Copy).then_inc(S["hi_ok"], 1)
            every_chunk(act, step)

        @block.vector
        def _(dve):
            dve.sem_inc(S["up_ok"], 2)

            def step(n, x, i):
                dve.wait_ge(S["silu_ok"], n + 1)
                dve.wait_ge(S["chunk_ok"], n + 1)
                dve.tensor_tensor(prod[:, x, :, :], silu[:, x, :, :], K.ps[:, 4 * x + 2:4 * x + 4, 0:H], ALU.mult)\
                   .then_inc(S["up_ok"], 1)
                if i is None:
                    W.lo(dve, first + n + 2)
                else:
                    W.lo(dve, first + x + 2, i * 2)
                dve.wait_ge(S["hi_ok"], n + 1)
                dve.wait_ge(S["up_ok"], n + 3)
                dve.tensor_tensor(at(act_lo, n), prod[:, x, :, :], at(act_hi, n).bitcast(F32), ALU.subtract)\
                   .then_inc(S["chunk_ok"], 1)
            dve.sem_inc(S["chunk_ok"], 2)
            every_chunk(dve, step)


def select_keys(nc, K):
    names = ("kidx_turned", "kt_ok", "p_scored", "p_relu", "p_ok", "s_scored", "s_relu", "s_mixed", "s_out",
             "row_stored", "rows_in", "masked", "chain", "weights_in", "weights_out", "q_ok", "mask_stored")
    S = {n: K.sem("select_" + n) for n in names}
    kidx_in = [K.sem(f"select_kidx_in_{i}") for i in range(2)]
    row_stored = [K.sem(f"select_row_stored_{i}") for i in range(2)]
    with ExitStack() as mem:
        sb = lambda name, shape: mem.enter_context(nc.sbuf_tensor("select_" + name, shape, F32))
        relu = sb("relu", [P, 2, SEQ])
        pages = sb("pages", [P, 2, N_PAGES, HEAD_DIM])
        kt = sb("kt", [P, 2, 4, P])
        qs = sb("qs", [P, DEC_BATCH, IDXH, DEC_SEQ])
        wt = sb("wt", [IDXH * DEC_SEQ, DEC_BATCH])
        mix = sb("mix", [IDXH * DEC_SEQ, DEC_BATCH, DEC_SEQ])
        srelu = sb("srelu", [IDXH * DEC_SEQ, KEYS])
        srow = sb("srow", [DEC_SEQ, 2, KEYS])
        sample = sb("sample", [SAMP, KEYS])
        prompt = sb("prompt", [P, 3, SEQ])
        best = sb("best", [P, 4, 8])
        block = mem.enter_context(nc.Block())
        NEWS, NEWO = K.ps[0:32, 3, 0:DEC_SEQ], K.ps[0:DEC_SEQ, 3, 64:64 + DEC_SEQ]
        p_units = [(qt, h) for qt in range(1, PT) for h in range(IDXH)]
        B = range(DEC_BATCH)

        @block.sync
        def _(sp):
            for b in B:
                if b >= 2:
                    sp.wait_ge(S["kidx_turned"], b - 1)
                for j in range(N_PAGES):
                    n = b * N_PAGES + j
                    pid = sp.value_load(K.pages[0:1, n:n + 1], min_val=0, max_val=K.cache_l1_kidx.shape[0] - 1)
                    sp.dma_start(pages[:, b % 2, j, :], K.cache_l1_kidx[ds(pid, 1), :, :]
                                 .rearrange("a k d -> (a k) d")).then_inc(kidx_in[b % 2], 16)
                if b >= 2:
                    sp.wait_ge(S["s_out"], b - 1)
                    sp.dma_start(K.idx_rows[b - 2], srow[:, b % 2, :]).then_inc(row_stored[b % 2], 16)
            for b in B[-2:]:
                sp.wait_ge(S["s_out"], b + 1)
                sp.dma_start(K.idx_rows[b], srow[:, b % 2, :]).then_inc(row_stored[b % 2], 16)
            for x in row_stored:
                sp.wait_ge(x, 16 * DEC_BATCH // 2)
            sp.dma_start(sample[:, :], K.idx_rows.rearrange("b q k -> (b q) k")).then_inc(S["rows_in"], 16)
            sp.wait_ge(S["masked"], 1)
            sp.dma_start(K.mask_rows.rearrange("b q k -> (b q) k"), sample[:, :]).then_inc(S["mask_stored"], 16)
            sp.wait_ge(S["mask_stored"], 16)

        @block.tensor
        def _(pe):
            for u, (qt, h) in enumerate(p_units):
                if u >= 2:
                    pe.wait_ge(S["p_relu"], u - 1)
                lo = (h % 2) * HEAD_DIM
                w = (qt + 1) * P
                pe.matmul(K.ps[:, 6 + u % 2, 0:w], K.qi[lo:lo + HEAD_DIM, h // 2, qt * P:w], K.ki[lo:lo + HEAD_DIM, 0:w],
                          start=True, stop=True).then_inc(S["p_scored"], 1)
            for b in B:
                pe.wait_ge(kidx_in[b % 2], 16 * N_PAGES * (b // 2 + 1))
                if b >= 1:
                    pe.wait_ge(S["kt_ok"], b)
                for j in range(0, N_PAGES, 2):
                    ins = pe.transpose(K.ps[:, 0, j // 2 * P:(j // 2 + 1) * P],
                                       pages[:, b % 2, j:j + 2, :].rearrange("p a d -> p (a d)"), K.c("ident"))
                ins.then_inc(S["kidx_turned"], 1)
                pe.wait_ge(S["kt_ok"], b + 1)
                pe.wait_ge(S["q_ok"], 1)
                if b >= 1:
                    pe.wait_ge(S["s_relu"], 2 * b)
                for j in range(N_PAGES):
                    lo = (j % 2) * HEAD_DIM
                    pe.matmul(K.ps[0:32, 1 + j % 2, j // 2 * P:(j // 2 + 1) * P],
                              qs[lo:lo + HEAD_DIM, b, :, :].rearrange("p h q -> p (h q)"),
                              kt[lo:lo + HEAD_DIM, b % 2, j // 2, :], start=True, stop=True)
                if b >= 1:
                    pe.wait_ge(S["s_out"], b)
                pe.matmul(NEWS, qs[0:HEAD_DIM, b, :, :].rearrange("p h q -> p (h q)"),
                          K.ki[0:HEAD_DIM, SEQ + b * DEC_SEQ:SEQ + (b + 1) * DEC_SEQ], start=True, stop=True)\
                  .then_inc(S["s_scored"], 1)
                pe.wait_ge(S["s_relu"], 2 * b + 2)
                for dst, lo, hi in ((K.ps[0:DEC_SEQ, 4, :], 0, BANK), (K.ps[0:DEC_SEQ, 5, :], BANK, PAST_LEN),
                                    (NEWO, PAST_LEN, KEYS)):
                    ins = pe.matmul(dst, mix[:, b, :], srelu[:, lo:hi], start=True, stop=True)
                ins.then_inc(S["s_mixed"], 1)

        @block.scalar
        def _(act):
            act.dma_start(K.idx_weights, K.wi[0:SAMP, PT, :]).then_inc(S["weights_out"], 16)
            act.wait_ge(S["weights_out"], 16)
            with nc.allow_non_contiguous_dma(reason="256 words"):
                for h in range(IDXH):
                    act.dma_start(wt[h * DEC_SEQ:(h + 1) * DEC_SEQ, :],
                                   K.idx_weights[:, h:h + 1].rearrange("(b q) a -> q (b a)", b=DEC_BATCH))\
                        .then_inc(S["weights_in"], 16)
            for u, (qt, h) in enumerate(p_units):
                w = (qt + 1) * P
                act.wait_ge(S["p_scored"], u + 1)
                if u >= 2:
                    act.wait_ge(S["p_ok"], u - 1)
                act.activation(relu[:, u % 2, 0:w], K.ps[:, 6 + u % 2, 0:w], ACT.Relu).then_inc(S["p_relu"], 1)
            for b in B:
                act.wait_ge(S["kidx_turned"], b + 1)
                if b >= 2:
                    act.wait_ge(S["s_scored"], b - 1)
                act.activation(kt[:, b % 2, :, :], K.ps[:, 0, :].rearrange("p (j n) -> p j n", j=4), ACT.Copy)\
                   .then_inc(S["kt_ok"], 1)
                act.wait_ge(S["s_scored"], b + 1)
                if b >= 1:
                    act.wait_ge(S["s_mixed"], b)
                act.activation(srelu[:, 0:PAST_LEN].rearrange("p (j a k) -> p a j k", a=2, k=P),
                               K.ps[0:32, 1:3, :].rearrange("p a (j k) -> p a j k", k=P), ACT.Relu)\
                   .then_inc(S["s_relu"], 1)
                act.activation(srelu[:, PAST_LEN:KEYS], NEWS, ACT.Relu).then_inc(S["s_relu"], 1)

        @block.vector
        def _(dve):
            s = Steps(dve, S["chain"])
            for half in range(2):
                for par in range(2):
                    src = K.qi[par * HEAD_DIM:(par + 1) * HEAD_DIM, :, SEQ:TOK].rearrange(
                        "p c (b q) -> p b c q", b=DEC_BATCH)
                    dst = qs[half * HEAD_DIM:(half + 1) * HEAD_DIM, :, par:IDXH:2, :]
                    s.ok(dve.tensor_copy(dst, src))
            dve.wait_ge(S["weights_in"], 16 * IDXH)
            s.ok(dve.tensor_tensor(mix[:, :, :], bc(K.c("idx_sel")[0:32, :], 1, DEC_BATCH),
                                   bc(wt[:, :], 2, DEC_SEQ), ALU.mult))
            s.wait()
            dve.sem_inc(S["q_ok"], 1)
            for u, (qt, h) in enumerate(p_units):
                w = (qt + 1) * P
                dst, src, wh = prompt[:, qt - 1, 0:w], relu[:, u % 2, 0:w], K.wi[:, qt, h:h + 1]
                dve.wait_ge(S["p_relu"], u + 1)
                if h == 0:
                    dve.tensor_scalar(dst, src, wh, None, ALU.mult).then_inc(S["p_ok"], 1)
                else:
                    dve.wait_ge(S["p_ok"], u)
                    dve.scalar_tensor_tensor(out=dst, in0=src, scalar=wh, in1=dst, op0=ALU.mult, op1=ALU.add)\
                       .then_inc(S["p_ok"], 1)
                if h == IDXH - 1:
                    dve.wait_ge(S["p_ok"], u + 1)
                    s.ok(dve.tensor_tensor(dst[:, qt * P:w], dst[:, qt * P:w], K.c("causal"), ALU.add))
            for b in B:
                dve.wait_ge(S["s_mixed"], b + 1)
                if b >= 2:
                    dve.wait_ge(row_stored[b % 2], 16 * (b // 2))
                s.ok(dve.tensor_copy(srow[:, b % 2, 0:PAST_LEN].rearrange("p (g k) -> p g k", g=2),
                                     K.ps[0:DEC_SEQ, 4:6, :]))
                s.ok(dve.tensor_tensor(srow[:, b % 2, PAST_LEN:KEYS], NEWO, K.c("new_mask")[0:DEC_SEQ, :], ALU.add))
                s.wait()
                dve.sem_inc(S["s_out"], 1)

            def rounds(views, bests, k):
                for _ in range(k // 8):
                    for v, b8 in zip(views, bests):
                        s.ok(dve.max(b8, v))
                    s.wait()
                    for v, b8 in zip(views, bests):
                        s.ok(dve.match_replace(v, b8, v, TAKEN))
                    s.wait()

            def to_mask(dst, view):
                return dve.tensor_scalar(dst, view, TAKEN * 0.5, NEG, ALU.is_gt, ALU.mult)

            views = [prompt[:, qt - 1, 0:(qt + 1) * P] for qt in range(1, PT)]
            rounds(views, [best[:, i, :] for i in range(3)], K_PROMPT)
            s.ok(dve.tensor_copy(K.mask[:, 0, 0:P], K.c("causal")))
            for i, v in enumerate(views):
                s.ok(to_mask(K.mask[:, i + 1, 0:(i + 2) * P], v))
            dve.wait_ge(S["rows_in"], 16)
            rounds([sample[:, :]], [best[0:SAMP, 3, :]], K_SAMPLE)
            to_mask(sample[:, :], sample[:, :]).then_inc(S["masked"], 1)
            s.wait()


def store_results(nc, K):
    done = K.sem("results_stored")
    with nc.Block() as block:
        @block.sync
        def _(sp):
            sp.dma_start(K.y_prompt[0].rearrange("(t p) d -> p t d", p=P), K.resid[:, 0:PT, :]).then_inc(done, 16)
            sp.dma_start(K.y_sample.rearrange("b t d -> (b t) d"), K.resid[0:SAMP, PT, :]).then_inc(done, 16)
            sp.wait_ge(done, 32)


def two_layers(nc, K):
    W = K.weights = Weights(K, lambda name: nc.alloc_semaphore(name=name))
    cuts0 = dict(qa=0, ka=512, va=1024, fa=1536, qb=1544, kb=2056, vb=2568)

    def by_halves(w, c0, width):
        return [(W.add(column_tile(w, k, 4, c0, width)), range(k, k + 4)) for k in (0, 4)]

    l0 = {n: by_halves(K.w_in0, c, 512) if n != "fa" else [(W.add(column_tile(K.w_in0, 0, KC, c, FOX)), range(KC))]
          for n, c in cuts0.items()}

    FH = FC // 2

    def products(w_out, wg, wu, wd):
        out = [by_halves(w_out, h * BANK, BANK) for h in range(2)]
        halves = []
        for f in range(2):
            gu = [W.add(gate_up_tile(wg, wu, (f * FH + i) * P)) for i in range(FH)]
            down = [[(W.add(column_tile(wd, f * FH + k, min(4, FH - k), h * BANK, BANK)), range(k, min(k + 4, FH)))
                     for k in range(0, FH, 4)] for h in range(2)]
            halves.append((gu[0], down))
        return out, halves

    out0, ffn0 = products(K.w_out0, K.w_gate0, K.w_up0, K.w_down0)
    l1 = {n: by_halves(K.w_in1, c, w) for n, c, w in
          (("idx", 1536, 324), ("kv", 1024, 512), ("q0", 0, 512), ("q1", 512, 512))}
    out1, ffn1 = products(K.w_out1, K.w_gate1, K.w_up1, K.w_down1)

    load_inputs(nc, K)

    def tok_rows(prompt, sample, c0, c1):
        def at(t):
            return prompt[t * P:(t + 1) * P, c0:c1] if t < PT else sample[:, c0:c1]
        return at

    def plain(j):
        return lambda r: r[:, j * P:(j + 1) * P]

    def to(prompt, sample, c):
        return lambda t: prompt[:, c, t * P:(t + 1) * P] if t < PT else sample[:, c, :]

    def ffn(tag, gain, halves):
        norm_to_features(nc, K, gain, tag + "n")
        with ExitStack() as mem:
            act_hi, act_lo = (mem.enter_context(nc.sbuf_tensor(f"{tag}_act_{x}", [P, FH * TOK], F32R)) for x in ("hi", "lo"))

            def lhs(c, t):
                cols = slice(c * TOK + t * P, c * TOK + t * P + rows_of(t))
                return act_hi[:, cols], act_lo[:, cols]
            for f, (gu, down) in enumerate(halves):
                gate_up(nc, K, f"{tag}g{f}", act_hi, act_lo, gu, FH)
                add_product(nc, K, f"{tag}d{f}", lhs, down)

    def feat_lhs(c, t):
        cols = slice(t * P, t * P + rows_of(t))
        return K.feat_hi[:, c, cols], K.feat_lo[:, c, cols]

    norm_to_features(nc, K, 0, "n0")
    with ExitStack() as layer:
        sb = lambda mem, name, shape: mem.enter_context(nc.sbuf_tensor(name, shape, F32))
        qs, ks = sb(layer, "qs0", [P, KC, SAMP]), sb(layer, "ks0", [P, KC, SAMP])
        K.logf = sb(layer, "logf", [P, NT, FOX])
        with ExitStack() as pr:
            qp, kp = sb(pr, "qp0", [P, KC, SEQ]), sb(pr, "kp0", [P, KC, SEQ])
            vp = sb(pr, "vp0", [P, PT, D_MODEL])
            vs = sb(pr, "vs0", [SAMP, D_MODEL])

            def q_part(name, norm, rope, c):
                return Part(l0[name], 512, 512, norm, rope,
                            turns=[(plain(j), to(qp, qs, c + j), SCALE) for j in range(4)])

            def k_part(name, norm, rope, c):
                return Part(l0[name], 512, 512, norm, rope,
                            stores=[(slice(0, 512), tok_rows(K.p_l0_k, K.s_l0_k, c * P, c * P + 512))],
                            turns=[(plain(j), to(kp, ks, c + j), 1.0) for j in range(4)])

            def v_part(name, c0):
                rows = tok_rows(K.p_l0_v, K.s_l0_v, c0, c0 + 512)
                return Part(l0[name], 512, copies=[(
                    slice(0, 512), lambda t: vp[:, t, c0:c0 + 512] if t < PT else vs[:, c0:c0 + 512],
                    rows, rows, None)])

            f_rows = tok_rows(K.p_l0_logf, K.s_l0_logf, 0, FOX)

            def log_sigmoid_in(dve, dst, src, s):
                return dve.tensor_tensor(dst, src, K.bias_f[0:src.shape[0], :], ALU.add)

            parts = [q_part("qa", 0, False, 0), k_part("ka", 1, False, 0), v_part("va", 0),
                     Part(l0["fa"], FOX, copies=[(slice(0, FOX), lambda t: K.logf[0:rows_of(t), t, :], None, None,
                                                  log_sigmoid_in)]),
                     q_part("qb", 2, True, 4), k_part("kb", 3, True, 4), v_part("vb", 512)]
            project(nc, K, parts, "p0")
            log_sigmoid(nc, K, f_rows)
            forget_sums(nc, K)

            def lo(h):
                return slice((h % 2) * HEAD_DIM, (h % 2 + 1) * HEAD_DIM)

            def v_cols(h):
                return slice(h * HEAD_DIM, (h + 1) * HEAD_DIM) if h < FOX else \
                    slice(512 + (h - FOX) // 2 * P, 512 + ((h - FOX) // 2 + 1) * P)
            prompt_attention(
                nc, K, "a0", q_at=lambda h, qt: qp[lo(h), h // 2, qt * P:(qt + 1) * P], k_at=lambda h: kp[lo(h), h // 2, :],
                v_at=lambda h, j: vp[:, j, v_cols(h)],
                bias_at=lambda h, qt: K.minus_c[:, h, 0:(qt + 1) * P] if h < FOX else None, diag=True,
                out_at=lambda h, qt: K.att[:, qt, v_cols(h)], second=lambda h: h >= FOX and h % 2 == 1)

        def fill_q0(dve, qz, b, ok):
            flat = qz[:, :, :].rearrange("p c n -> p (c n)")
            for half in range(2):
                rows = slice(half * HEAD_DIM, (half + 1) * HEAD_DIM)
                for c in range(KC):
                    col = c * P + 16 * c + 8 * half
                    ins = dve.tensor_copy(flat[rows, col:col + DEC_SEQ], qs[rows, c, ds(b * DEC_SEQ, DEC_SEQ)])
            ins.then_inc(ok, 1)

        def out0_fn(dve, OT, b):
            now = ds(b * DEC_SEQ, DEC_SEQ)
            for x in range(2):
                o = OT[:, x, :].rearrange("p (i x a q) -> p i x a q", i=4, x=2, a=2)[:, :, x]
                for half in range(2):
                    rows = slice(half * HEAD_DIM, (half + 1) * HEAD_DIM)
                    dve.tensor_copy(K.feat_s[rows, x:4:2, now], o[rows, 0:2, half, :])
                dve.tensor_reduce(K.feat_s[:, 4 + x:8:2, now], o[:, 2:4].rearrange("p i a q -> p i q a"), AX, ALU.add)

        sample_attention(
            nc, K, "s0", K.cache_l0_k, K.cache_l0_v, lambda b: K.s_l0_v[ds(b * DEC_SEQ, DEC_SEQ), :],
            lambda b: K.fox_rows[ds(b, 1), :, :].rearrange("a h k -> (a h) k"), K.c("fox_sel")[0:FOX, :], D_MODEL, KC, fill_q0,
            ks, K.c("new_mask"), K.coef[:, 0:1], out0_fn)
        sample_subln(nc, K)
    turn_attention(nc, K, K.att, "t0", True)
    split_sample(nc, K, "x0")
    add_product(nc, K, "o0", feat_lhs, out0)
    ffn("f0", 1, ffn0)

    renew_semaphores(nc, K)

    norm_to_features(nc, K, 2, "n1")
    with ExitStack() as layer:
        sb = lambda mem, name, shape: mem.enter_context(nc.sbuf_tensor(name, shape, F32))
        qs, ks = sb(layer, "qs1", [P, KC, SAMP]), sb(layer, "ks1", [P, 2, SAMP])
        vs = sb(layer, "vs1", [SAMP, 256])
        with ExitStack() as pr:
            qp, kp = sb(pr, "qp1", [P, KC, SEQ]), sb(pr, "kp1", [P, 2, SEQ])
            vp = sb(pr, "vp1", [P, PT, 256])
            K.qi = sb(pr, "qi", [P, 2, TOK])
            K.ki = sb(pr, "ki", [P, TOK])
            K.wi = sb(pr, "wi", [P, NT, IDXH])
            span = lambda t: slice(t * P, t * P + rows_of(t))
            idx_rows = tok_rows(K.p_l1_kidx, K.s_l1_kidx, 0, HEAD_DIM)
            parts = [Part(l1["idx"], 324, 320, None, True,
                          stores=[(slice(256, 320), idx_rows)],
                          turns=[(plain(0), lambda t: K.qi[:, 0, span(t)], 1.0),
                                 (plain(1), lambda t: K.qi[:, 1, span(t)], 1.0),
                                 (plain(2), lambda t: K.ki[:, span(t)], 1.0)],
                          copies=[(slice(320, 324), lambda t: K.wi[0:rows_of(t), t, :], None, None,
                                   lambda dve, dst, src, s: dve.tensor_scalar(dst, src, SCALE * IDXH ** -0.5, None,
                                                                              ALU.mult))]),
                     Part(l1["kv"], 512, 256, 5, True,
                          stores=[(slice(0, 256), tok_rows(K.p_l1_k, K.s_l1_k, 0, 256))],
                          turns=[(plain(j), to(kp, ks, j), 1.0) for j in range(2)],
                          copies=[(slice(256, 512), lambda t: vp[:, t, :] if t < PT else vs[:, :],
                                   tok_rows(K.p_l1_v, K.s_l1_v, 0, 256), tok_rows(K.p_l1_v, K.s_l1_v, 0, 256), None)])]

            for g in range(2):
                parts.append(Part(l1[f"q{g}"], 512, 512, 4, True, paired=True,
                                  turns=[(plain(r), to(qp, qs, 4 * g + r), SCALE) for r in range(4)]))
            project(nc, K, parts, "p1")
            select_keys(nc, K)

            def kv_half(h):
                a = h // 4 % 2
                return slice(a * HEAD_DIM, (a + 1) * HEAD_DIM)
            prompt_attention(
                nc, K, "a1", q_at=lambda h, qt: qp[kv_half(h), 4 * (h // 8) + h % 4, qt * P:(qt + 1) * P],
                k_at=lambda h: kp[kv_half(h), h // 8, :],
                v_at=lambda h, j: vp[:, j, h // 4 * HEAD_DIM:(h // 4 + 1) * HEAD_DIM],
                bias_at=lambda h, qt: K.mask[:, qt, 0:(qt + 1) * P], diag=False,
                out_at=lambda h, qt: K.att[:, qt, h * HEAD_DIM:(h + 1) * HEAD_DIM], second=lambda h: False)

        def fill_q1(dve, qz, b, ok):
            for half in range(2):
                rows = slice(half * HEAD_DIM, (half + 1) * HEAD_DIM)
                for g in range(2):
                    col = (8 * g + 4 * half) * DEC_SEQ
                    dst = qz[rows, g, col:col + 4 * DEC_SEQ].rearrange("p (r q) -> p r q", r=4)
                    ins = dve.tensor_copy(dst, qs[rows, 4 * g:4 * g + 4, ds(b * DEC_SEQ, DEC_SEQ)])
            ins.then_inc(ok, 1)

        def out1_fn(dve, OT, b):
            o = OT[0:HEAD_DIM, 0, :].rearrange("p (c a q) -> p c a q", c=KC, a=2)
            for half in range(2):
                dve.tensor_copy(K.feat_s[half * HEAD_DIM:(half + 1) * HEAD_DIM, :, ds(b * DEC_SEQ, DEC_SEQ)],
                                o[:, :, half, :])

        sample_attention(
            nc, K, "s1", K.cache_l1_k.rearrange("n k g d -> n k (g d)"), K.cache_l1_v.rearrange("n k g d -> n k (g d)"),
            lambda b: K.s_l1_v[ds(b * DEC_SEQ, DEC_SEQ), :],
            lambda b: K.mask_rows[ds(b, 1), :, :].rearrange("a q k -> (a q) k"), K.c("query_sel")[0:DEC_SEQ, :], 256, 2, fill_q1,
            ks, None, None, out1_fn)
    turn_attention(nc, K, K.att, "t1", False)
    split_sample(nc, K, "x1")
    add_product(nc, K, "o1", feat_lhs, out1)
    ffn("f1", 3, ffn1)
    store_results(nc, K)


def renew_semaphores(nc, K):
    numbers = sorted(h.num for h in K.phase_sems)
    runs = []
    for n in numbers:
        if runs and runs[-1][1] == n:
            runs[-1][1] = n + 1
        else:
            runs.append([n, n + 1])
    with nc.Block() as block:
        @block.gpsimd
        def _(pool):
            for lo, hi in runs:
                pool.sem_clear(range(lo, hi))
    for h in K.phase_sems:
        nc.release_semaphore(h)
    K.phase_sems = []


def log_sigmoid(nc, K, rows):
    S = {n: K.sem("logsig_" + n) for n in ("act", "dve", "stored")}
    with ExitStack() as mem:
        low = mem.enter_context(nc.sbuf_tensor("logsig_low", [P, NT, FOX], F32))
        e = mem.enter_context(nc.sbuf_tensor("logsig_e", [P, NT, FOX], F32))
        block = mem.enter_context(nc.Block())
        parts = [lambda x: x[:, 0:PT, :], lambda x: x[0:SAMP, PT, :]]

        @block.scalar
        def _(act):
            for i, (f, src) in enumerate(((ACT.Abs, K.logf), (ACT.Exp, e), (ACT.Ln, e))):
                if i:
                    act.wait_ge(S["act"], 2 * i)
                if i == 2:
                    act.wait_ge(S["dve"], 4)
                for p in parts:
                    act.activation(p(e), p(src), f, scale=-1.0 if f == ACT.Exp else 1.0).then_inc(S["act"], 1)

        @block.vector
        def _(dve):
            for p in parts:
                dve.tensor_scalar(p(low), p(K.logf), 0.0, None, ALU.min).then_inc(S["dve"], 1)
            dve.wait_ge(S["act"], 4)
            for p in parts:
                dve.tensor_scalar(p(e), p(e), 1.0, None, ALU.add).then_inc(S["dve"], 1)
            dve.wait_ge(S["dve"], 2)
            dve.wait_ge(S["act"], 6)
            for p in parts:
                dve.tensor_tensor(p(K.logf), p(low), p(e), ALU.subtract).then_inc(S["dve"], 1)

        @block.sync
        def _(sp):
            sp.wait_ge(S["dve"], 6)
            for t in range(NT):
                sp.dma_start(rows(t), K.logf[0:rows_of(t), t, :]).then_inc(S["stored"], 16)
            sp.wait_ge(S["stored"], 16 * NT)


def build(nc, ins, outs, const_in):
    with ExitStack() as ctx:
        sb = lambda name, shape, dt=F32: ctx.enter_context(nc.sbuf_tensor(name, shape, dt))
        K = Kernel()
        K.x_prompt, K.x_sample, K.cache_l0_k = ins["x_prompt"], ins["x_sample"], ins["cache_l0_k"]
        K.cache_l0_v, K.cache_l0_logf, K.cache_l1_k = ins["cache_l0_v"], ins["cache_l0_logf"], ins["cache_l1_k"]
        K.cache_l1_v, K.cache_l1_kidx, K.page_table = ins["cache_l1_v"], ins["cache_l1_kidx"], ins["page_table"]
        K.b_f0, K.subln0, K.w_in0 = ins["b_f0"], ins["subln0"], ins["w_in0"]
        K.w_out0, K.w_gate0, K.w_up0 = ins["w_out0"], ins["w_gate0"], ins["w_up0"]
        K.w_down0, K.w_in1, K.w_out1 = ins["w_down0"], ins["w_in1"], ins["w_out1"]
        K.w_gate1, K.w_up1, K.w_down1 = ins["w_gate1"], ins["w_up1"], ins["w_down1"]
        flat = lambda x: x.rearrange("b t d -> (b t) d")
        heads_flat = lambda x: x.rearrange("b t g d -> (b t) (g d)")
        K.y_prompt, K.y_sample = outs["y_prompt"], outs["y_sample"]
        K.p_l0_k, K.p_l0_v, K.p_l0_logf = flat(outs["p_l0_k"]), flat(outs["p_l0_v"]), flat(outs["p_l0_logf"])
        K.p_l1_kidx, K.s_l0_k, K.s_l0_v = flat(outs["p_l1_kidx"]), flat(outs["s_l0_k"]), flat(outs["s_l0_v"])
        K.s_l0_logf, K.s_l1_kidx = flat(outs["s_l0_logf"]), flat(outs["s_l1_kidx"])
        K.p_l1_k, K.p_l1_v, K.s_l1_k = heads_flat(outs["p_l1_k"]), heads_flat(outs["p_l1_v"]), heads_flat(outs["s_l1_k"])
        K.s_l1_v = heads_flat(outs["s_l1_v"])
        K.phase_sems = []

        def sem(name):
            handle = nc.alloc_semaphore(name=name)
            K.phase_sems.append(handle)
            return handle
        K.sem = sem
        K.const_in = const_in
        K.head_gains = [ins[n] for n in ("qn_fox0", "kn_fox0", "qn_diff0", "kn_diff0", "qn_dsa1", "kn_dsa1")]
        K.norm_gains = [ins[n] for n in ("attn_norm0", "ffn_norm0", "attn_norm1", "ffn_norm1")]
        K.lam_vecs = [ins[n] for n in ("lam_q1_0", "lam_k1_0", "lam_q2_0", "lam_k2_0")]
        scratch = lambda name, shape: nc.dram_tensor(name, shape, F32, kind="Internal").ap()
        K.prompt_rows = scratch("prompt_rows", (FOX, SEQ))
        K.fox_rows = scratch("fox_rows", (DEC_BATCH, FOX, KEYS))
        K.idx_rows = scratch("idx_rows", (DEC_BATCH, DEC_SEQ, KEYS))
        K.mask_rows = scratch("mask_rows", (DEC_BATCH, DEC_SEQ, KEYS))
        K.idx_weights = scratch("idx_weights", (SAMP, IDXH))
        K.ps = ctx.enter_context(nc.psum_tensor("ps", [P, 8, BANK], F32))
        K.resid = sb("resid", [P, NT, D_MODEL])
        feat_hi_at = nc.sbuf_base
        K.feat_hi = sb("feat_hi", [P, KC, TOK], F32R)
        feat_lo_at = nc.sbuf_base
        K.feat_lo = sb("feat_lo", [P, KC, TOK], F32R)
        K.att = nc.alloc_sbuf_tensor_at("att", [P, PT, D_MODEL], F32, offset=feat_lo_at)
        K.minus_c = nc.alloc_sbuf_tensor_at("minus_c", [P, FOX, SEQ], F32, offset=feat_hi_at)
        K.mask = nc.alloc_sbuf_tensor_at("mask", [P, PT, SEQ], F32, offset=feat_hi_at)
        K.kt0 = nc.alloc_sbuf_tensor_at("kt0", [P, 2 * Weights.SIZE], F32, offset=feat_hi_at)
        K.feat_s = sb("feat_s", [P, KC, SAMP])
        K.w_raw = sb("w_raw", [P, 2, Weights.SIZE])
        K.w_hi, K.w_lo = sb("w_hi", [P, 2, Weights.SIZE], F32R), sb("w_lo", [P, 2, Weights.SIZE], F32R)
        K.const = sb("const", [P, const_in.shape[1]])
        K.c = lambda name: K.const[:, CONST_AT[name][0]:CONST_AT[name][0] + CONST_AT[name][1]]
        K.gain_cols = sb("gain_cols", [P, 4, KC])
        K.head_gain = sb("head_gain", [P, 6, HEAD_DIM])
        K.subln_row, K.subln_col = sb("subln_row", [P, P]), sb("subln_col", [P, 1])
        K.subln_row8, K.subln_col8 = sb("subln_row8", [P, P]), sb("subln_col8", [P, 1])
        K.bias_f = sb("bias_f", [P, FOX])
        K.pages = sb("pages", [1, DEC_BATCH * N_PAGES], I32)
        K.page_rows = sb("page_rows", [DEC_BATCH * N_PAGES, 1], I32)
        K.lams = sb("lams", [P, 4, HEAD_DIM])
        K.lam, K.minus_lam, K.coef = sb("lam", [P, 1]), sb("minus_lam", [P, 1]), sb("coef", [P, 1])
        two_layers(nc, K)


_INS = ['x_prompt', 'x_sample', 'cache_l0_k', 'cache_l0_v', 'cache_l0_logf', 'cache_l1_k', 'cache_l1_v',
        'cache_l1_kidx', 'page_table', 'attn_norm0', 'w_in0', 'b_f0', 'qn_fox0', 'kn_fox0', 'qn_diff0', 'kn_diff0',
        'lam_q1_0', 'lam_k1_0', 'lam_q2_0', 'lam_k2_0', 'subln0', 'w_out0', 'ffn_norm0', 'w_gate0', 'w_up0', 'w_down0',
        'attn_norm1', 'w_in1', 'qn_dsa1', 'kn_dsa1', 'w_out1', 'ffn_norm1', 'w_gate1', 'w_up1', 'w_down1']
_OUTS = {'y_prompt': (1, SEQ, D_MODEL), 'y_sample': (DEC_BATCH, DEC_SEQ, D_MODEL),
         'p_l0_k': (1, SEQ, 1024), 'p_l0_v': (1, SEQ, 1024), 'p_l0_logf': (1, SEQ, FOX),
         'p_l1_k': (1, SEQ, KVH, HEAD_DIM), 'p_l1_v': (1, SEQ, KVH, HEAD_DIM), 'p_l1_kidx': (1, SEQ, HEAD_DIM),
         's_l0_k': (DEC_BATCH, DEC_SEQ, 1024), 's_l0_v': (DEC_BATCH, DEC_SEQ, 1024),
         's_l0_logf': (DEC_BATCH, DEC_SEQ, FOX), 's_l1_k': (DEC_BATCH, DEC_SEQ, KVH, HEAD_DIM),
         's_l1_v': (DEC_BATCH, DEC_SEQ, KVH, HEAD_DIM), 's_l1_kidx': (DEC_BATCH, DEC_SEQ, HEAD_DIM)}


def kernel(**inputs):
    import numpy as _np
    import concourse.bacc as _bacc
    from concourse import mybir as _mybir
    from concourse.bass_utils import run_bass_kernel_spmd as _run

    nc = _bacc.Bacc("TRN2", target_bir_lowering=False, num_devices=1)
    arrays, ins, outs = {"in_const_dram": CONST}, {}, {}
    for name in _INS:
        a = _np.ascontiguousarray(inputs[name])
        arrays[f"in_{name}_dram"] = a
        ins[name] = nc.dram_tensor(f"in_{name}_dram", a.shape, _mybir.dt.from_np(a.dtype), kind="ExternalInput").ap()
    const_in = nc.dram_tensor("in_const_dram", CONST.shape, _mybir.dt.float32, kind="ExternalInput").ap()
    for name, shape in _OUTS.items():
        outs[name] = nc.dram_tensor(f"out_{name}_dram", shape, _mybir.dt.float32, kind="ExternalOutput").ap()
    build(nc, ins, outs, const_in)
    r = _run(nc, [arrays], core_ids=[0])
    return tuple(r.results[0][f"out_{name}_dram"] for name in _OUTS)
```

```python
from contextlib import ExitStack
import math

import numpy as np
import concourse.bass as bass
from concourse import mybir

P = 128
D_MODEL, SEQ, DEC_BATCH, DEC_SEQ = 1024, 512, 8, 8
PAST_LEN, PAGE_SIZE, HEAD_DIM = 1024, 128, 64
N_PAGES = PAST_LEN // PAGE_SIZE
SAMP = DEC_BATCH * DEC_SEQ
TOK = SEQ + SAMP
PT = SEQ // P
NT = PT + 1
KC = D_MODEL // P
D_FF = ((8 * D_MODEL + 3 * 256 - 1) // (3 * 256)) * 256
FC = D_FF // P
HALF = HEAD_DIM // 2
FOX = D_MODEL // (2 * HEAD_DIM)
DIFF = D_MODEL // (4 * HEAD_DIM)
HEADS = 16
KVH = 4
IDXH = 4
KEYS = PAST_LEN + DEC_SEQ
BANK = 512
EPS = 1e-6
SCALE = HEAD_DIM ** -0.5
LAMBDA_INIT = 0.8 - 0.6 * math.exp(-0.3 * 0)
NEG = -1e30
TAKEN = -3e38
K_PROMPT, K_SAMPLE = min(256, SEQ // 4), min(256, KEYS // 4)

ALU = mybir.AluOpType
ACT = mybir.ActivationFunctionType
AX = mybir.AxisListType.X
F32 = mybir.dt.float32
F32R = mybir.dt.float32r
I32 = mybir.dt.int32
ds = bass.ds


def rows_of(t):
    return P if t < PT else SAMP


def bc(ap, axis, n):
    shape = list(ap.shape)
    shape.insert(axis, n)
    return ap.unsqueeze(axis).to_broadcast(shape)


def constant_table():
    cols, at = [], {}

    def put(name, a):
        a = np.asarray(a, np.float32)
        full = np.zeros((P, a.shape[1]), np.float32)
        full[:a.shape[0]] = a
        at[name] = (sum(c.shape[1] for c in cols), a.shape[1])
        cols.append(full)

    i = np.arange(P)
    put("ident", np.eye(P))
    put("causal", np.where(i[None, :] <= i[:, None], 0.0, NEG))
    put("step", np.arange(SEQ)[None, :] >= i[:, None])
    row_head, row_query = i // DEC_SEQ, i % DEC_SEQ
    h8 = np.arange(8)
    put("fox_sel", -(h8[:, None] == row_head[None, :]).astype(float))
    put("query_sel", h8[:, None] == row_query[None, :])
    put("new_mask", np.where(h8[None, :] <= row_query[:, None], 0.0, NEG))
    put("idx_sel", (i[:32, None] % DEC_SEQ) == h8[None, :])
    s = np.arange(SAMP)
    put("page_tri", (s[:, None] // N_PAGES == s[None, :] // N_PAGES) & (s[:, None] < s[None, :]))
    put("tok_tri", (s[:, None] // DEC_SEQ == s[None, :] // DEC_SEQ) & (s[:, None] <= s[None, :]))
    put("same_batch", s[:, None] // DEC_SEQ == s[None, :] // DEC_SEQ)
    second = (row_head >= FOX) & (row_head % 2 == 1)
    put("is_first", ~second[:, None])
    put("is_second", -second[:, None].astype(float))
    put("minus_half", np.full((P, 16), -0.5))
    put("ones", np.ones((P, P)))
    pos = np.concatenate([np.arange(SEQ), np.tile(PAST_LEN + np.arange(DEC_SEQ), DEC_BATCH), np.zeros(SAMP)])
    expo = -np.arange(HALF, dtype=np.float32) * np.float32(2.0 / HEAD_DIM)
    inv = np.power(np.float32(10000.0), expo).astype(np.float32)
    ang = (pos.astype(np.float32)[:, None] * inv[None, :]).astype(np.float64)
    tile = lambda a: a.reshape(NT, P, HALF).transpose(1, 0, 2).reshape(P, NT * HALF)
    put("cos", tile(np.cos(ang)))
    put("sin", tile(np.sin(ang)))
    put("minus_sin", tile(-np.sin(ang)))
    return np.ascontiguousarray(np.concatenate(cols, axis=1)), at


CONST, CONST_AT = constant_table()


class Steps:

    def __init__(self, eng, sem, before=0):
        self.eng, self.sem, self.before, self.n = eng, sem, before, 0

    def ok(self, ins):
        self.n += 1
        return ins.then_inc(self.sem, 1)

    def wait(self):
        self.eng.wait_ge(self.sem, self.before + self.n)


class Kernel:
    pass


class Weights:

    SIZE = 4 * BANK

    def __init__(self, K, sem):
        self.K, self.tiles, self.issued, self.counts, self.landed = K, [], 0, [0, 0], []
        self.sem_landed = [sem("weights_landed_0"), sem("weights_landed_1")]
        self.split_hi, self.split_lo = sem("weights_split_hi"), sem("weights_split_lo")
        self.used, self.late = {}, None

    def leave(self, n):
        self.late = n if n < len(self.tiles) else None

    def take_late(self):
        n, self.late = self.late, None
        return n

    def add(self, parts):
        n = len(self.tiles)
        pieces = parts(self.K.w_raw[:, n % 2, :])
        self.tiles.append(pieces)
        self.counts[n % 2] += 16 * len(pieces)
        self.landed.append(self.counts[n % 2])
        return n

    def load_up_to(self, sp, last):
        while self.issued <= min(last, len(self.tiles) - 1):
            n = self.issued
            if n >= 2:
                sp.wait_ge(self.split_lo, n - 1)
            for dst, src in self.tiles[n]:
                sp.dma_start(dst, src).then_inc(self.sem_landed[n % 2], 16)
            self.issued += 1

    def hi(self, act, n, landed_more=0):
        if n < len(self.tiles):
            act.wait_ge(self.sem_landed[n % 2], self.landed[n] + landed_more)
            act.activation(self.K.w_hi[:, n % 2, :], self.K.w_raw[:, n % 2, :], ACT.Copy).then_inc(self.split_hi, 1)

    def lo(self, dve, n, count_more=0):
        if n < len(self.tiles):
            dve.wait_ge(self.split_hi, n + 1 + count_more)
            dve.tensor_tensor(self.K.w_lo[:, n % 2, :], self.K.w_raw[:, n % 2, :],
                              self.K.w_hi[:, n % 2, :].bitcast(F32), ALU.subtract).then_inc(self.split_lo, 1)

    def split_after(self, eng, n, half):
        if n + 2 < len(self.tiles):
            eng.wait_ge(*self.used[n])
            half(eng, n + 2)

    def parts_of(self, n):
        return self.K.w_hi[:, n % 2, :], self.K.w_lo[:, n % 2, :]

    def ready(self, eng, n, more=0):
        eng.wait_ge(self.split_lo, n + 1 + more)


def three_passes(pe, out, lhs, rhs, start, stop):
    pe.matmul(out, lhs[0], rhs[1], start=start, stop=False)
    pe.matmul(out, lhs[1], rhs[0], start=False, stop=False)
    return pe.matmul(out, lhs[0], rhs[0], start=False, stop=stop)


def column_tile(w, k0, kn, c0, cn):
    def parts(slot):
        view = slot[:, 0:kn * cn].rearrange("p (k n) -> p k n", k=kn)
        return [(view, w[k0 * P:(k0 + kn) * P, c0:c0 + cn].rearrange("(k p) n -> p k n", p=P))]
    return parts


def gate_up_tile(wg, wu, c0):
    def parts(slot):
        view = slot.rearrange("p (a k n) -> p a k n", a=2, k=KC)
        return [(view[:, a], w[:, c0:c0 + P].rearrange("(k p) n -> p k n", p=P)) for a, w in enumerate((wg, wu))]
    return parts


def load_inputs(nc, K):
    dma, small = K.sem("tokens_landed"), K.sem("small_landed")
    K.weights.leave(1)
    with nc.Block() as block:
        @block.sync
        def _(sp):
            sp.dma_start(K.resid[:, 0:PT, :], K.x_prompt[0].rearrange("(t p) d -> p t d", p=P)).then_inc(dma, 16)
            sp.dma_start(K.resid[0:SAMP, PT, :], K.x_sample.rearrange("b t d -> (b t) d")).then_inc(dma, 16)
            sp.dma_start(K.const[:, :], K.const_in).then_inc(dma, 16)
            K.weights.load_up_to(sp, 2)
            sp.wait_ge(dma, 48)

        @block.scalar
        def _(act):
            pairs = [(K.head_gain[:, i, :], g.partition_broadcast(P)) for i, g in enumerate(K.head_gains)]
            pairs += [(K.subln_row[:, :], K.subln0.partition_broadcast(P)),
                      (K.bias_f[:, :], K.b_f0.partition_broadcast(P)),
                      (K.pages[:, :], K.page_table.rearrange("(a b) n -> a (b n)", a=1)),
                      (K.page_rows[:, :], K.page_table.rearrange("b (n a) -> (b n) a", a=1)),
                      (K.subln_col[:, :], K.subln0.rearrange("(p a) -> p a", a=1))]
            pairs += [(K.lams[:, i, :], g.partition_broadcast(P)) for i, g in enumerate(K.lam_vecs)]
            for dst, src in pairs:
                act.dma_start(dst, src).then_inc(small, 16)
            K.weights.hi(act, 0)
            act.wait_ge(small, 16 * len(pairs))

        @block.vector
        def _(dve):
            K.weights.lo(dve, 0)


def norm_to_features(nc, K, gain, tag):
    squared, mean_ok, rstd_ok, scaled = (K.sem(f"{tag}_{x}") for x in ("squared", "mean_ok", "rstd_ok", "scaled"))
    turned, out_act, out_dve, gain_in = (K.sem(f"{tag}_{x}") for x in ("turned", "out_act", "out_dve", "gain_in"))
    with ExitStack() as mem:
        sb = lambda name, shape: mem.enter_context(nc.sbuf_tensor(f"{tag}_{name}", shape, F32))
        square = sb("square", [P, D_MODEL])
        ms = sb("ms", [P, NT])
        rstd = sb("rstd", [P, NT])
        xn = sb("xn", [P, 2, D_MODEL])
        gain_row = sb("gain_row", [P, D_MODEL])
        block = mem.enter_context(nc.Block())

        def out_of_psum(eng):
            for t in range(NT):
                n = rows_of(t)
                yield t
                for half in range(2):
                    u = 2 * t + half
                    src = K.ps[:, u % 4, :].rearrange("p (c n) -> p c n", n=P)[:, :, 0:n]
                    hi, lo = (x[:, 4 * half:4 * half + 4, t * P:t * P + n] for x in (K.feat_hi, K.feat_lo))
                    eng.wait_ge(turned, u + 1)
                    if eng is nc.vector:
                        eng.wait_ge(out_act, u + 1)
                        eng.tensor_tensor(lo, src, hi.bitcast(F32), ALU.subtract).then_inc(out_dve, 1)
                    else:
                        eng.activation(hi, src, ACT.Copy).then_inc(out_act, 1)

        @block.sync
        def _(sp):
            sp.dma_start(gain_row[:, :], K.norm_gains[gain].partition_broadcast(P)).then_inc(gain_in, 16)

        @block.scalar
        def _(act):
            for t in range(NT):
                n = rows_of(t)
                if t:
                    act.wait_ge(squared, t)
                act.activation(square[0:n, :], K.resid[0:n, t, :], ACT.Square,
                               accum_out=ms[0:n, t:t + 1]).then_inc(squared, 1)
            for _t in out_of_psum(act):
                pass

        @block.gpsimd
        def _(pool):
            for t in range(NT):
                n = rows_of(t)
                pool.wait_ge(mean_ok, t + 1)
                pool.tensor_tensor(rstd[0:n, t:t + 1], ms[0:n, t:t + 1], K.c("minus_half")[0:n, 0:1],
                                   ALU.pow).then_inc(rstd_ok, 1)

        @block.vector
        def _(dve):
            def mean(t):
                n = rows_of(t)
                dve.wait_ge(squared, t + 1)
                dve.tensor_scalar(ms[0:n, t:t + 1], ms[0:n, t:t + 1], 1.0 / D_MODEL, EPS, ALU.mult, ALU.add)\
                   .then_inc(mean_ok, 1)
            out = out_of_psum(dve)
            mean(0)
            for t in range(NT):
                n = rows_of(t)
                if t + 1 < NT:
                    mean(t + 1)
                dve.wait_ge(rstd_ok, t + 1)
                if t >= 2:
                    dve.wait_ge(turned, 2 * (t - 1))
                if t == 0:
                    dve.wait_ge(gain_in, 16)
                dve.scalar_tensor_tensor(out=xn[0:n, t % 2, :], in0=K.resid[0:n, t, :], scalar=rstd[0:n, t:t + 1],
                                         in1=gain_row[0:n, :], op0=ALU.mult, op1=ALU.mult).then_inc(scaled, 1)
                if t >= 1:
                    next(out)
            for _t in out:
                pass

        @block.tensor
        def _(pe):
            for t in range(NT):
                n = rows_of(t)
                pe.wait_ge(scaled, t + 1)
                for half in range(2):
                    if t >= 2:
                        pe.wait_ge(out_dve, 2 * t + half - 3)
                    for j in range(4):
                        c = 4 * half + j
                        ins = pe.transpose(K.ps[:, (2 * t + half) % 4, j * P:j * P + n],
                                           xn[0:n, t % 2, c * P:(c + 1) * P], K.c("ident")[0:n, 0:n])
                    ins.then_inc(turned, 1)


class Part:

    def __init__(self, tiles, width, heads=0, norm=None, rope=False, stores=(), turns=(), copies=(), paired=False):
        self.paired = paired
        self.tiles, self.width, self.heads, self.norm, self.rope = tiles, width, heads, norm, rope
        self.stores, self.turns, self.copies = stores, turns, copies


class Item:

    def __init__(self, part, t):
        self.p, self.t, self.rows = part, t, rows_of(t)
        self.norm = self.head = self.ready = self.copy = None


def project(nc, K, parts, tag, aside=None):
    names = ("multiplied", "squared", "mean_ok", "rstd_ok", "gained", "psum_free", "roped", "turned",
             "turned_out", "copied", "chain", "copies_stored", "passed")
    S = {n: K.sem(f"{tag}_{n}") for n in names}
    stored = [K.sem(f"{tag}_stored_{i}") for i in range(3)]
    items = [(p, t) for p in parts for t in range(NT)]
    n_norm = n_rope = n_head = n_copy = 0
    info = []
    for p, t in items:
        it = Item(p, t)
        if p.heads:
            it.head = n_head
            n_head += 1
            if p.norm is not None:
                it.norm = n_norm
                n_norm += 1
            if p.rope:
                n_rope += 1
                it.ready = (S["roped"], n_rope)
            else:
                it.ready = (S["gained"], n_norm)
        if p.copies:
            it.copy = n_copy
            n_copy += 1
        info.append(it)
    store_count = [0, 0, 0]
    for it in info:
        it.store_before = None
        if it.head is not None:
            it.store_before = store_count[it.head % 3]
            if it.p.stores:
                store_count[it.head % 3] += 16
    W = K.weights
    late = W.take_late()
    n_passed = 0
    for i, p in enumerate(parts):
        for n, _ in p.tiles[:-1]:
            n_passed += 1
            W.used[n] = (S["passed"], n_passed)
        W.used[p.tiles[-1][0]] = (S["multiplied"], NT * (i + 1))

    def splits(eng, half, i):
        p, t = items[i]
        for n, _ in p.tiles[:-1] if t == 0 else p.tiles[-1:] if t == NT - 1 else ():
            W.split_after(eng, n, half)
    copy_stores = sum(len([c for c in it.p.copies if c[2 if it.t < PT else 3] is not None]) for it in info)
    heads = [it for it in info if it.head is not None]

    with ExitStack() as mem:
        sb = lambda name, shape: mem.enter_context(nc.sbuf_tensor(f"{tag}_{name}", shape, F32))
        square = sb("square", [P, 2, BANK])
        ms = sb("ms", [P, 2, 8])
        rstd = sb("rstd", [P, 2, 8])
        xn = sb("xn", [P, 2, BANK])
        straight = sb("straight", [P, BANK])
        crossed = sb("crossed", [P, BANK])
        res = sb("res", [P, 3, BANK])
        block = mem.enter_context(nc.Block())

        def res_free(eng, it):
            if it.head >= 3:
                eng.wait_ge(S["turned"], it.head - 2)
                if it.store_before:
                    eng.wait_ge(stored[it.head % 3], it.store_before)

        @block.sync
        def _(sp):
            tiles = [n for p in parts for n, _ in p.tiles]
            for i, n in enumerate(tiles):
                W.load_up_to(sp, n + 2)
                if aside is not None:
                    for j in range(DEC_BATCH * i // len(tiles), DEC_BATCH * (i + 1) // len(tiles)):
                        aside(sp, j)

        @block.tensor
        def _(pe):
            def turn(it):
                pe.wait_ge(*it.ready)
                if it.head >= 2:
                    pe.wait_ge(S["turned_out"], it.head - 1)
                for j, (src, _, _) in enumerate(it.p.turns):
                    n = it.rows
                    ins = pe.transpose(K.ps[:, 6 + it.head % 2, j * P:j * P + n], src(res[0:n, it.head % 3, :]),
                                       K.c("ident")[0:n, 0:n])
                ins.then_inc(S["turned"], 1)

            MAIN = 6
            for b, p in enumerate(parts):
                block_items = info[b * NT:(b + 1) * NT]
                for a, (tile, chunks) in enumerate(p.tiles):
                    W.ready(pe, tile)
                    hi, lo = (x[:, 0:len(chunks) * p.width].rearrange("p (k n) -> p k n", n=p.width)
                              for x in W.parts_of(tile))
                    last = a == len(p.tiles) - 1
                    for t, it in enumerate(block_items):
                        i, n = b * NT + t, it.rows
                        if a == 0 and i >= MAIN:
                            pe.wait_ge(S["psum_free"], i - MAIN + 1)
                        for k, c in enumerate(chunks):
                            cols = slice(t * P, t * P + n)
                            ins = three_passes(pe, K.ps[0:n, i % MAIN, 0:p.width],
                                               (K.feat_hi[:, c, cols], K.feat_lo[:, c, cols]), (hi[:, k, :], lo[:, k, :]),
                                               c == 0, c == KC - 1)
                        if last:
                            ins.then_inc(S["multiplied"], 1)
                        elif t == NT - 1:
                            ins.then_inc(S["passed"], 1)
                        if ((a == 0 and t < 3) or (last and t >= 3)) and i >= 3 and info[i - 3].head is not None:
                            turn(info[i - 3])
            for it in info[-3:]:
                if it.head is not None:
                    turn(it)

        @block.scalar
        def _(act):
            def turn_out(it):
                act.wait_ge(S["turned"], it.head + 1)
                n = it.rows
                todo = it.p.turns
                for j, (_, dst, scale) in enumerate(todo):
                    src = K.ps[:, 6 + it.head % 2, j * P:j * P + n]
                    ins = act.activation(dst(it.t), src, ACT.Copy, scale=scale)
                ins.then_inc(S["turned_out"], 1)

            def store(it):
                act.wait_ge(*it.ready)
                for sl, dst in it.p.stores:
                    act.dma_start(dst(it.t), res[0:it.rows, it.head % 3, sl]).then_inc(stored[it.head % 3], 16)

            def store_copies(it):
                act.wait_ge(S["copied"], it.copy + 1)
                for c in it.p.copies:
                    dram = c[2 if it.t < PT else 3]
                    if dram is not None:
                        act.dma_start(dram(it.t), c[1](it.t)).then_inc(S["copies_stored"], 16)

            if late is not None:
                W.hi(act, late)
            for b in range(len(parts)):
                now = info[b * NT:(b + 1) * NT]
                for x in range(NT + 3):
                    if x < NT:
                        it = now[x]
                        splits(act, W.hi, b * NT + x)
                        if it.norm is not None:
                            act.wait_ge(S["multiplied"], b * NT + x + 1)
                            if it.norm >= 2:
                                act.wait_ge(S["mean_ok"], it.norm - 1)
                            act.activation(square[0:it.rows, it.norm % 2, 0:it.p.heads],
                                           K.ps[0:it.rows, (b * NT + x) % 6, 0:it.p.heads],
                                           ACT.Square).then_inc(S["squared"], 1)
                    if 1 <= x <= NT and now[x - 1].copy is not None:
                        store_copies(now[x - 1])
                    if 2 <= x <= NT + 1 and now[x - 2].p.stores:
                        store(now[x - 2])
                    if 3 <= x and now[x - 3].head is not None:
                        turn_out(now[x - 3])
            for s, n in zip(stored, store_count):
                if n:
                    act.wait_ge(s, n)
            if copy_stores:
                act.wait_ge(S["copies_stored"], 16 * copy_stores)

        @block.gpsimd
        def _(pool):
            def power(it):
                n, m, nh = it.rows, it.norm, it.p.heads // HEAD_DIM
                pool.wait_ge(S["mean_ok"], m + 1)
                pool.tensor_tensor(rstd[0:n, m % 2, 0:nh], ms[0:n, m % 2, 0:nh], K.c("minus_half")[0:n, 0:nh],
                                   ALU.pow).then_inc(S["rstd_ok"], 1)

            def gained(it, i):
                n, m, nh = it.rows, it.norm, it.p.heads // HEAD_DIM
                pool.wait_ge(S["psum_free"], i + 1)
                view = xn[0:n, m % 2, 0:it.p.heads].rearrange("p (h d) -> p h d", d=HEAD_DIM)
                gain = bc(K.head_gain[0:n, it.p.norm, :], 1, nh)
                if it.p.rope:
                    dst = view
                else:
                    res_free(pool, it)
                    dst = res[0:n, it.head % 3, 0:it.p.heads].rearrange("p (h d) -> p h d", d=HEAD_DIM)
                pool.tensor_tensor(dst, view, gain, ALU.mult).then_inc(S["gained"], 1)
            for b, p in enumerate(parts):
                if p.norm is not None:
                    for x in range(NT + 1):
                        if x < NT:
                            power(info[b * NT + x])
                        if x >= 1:
                            gained(info[b * NT + x - 1], b * NT + x - 1)

        @block.vector
        def _(dve):
            s = Steps(dve, S["chain"])

            def mean(i):
                it = info[i]
                n, m, nh = it.rows, it.norm, it.p.heads // HEAD_DIM
                dve.wait_ge(S["squared"], m + 1)
                if m >= 2:
                    dve.wait_ge(S["rstd_ok"], m - 1)
                s.ok(dve.tensor_reduce(ms[0:n, m % 2, 0:nh],
                                       square[0:n, m % 2, 0:it.p.heads].rearrange("p (h d) -> p h d", d=HEAD_DIM),
                                       AX, ALU.add))
                s.wait()
                dve.tensor_scalar(ms[0:n, m % 2, 0:nh], ms[0:n, m % 2, 0:nh], 1.0 / HEAD_DIM, EPS,
                                  ALU.mult, ALU.add).then_inc(S["mean_ok"], 1)

            def leave_psum(i):
                it = info[i]
                n, p, m, nh = it.rows, it.p, it.norm, it.p.heads // HEAD_DIM
                ps = K.ps[0:n, i % 6, :]
                dve.wait_ge(S["multiplied"], i + 1)
                if p.copies:
                    for k, (sl, dst, _, _, how) in enumerate(p.copies):
                        ins = how(dve, dst(it.t), ps[:, sl], s) if how else dve.tensor_copy(dst(it.t), ps[:, sl])
                        if k < len(p.copies) - 1:
                            s.ok(ins)
                    ins.then_inc(S["copied"], 1)
                if m is not None:
                    dve.wait_ge(S["rstd_ok"], m + 1)
                    if m >= 2:
                        dve.wait_ge(S["gained"], m - 1)
                    s.wait()
                    dve.tensor_tensor(xn[0:n, m % 2, 0:p.heads].rearrange("p (h d) -> p h d", d=HEAD_DIM),
                                      ps[:, 0:p.heads].rearrange("p (h d) -> p h d", d=HEAD_DIM),
                                      bc(rstd[0:n, m % 2, 0:nh], 2, HEAD_DIM), ALU.mult).then_inc(S["psum_free"], 1)
                elif p.rope:
                    rotate(i, ps[:, 0:p.heads])
                else:
                    dve.wait_ge(S["copied"], it.copy + 1)
                    dve.sem_inc(S["psum_free"], 1)

            def rotate(i, src):
                it = info[i]
                n, p, t, nh = it.rows, it.p, it.t, it.p.heads // HEAD_DIM
                four = src.rearrange("p (h a d) -> p h a d", a=2, d=HALF)
                st = straight[0:n, 0:p.heads].rearrange("p (h a d) -> p h a d", a=2, d=HALF)
                cr = crossed[0:n, 0:p.heads].rearrange("p (h a d) -> p h a d", a=2, d=HALF)
                cos, sin, msin = (K.c(x)[0:n, t * HALF:(t + 1) * HALF] for x in ("cos", "sin", "minus_sin"))
                s.wait()
                for a in range(2):
                    s.ok(dve.tensor_tensor(st[:, :, a, :], four[:, :, a, :], bc(cos, 1, nh), ALU.mult))
                s.ok(dve.tensor_tensor(cr[:, :, 0, :], four[:, :, 1, :], bc(msin, 1, nh), ALU.mult))
                ins = dve.tensor_tensor(cr[:, :, 1, :], four[:, :, 0, :], bc(sin, 1, nh), ALU.mult)
                if it.norm is None:
                    ins.then_inc(S["psum_free"], 1)
                    dve.wait_ge(S["psum_free"], i + 1)
                else:
                    s.ok(ins)
                s.wait()
                res_free(dve, it)
                if p.heads == 5 * HEAD_DIM:
                    s.ok(dve.tensor_tensor(res[0:n, it.head % 3, p.heads:p.heads + HEAD_DIM],
                                           straight[0:n, p.heads - HEAD_DIM:p.heads],
                                           crossed[0:n, p.heads - HEAD_DIM:p.heads], ALU.add))
                    s.wait()
                dst, a, b = res[0:n, it.head % 3, 0:p.heads], straight[0:n, 0:p.heads], crossed[0:n, 0:p.heads]
                if p.paired:
                    dst = dst.rearrange("p (r a d) -> p a r d", a=2, d=HEAD_DIM)
                    a, b = (x.rearrange("p (a r d) -> p a r d", a=2, d=HEAD_DIM) for x in (a, b))
                dve.tensor_tensor(dst, a, b, ALU.add).then_inc(S["roped"], 1)
                dve.wait_ge(*it.ready)

            if late is not None:
                W.lo(dve, late)
            for b, p in enumerate(parts):
                for x in range(NT + 2):
                    i = b * NT + x
                    if x < NT:
                        splits(dve, W.lo, i)
                        if p.norm is not None:
                            mean(i)
                    if 1 <= x <= NT:
                        leave_psum(i - 1)
                    if 2 <= x and p.norm is not None and p.rope:
                        it = info[i - 2]
                        dve.wait_ge(S["gained"], it.norm + 1)
                        rotate(i - 2, xn[0:it.rows, it.norm % 2, 0:p.heads])


def forget_sums(nc, K):
    S = {n: K.sem("sums_" + n) for n in ("chain", "scanned", "summed", "out", "scratch", "broadcast", "lam_sum", "lam_exp")}
    S["pages_in"] = nc.alloc_semaphore(name="sums_pages_in")
    with ExitStack() as mem:
        sb = lambda name, shape: mem.enter_context(nc.sbuf_tensor("sums_" + name, shape, F32))
        page_logf = sb("page_logf", [SAMP, PAGE_SIZE * FOX])
        page_cum = sb("page_cum", [SAMP, FOX, PAGE_SIZE])
        zero = sb("zero", [SAMP, PAGE_SIZE])
        total = sb("total", [SAMP, FOX])
        carry = sb("carry", [SAMP, FOX])
        prompt_row = sb("prompt_row", [FOX, SEQ])
        new_row = sb("new_row", [FOX, SAMP])
        prod = sb("prod", [P, HEAD_DIM])
        lam_sum = sb("lam_sum", [P, 2])
        lam_exp = sb("lam_exp", [P, 2])
        block = mem.enter_context(nc.Block())
        CP, CARRY, NEW = K.ps[0:FOX, 0, :], K.ps[0:SAMP, 1, 0:FOX], K.ps[0:FOX, 2, 0:SAMP]
        scr = K.fox_rows

        @block.gpsimd
        def _(pool):
            pool.indirect_dma_start(page_logf[:, :], None, K.cache_l0_logf.rearrange("n k h -> n (k h)"),
                                    bass.IndirectOffsetOnAxis(ap=K.page_rows[:, 0:1], axis=0)).then_inc(S["pages_in"], 16)

        @block.tensor
        def _(pe):
            for t in range(PT):
                ins = pe.matmul(CP[:, t * P:SEQ], K.logf[:, t, :], K.c("step")[:, 0:SEQ - t * P],
                                start=(t == 0), stop=(t == PT - 1))
            ins.then_inc(S["summed"], 1)
            pe.wait_ge(S["scanned"], 1)
            pe.matmul(CARRY, K.c("page_tri")[0:SAMP, :], total[:, :], start=True, stop=True).then_inc(S["summed"], 1)
            pe.matmul(NEW, K.logf[0:SAMP, PT, :], K.c("tok_tri")[0:SAMP, :], start=True, stop=False)
            pe.matmul(NEW, total[:, :], K.c("same_batch")[0:SAMP, :], start=False, stop=True).then_inc(S["summed"], 1)

        @block.scalar
        def _(act):
            act.wait_ge(S["lam_sum"], 2)
            act.activation(lam_exp[:, :], lam_sum[:, :], ACT.Exp).then_inc(S["lam_exp"], 1)

        @block.vector
        def _(dve):
            s = Steps(dve, S["chain"])
            s.ok(dve.memset(zero[:, :], 0.0))
            for i in range(2):
                if i:
                    dve.wait_ge(S["lam_sum"], 1)
                dve.tensor_tensor_reduce(prod[:, :], K.lams[:, 2 * i, :], K.lams[:, 2 * i + 1, :], 1.0, 0.0,
                                         ALU.mult, ALU.add, lam_sum[:, i:i + 1]).then_inc(S["lam_sum"], 1)
            dve.wait_ge(S["summed"], 1)
            dve.tensor_scalar(prompt_row[:, :], CP, -1.0, None, ALU.mult).then_inc(S["out"], 1)
            dve.wait_ge(S["pages_in"], 16)
            s.wait()
            by_head = page_logf[:, :].rearrange("p (k h) -> p h k", h=FOX)
            for h in range(FOX):
                s.ok(dve.tensor_tensor_scan(page_cum[:, h, :], by_head[:, h, :], zero[:, :], 0.0, ALU.add, ALU.add))
            s.wait()
            dve.tensor_copy(total[:, :], page_cum[:, :, PAGE_SIZE - 1]).then_inc(S["scanned"], 1)
            dve.wait_ge(S["summed"], 2)
            s.ok(dve.tensor_copy(carry[:, :], CARRY))
            s.wait()
            dve.wait_ge(S["scanned"], 1)
            dve.tensor_tensor(page_cum[:, :, :], page_cum[:, :, :], bc(carry[:, :], 2, PAGE_SIZE), ALU.add)\
               .then_inc(S["out"], 1)
            dve.wait_ge(S["summed"], 3)
            dve.tensor_copy(new_row[:, :], NEW).then_inc(S["out"], 1)
            dve.wait_ge(S["lam_exp"], 1)
            s.ok(dve.tensor_scalar(K.lam[:, :], lam_exp[:, 0:1], lam_exp[:, 1:2], LAMBDA_INIT, ALU.subtract, ALU.add))
            s.wait()
            s.ok(dve.tensor_scalar(K.coef[:, :], K.c("is_second"), K.lam[:, 0:1], K.c("is_first"),
                                   ALU.mult, ALU.add))
            s.ok(dve.tensor_scalar(K.minus_lam[:, :], K.lam[:, :], -1.0, None, ALU.mult))
            s.ok(dve.tensor_scalar(K.subln_col8[:, :], K.subln_col[:, :], 1.0 - LAMBDA_INIT, None, ALU.mult))
            s.ok(dve.tensor_scalar(K.subln_row8[:, :], K.subln_row[:, :], 1.0 - LAMBDA_INIT, None, ALU.mult))
            s.wait()

        @block.sync
        def _(sp):
            sp.wait_ge(S["out"], 1)
            sp.dma_start(K.prompt_rows, prompt_row[:, :]).then_inc(S["scratch"], 16)
            sp.wait_ge(S["scratch"], 16)
            sp.dma_start(K.minus_c[:, :, :], K.prompt_rows.partition_broadcast(P)).then_inc(S["broadcast"], 16)
            sp.wait_ge(S["out"], 2)
            for b in range(DEC_BATCH):
                dst = scr[b, :, 0:PAST_LEN].rearrange("h (j k) -> j h k", j=N_PAGES)
                sp.dma_start(dst, page_cum[b * N_PAGES:(b + 1) * N_PAGES, :, :]).then_inc(S["scratch"], 16)
            sp.wait_ge(S["out"], 3)
            sp.dma_start(scr[:, :, PAST_LEN:KEYS].rearrange("b h t -> h b t"),
                         new_row[:, :].rearrange("h (b t) -> h b t", b=DEC_BATCH)).then_inc(S["scratch"], 16)
            sp.wait_ge(S["scratch"], 16 * (2 + DEC_BATCH))
            sp.wait_ge(S["broadcast"], 16)


def prompt_attention(nc, K, tag, q_at, k_at, v_at, bias_at, diag, out_at, second, sample_top=None):
    names = ("scored", "shifted", "exped", "turned", "turned_out", "weighed", "out", "chain")
    S = {n: K.sem(f"{tag}_{n}") for n in names}
    units = [(h, qt) for h in range(HEADS) for qt in range(PT)]
    n = len(units)
    with ExitStack() as mem:
        sb = lambda name, shape: mem.enter_context(nc.sbuf_tensor(f"{tag}_{name}", shape, F32))
        scores = sb("scores", [P, 4, SEQ])
        probs = sb("probs", [P, 4, SEQ])
        probs_t = sb("probs_t", [P, 3, SEQ])
        top, minus, total, scale, scale2 = (sb(x, [P, n]) for x in ("top", "minus", "total", "scale", "scale2"))
        block = mem.enter_context(nc.Block())

        @block.tensor
        def _(pe):
            for u in range(n + 4):
                if u < n:
                    h, qt = units[u]
                    if u >= 4:
                        pe.wait_ge(S["exped"], u - 3)
                    w = (qt + 1) * P
                    pe.matmul(K.ps[:, u % 4, 0:w], q_at(h, qt), k_at(h)[:, 0:w], start=True, stop=True)\
                      .then_inc(S["scored"], 1)
                if 3 <= u < n + 3:
                    v = u - 3
                    pe.wait_ge(S["exped"], v + 1)
                    if v >= 2:
                        pe.wait_ge(S["turned_out"], v - 1)
                    for j in range(units[v][1] + 1):
                        ins = pe.transpose(K.ps[:, 4 + v % 2, j * P:(j + 1) * P], probs[:, v % 4, j * P:(j + 1) * P],
                                           K.c("ident"))
                    ins.then_inc(S["turned"], 1)
                if u >= 4:
                    v = u - 4
                    h, qt = units[v]
                    pe.wait_ge(S["turned_out"], v + 1)
                    if v >= 2:
                        pe.wait_ge(S["out"], v - 1)
                    for j in range(qt + 1):
                        val = v_at(h, j)
                        ins = pe.matmul(K.ps[:, 6 + v % 2, 0:val.shape[1]], probs_t[:, v % 3, j * P:(j + 1) * P], val,
                                        start=(j == 0), stop=(j == qt))
                    ins.then_inc(S["weighed"], 1)

        @block.scalar
        def _(act):
            for u in range(n + 3):
                if u < n:
                    h, qt = units[u]
                    w = (qt + 1) * P
                    act.wait_ge(S["shifted"], u + 1)
                    if u >= 4:
                        act.wait_ge(S["turned"], u - 3)
                    src = scores[:, u % 4, 0:w] if bias_at(h, qt) is not None else K.ps[:, u % 4, 0:w]
                    act.activation(probs[:, u % 4, 0:w], src, ACT.Exp, bias=minus[:, u:u + 1],
                                   accum_out=total[:, u:u + 1]).then_inc(S["exped"], 1)
                if u >= 3:
                    v = u - 3
                    w = (units[v][1] + 1) * P
                    act.wait_ge(S["turned"], v + 1)
                    if v >= 3:
                        act.wait_ge(S["weighed"], v - 2)
                    act.activation(probs_t[:, v % 3, 0:w], K.ps[:, 4 + v % 2, 0:w], ACT.Copy).then_inc(S["turned_out"], 1)

        @block.vector
        def _(dve):
            s = Steps(dve, S["chain"])
            for u in range(n + 4):
                if u < n:
                    h, qt = units[u]
                    w = (qt + 1) * P
                    ps = K.ps[:, u % 4, 0:w]
                    dve.wait_ge(S["scored"], u + 1)
                    if diag:
                        s.ok(dve.tensor_tensor(ps[:, qt * P:w], ps[:, qt * P:w], K.c("causal"), ALU.add))
                        s.wait()
                    bias = bias_at(h, qt)
                    if bias is not None:
                        if u >= 4:
                            dve.wait_ge(S["exped"], u - 3)
                        s.ok(dve.tensor_tensor_reduce(scores[:, u % 4, 0:w], ps, bias, 1.0, -3e38, ALU.add, ALU.max,
                                                      top[:, u:u + 1]))
                        s.wait()
                        dve.tensor_scalar(minus[:, u:u + 1], top[:, u:u + 1], -1.0, None, ALU.mult)\
                           .then_inc(S["shifted"], 1)
                    else:
                        dve.tensor_reduce(minus[:, u:u + 1], ps, AX, ALU.max, negate=True).then_inc(S["shifted"], 1)
                    if sample_top is not None:
                        for i in range(SampleTop.HALVES * u // n, SampleTop.HALVES * (u + 1) // n):
                            sample_top.half(dve, s, i)
                if u >= 4:
                    v = u - 4
                    h, qt = units[v]
                    dve.wait_ge(S["exped"], v + 1)
                    s.ok(dve.reciprocal(scale[:, v:v + 1], total[:, v:v + 1]))
                    s.wait()
                    dst = out_at(h, qt)
                    acc = K.ps[:, 6 + v % 2, 0:dst.shape[1]]
                    if second(h):
                        s.ok(dve.tensor_scalar(scale2[:, v:v + 1], scale[:, v:v + 1], K.minus_lam[:, 0:1], None,
                                               ALU.mult))
                        s.wait()
                        dve.wait_ge(S["weighed"], v + 1)
                        dve.wait_ge(S["out"], v + 1 - PT)
                        dve.scalar_tensor_tensor(out=dst, in0=acc, scalar=scale2[:, v:v + 1], in1=dst,
                                                 op0=ALU.mult, op1=ALU.add).then_inc(S["out"], 1)
                    else:
                        dve.wait_ge(S["weighed"], v + 1)
                        dve.tensor_scalar(dst, acc, scale[:, v:v + 1], None, ALU.mult).then_inc(S["out"], 1)


        if sample_top is not None:
            @block.sync
            def _(sp):
                sample_top.store(sp)


def turn_attention(nc, K, att, tag, subln):
    S = {n: K.sem(f"{tag}_{n}") for n in ("squared", "mean_ok", "rstd_ok", "normed", "chain", "turned", "out_act", "out_dve",
                                      "sample_hi")}
    with ExitStack() as mem:
        sb = lambda name, shape: mem.enter_context(nc.sbuf_tensor(f"{tag}_{name}", shape, F32))
        if subln:
            square = sb("square", [P, 2, DIFF * P])
            ms = sb("ms", [P, PT, DIFF])
            rstd = sb("rstd", [P, PT, DIFF])
        block = mem.enter_context(nc.Block())

        def feat_part(feat, u):
            return feat[:, 4 * (u % 2):4 * (u % 2) + 4, u // 2 * P:(u // 2 + 1) * P]

        @block.tensor
        def _(pe):
            for t in range(PT):
                for half in range(2):
                    if subln and half:
                        pe.wait_ge(S["normed"], t + 1)
                    for j in range(4):
                        c = 4 * half + j
                        ins = pe.transpose(K.ps[:, 2 * t + half, j * P:(j + 1) * P], att[:, t, c * P:(c + 1) * P],
                                           K.c("ident"))
                    ins.then_inc(S["turned"], 1)

        @block.scalar
        def _(act):
            if subln:
                for t in range(PT):
                    if t >= 2:
                        act.wait_ge(S["mean_ok"], t - 1)
                    act.activation(square[:, t % 2, :], att[:, t, BANK:], ACT.Square).then_inc(S["squared"], 1)
            for u in range(2 * PT):
                act.wait_ge(S["turned"], u + 1)
                act.activation(feat_part(K.feat_hi, u), K.ps[:, u, :].rearrange("p (c n) -> p c n", c=4), ACT.Copy)\
                   .then_inc(S["out_act"], 1)

        @block.gpsimd
        def _(pool):
            if subln:
                for t in range(PT):
                    pool.wait_ge(S["mean_ok"], t + 1)
                    pool.tensor_tensor(rstd[:, t, :], ms[:, t, :], K.c("minus_half")[:, 0:DIFF], ALU.pow)\
                        .then_inc(S["rstd_ok"], 1)

        @block.vector
        def _(dve):
            s = Steps(dve, S["chain"])
            if subln:
                for t in range(PT):
                    dve.wait_ge(S["squared"], t + 1)
                    s.ok(dve.tensor_reduce(ms[:, t, :], square[:, t % 2, :].rearrange("p (h d) -> p h d", h=DIFF),
                                           AX, ALU.add))
                    s.wait()
                    dve.tensor_scalar(ms[:, t, :], ms[:, t, :], 1.0 / P, EPS, ALU.mult, ALU.add).then_inc(S["mean_ok"], 1)
                for t in range(PT):
                    view = att[:, t, BANK:].rearrange("p (h d) -> p h d", h=DIFF)
                    dve.wait_ge(S["rstd_ok"], t + 1)
                    s.ok(dve.tensor_tensor(view, view, bc(rstd[:, t, :], 2, P), ALU.mult))
                    s.wait()
                    dve.tensor_tensor(view, view, bc(K.subln_row8[:, :], 1, DIFF), ALU.mult).then_inc(S["normed"], 1)
            dve.tensor_copy(K.feat_hi[:, :, SEQ:TOK], K.feat_s[:, :, :]).then_inc(S["sample_hi"], 1)
            dve.wait_ge(S["turned"], 2 * PT)
            dve.wait_ge(S["sample_hi"], 1)
            dve.tensor_tensor(K.feat_lo[:, :, SEQ:TOK], K.feat_s[:, :, :], K.feat_hi[:, :, SEQ:TOK].bitcast(F32),
                              ALU.subtract).then_inc(S["sample_hi"], 1)
            for u in range(2 * PT):
                dve.wait_ge(S["out_act"], u + 1)
                dve.tensor_tensor(feat_part(K.feat_lo, u), K.ps[:, u, :].rearrange("p (c n) -> p c n", c=4),
                                  feat_part(K.feat_hi, u).bitcast(F32), ALU.subtract).then_inc(S["out_dve"], 1)


def sample_attention(nc, K, tag, cache_k, cache_v, new_v, row_bias, bias_sel, width, chunks, fill_q, new_k, new_mask,
                     coef, out):
    names = ("q_ok", "turned_act", "turned_dve", "kt_act", "kt_dve", "scored", "shifted",
             "exped", "o_read", "pt_turned", "pt_act", "pt_dve", "weighed", "o_copied", "o_turned", "chain",
             "new_v_in", "bias_in")
    S = {n: K.sem(f"{tag}_{n}") for n in names}
    k_in = [K.sem(f"{tag}_k_in_{j}") for j in range(N_PAGES)]
    v_in = [K.sem(f"{tag}_v_in_{j}") for j in range(N_PAGES)]
    per_bank = BANK // P // chunks if chunks <= 4 else 0
    units = [((j,), range(4 * a, 4 * a + 4)) for j in range(N_PAGES) for a in range(chunks // 4)] if chunks >= 4 else \
            [(range(j, j + per_bank), range(chunks)) for j in range(0, N_PAGES, per_bank)]
    half_units = len(units) // 2
    rows4 = [slice(32 * i, 32 * i + 32) for i in range(4)]
    group_chunks = [(2 * i, 2 * i + 1) if chunks == KC else (i // 2,) for i in range(4)]
    vw = width // 4
    with ExitStack() as mem:
        sb = lambda name, shape: mem.enter_context(nc.sbuf_tensor(f"{tag}_{name}", shape, F32))
        kslot = sb("kslot", [P, N_PAGES, width])
        vslot = sb("vslot", [P, N_PAGES, width])
        kt = [half.rearrange("p (c n) -> p c n", n=BANK)[:, 0:chunks, :] for half in (K.kt0[:, :], K.w_raw.rearrange("p a n -> p (a n)"))]
        qz = sb("qz", [P, chunks, P])
        vnew = sb("vnew", [DEC_SEQ, width])
        bias = sb("bias", [DEC_SEQ, KEYS])
        knew = sb("knew", [P, chunks, DEC_SEQ])
        snew = sb("snew", [P, DEC_SEQ])
        probs = sb("probs", [P, KEYS])
        pt = sb("pt", [P, N_PAGES, P])
        ptn = sb("ptn", [DEC_SEQ, P])
        st = sb("st", [P, 10])
        o_sb = sb("o_sb", [P, max(vw, P)])
        block = mem.enter_context(nc.Block())
        SC, NEWS, NEWT, O = K.ps[:, 2:4, :], K.ps[:, 4, 0:DEC_SEQ], K.ps[0:DEC_SEQ, 4, P:2 * P], K.ps[:, 7, 0:vw]
        OT = K.ps[:, 4, 2 * P:4 * P].rearrange("p (x n) -> p x n", x=2)

        n = len(units)
        cuts = (0, 6, 8, 10, 16) if n == 16 else (0, 2, 3, 4, 4)
        assert len(cuts) == 5 and cuts[4] == n
        stretch = [range(cuts[x], cuts[x + 1]) for x in range(4)]
        LAST = DEC_BATCH - 1

        @block.sync
        def _(sp):
            def page_ids(b):
                return [sp.value_load(K.pages[0:1, n:n + 1], min_val=0, max_val=cache_k.shape[0] - 1)
                        for n in range(b * N_PAGES, (b + 1) * N_PAGES)]

            def load_k(b, ids, pages_of):
                for j in pages_of:
                    i = [n for n, (pages, _) in enumerate(units) if j in pages][-1]
                    sp.wait_ge(S["turned_dve"] if i % 2 else S["turned_act"], b * half_units + i // 2 + 1)
                    sp.dma_start(kslot[:, j, :], cache_k[ds(ids[j], 1), :, :].rearrange("a k d -> (a k) d"))\
                      .then_inc(k_in[j], 16)

            def load_bias(b):
                sp.wait_ge(S["scored"], b * 3 + 1)
                sp.dma_start(bias[:, :], row_bias(b)).then_inc(S["bias_in"], 16)

            def load_v(b, ids, pages_of):
                if pages_of[0] == 0:
                    sp.wait_ge(S["weighed"], b + 1)
                    sp.dma_start(vnew[:, :], new_v(b)).then_inc(S["new_v_in"], 16)
                for j in pages_of:
                    sp.dma_start(vslot[:, j, :], cache_v[ds(ids[j], 1), :, :].rearrange("a k d -> (a k) d"))\
                      .then_inc(v_in[j], 16)
            ids = page_ids(0)
            load_k(0, ids, range(N_PAGES))
            load_bias(0)
            early = N_PAGES // 2 if chunks == KC else N_PAGES
            for b in range(LAST):
                next_ids = page_ids(b + 1)
                load_k(b + 1, next_ids, range(early))
                load_v(b, ids, range(N_PAGES))
                load_k(b + 1, next_ids, range(early, N_PAGES))
                load_bias(b + 1)
                ids = next_ids
            load_v(LAST, ids, range(N_PAGES))

        @block.tensor
        def _(pe):
            def turn_k(b, which):
                for i in which:
                    pages, cs = units[i]
                    for j in pages:
                        pe.wait_ge(k_in[j], b * 16 + 16)
                    pe.wait_ge(S["kt_dve"] if i % 2 else S["kt_act"], b * half_units + i // 2 + 1)
                    for x, (j, c) in enumerate((j, c) for c in cs for j in pages):
                        ins = pe.transpose(K.ps[:, i % 2, x * P:(x + 1) * P], kslot[:, j, c * P:(c + 1) * P],
                                           K.c("ident"))
                    ins.then_inc(S["turned_dve"] if i % 2 else S["turned_act"], 1)

            def score_groups(dst, bias_row, keys_at):
                pe.matmul(dst, bias_sel, bias_row, start=True, stop=True)
                for x in range(len(group_chunks[0])):
                    for i in range(4):
                        c = group_chunks[i][x]
                        ins = pe.matmul(dst[rows4[i], :], qz[:, c, rows4[i]], keys_at(c), start=False,
                                        stop=True, skip_group_check=True)
                ins.then_inc(S["scored"], 1)

            def scores(b):
                pe.wait_ge(S["q_ok"], b + 1)
                pe.wait_ge(S["bias_in"], b * 16 + 16)
                for g in range(2):
                    pe.wait_ge(S["kt_act"], (b * 2 + g + 1) * (half_units // 2) + 1)
                    pe.wait_ge(S["kt_dve"], (b * 2 + g + 1) * (half_units // 2) + 1)
                    if g == 1:
                        pe.wait_ge(S["o_read"], b + 1)
                    score_groups(SC[:, g, :], bias[:, g * BANK:(g + 1) * BANK], lambda c: kt[g][:, c, :])
                score_groups(NEWS, bias[:, PAST_LEN:KEYS], lambda c: knew[:, c, :])

            def turn_probs(b):
                for g in range(2):
                    pe.wait_ge(S["exped"], b * 3 + (1, 3)[g])
                    for j in range(4):
                        ins = pe.transpose(K.ps[:, 5 + g, j * P:(j + 1) * P],
                                           probs[:, (4 * g + j) * P:(4 * g + j + 1) * P], K.c("ident"))
                    if g == 1:
                        ins = pe.transpose(NEWT, probs[:, PAST_LEN:KEYS], K.c("ident"))
                    ins.then_inc(S["pt_turned"], 1)

            def weigh(b):
                pe.wait_ge(S["new_v_in"], b * 16 + 16)
                pe.wait_ge(S["o_copied"], b + 1)
                pe.wait_ge(S["pt_act"], b + 1)
                pe.wait_ge(S["pt_dve"], b + 1)
                for j in range(N_PAGES):
                    pe.wait_ge(v_in[j], b * 16 + 16)
                    for i in range(4):
                        pe.matmul(O[rows4[i], :], pt[:, j, rows4[i]], vslot[:, j, i * vw:(i + 1) * vw],
                                  start=(j == 0), stop=False)
                for i in range(4):
                    ins = pe.matmul(O[rows4[i], :], ptn[:, rows4[i]], vnew[:, i * vw:(i + 1) * vw],
                                    start=False, stop=True)
                ins.then_inc(S["weighed"], 1)

            def turn_o(b):
                pe.wait_ge(S["o_copied"], b + 2)
                for x in range(0, vw, P):
                    ins = pe.transpose(OT[:, x // P, :], o_sb[:, x:x + P], K.c("ident"))
                ins.then_inc(S["o_turned"], 1)

            pe.sem_inc(S["turned_act"], half_units)
            pe.sem_inc(S["turned_dve"], half_units)
            pe.sem_inc(S["weighed"], 1)
            pe.sem_inc(S["scored"], 1)
            pe.sem_inc(S["o_read"], 1)
            turn_k(0, range(len(units)))
            scores(0)
            with pe.Fori(0, LAST) as b:
                turn_k(b + 1, stretch[0])
                turn_probs(b)
                turn_k(b + 1, stretch[1])
                weigh(b)
                turn_k(b + 1, stretch[2])
                turn_o(b)
                turn_k(b + 1, stretch[3])
                scores(b + 1)
            turn_probs(LAST)
            weigh(LAST)
            turn_o(LAST)

        def kt_out(eng, i, b):
            pages, cs = units[i]
            g = pages[0] // 4
            eng.wait_ge(S["turned_dve"] if i % 2 else S["turned_act"], (b + 1) * half_units + i // 2 + 1)
            j0 = pages[0] % 4
            dst = kt[g][:, cs[0]:cs[-1] + 1, j0 * P:(j0 + len(pages)) * P]
            src = K.ps[:, i % 2, :].rearrange("p (c n) -> p c n", c=len(cs))
            if i % 2:
                eng.tensor_copy(dst, src).then_inc(S["kt_dve"], 1)
            else:
                eng.activation(dst, src, ACT.Copy).then_inc(S["kt_act"], 1)

        @block.scalar
        def _(act):
            act.sem_inc(S["kt_act"], 1)

            def keys(b, which):
                for i in which:
                    if i % 2 == 0:
                        kt_out(act, i, b)

            def exps(b):
                act.wait_ge(S["shifted"], b + 1)
                for x, (c0, c1, src) in enumerate(((0, BANK, SC[:, 0, :]), (BANK, PAST_LEN, SC[:, 1, :]),
                                                   (PAST_LEN, KEYS, snew[:, :]))):
                    act.activation(probs[:, c0:c1], src, ACT.Exp, bias=st[:, 3:4], accum_out=st[:, 4 + x:5 + x])\
                       .then_inc(S["exped"], 1)

            def probs_out(b):
                act.wait_ge(S["pt_turned"], b * 2 + 1)
                act.activation(pt[:, 0:4, :], K.ps[:, 5, :].rearrange("p (j n) -> p j n", j=4), ACT.Copy)\
                   .then_inc(S["pt_act"], 1)
            keys(0, range(len(units)))
            with act.Fori(0, LAST) as b:
                act.wait_ge(S["scored"], b * 3 + 4)
                keys(b + 1, stretch[0][:2])
                exps(b)
                keys(b + 1, stretch[0][2:])
                probs_out(b)
                for x in (1, 2, 3):
                    keys(b + 1, stretch[x])
            exps(LAST)
            probs_out(LAST)

        @block.vector
        def _(dve):
            s0 = Steps(dve, S["chain"])
            s0.ok(dve.memset(qz[:, :, :], 0.0))
            dve.memset(o_sb[:, :], 0.0)
            s0.wait()
            dve.sem_inc(S["kt_dve"], 1)
            dve.sem_inc(S["o_copied"], 1)
            STEPS = 7 + (0 if coef is None else 1)

            def queries(b):
                dve.tensor_copy(knew[:, :, :], new_k[:, :, ds(b * DEC_SEQ, DEC_SEQ)])
                fill_q(dve, qz, b, S["q_ok"])

            def keys(b, which):
                for i in which:
                    if i % 2:
                        kt_out(dve, i, b)

            def shift(b, s):
                for g in range(2):
                    dve.wait_ge(S["scored"], b * 3 + 2 + g)
                    s.ok(dve.tensor_reduce(st[:, g:g + 1], SC[:, g, :], AX, ALU.max))
                dve.wait_ge(S["scored"], b * 3 + 4)
                if new_mask is None:
                    s.ok(dve.tensor_copy(snew[:, :], NEWS))
                else:
                    s.ok(dve.tensor_tensor(snew[:, :], NEWS, new_mask, ALU.add))
                s.wait()
                s.ok(dve.tensor_reduce(st[:, 2:3], snew[:, :], AX, ALU.max))
                s.wait()
                dve.tensor_reduce(st[:, 3:4], st[:, 0:3], AX, ALU.max, negate=True).then_inc(S["shifted"], 1)

            def weights(b, s):
                dve.wait_ge(S["exped"], b * 3 + 3)
                s.ok(dve.tensor_reduce(st[:, 7:8], st[:, 4:7], AX, ALU.add))
                s.wait()
                s.ok(dve.reciprocal(st[:, 8:9], st[:, 7:8]))
                s.wait()
                if coef is not None:
                    s.ok(dve.tensor_scalar(st[:, 9:10], st[:, 8:9], coef, None, ALU.mult))
                    s.wait()

            def probs_out(b, s):
                dve.wait_ge(S["pt_turned"], b * 2 + 2)
                s.ok(dve.tensor_copy(ptn[:, :], NEWT))
                assert s.n == STEPS
                dve.tensor_copy(pt[:, 4:8, :], K.ps[:, 6, :].rearrange("p (j n) -> p j n", j=4))\
                   .then_inc(S["pt_dve"], 1)
                s.wait()

            def o_out(b):
                dve.wait_ge(S["weighed"], b + 2)
                dve.tensor_scalar(o_sb[:, 0:vw], O, st[:, 8:9] if coef is None else st[:, 9:10], None, ALU.mult)\
                   .then_inc(S["o_copied"], 1)

            def finish(b):
                dve.wait_ge(S["o_turned"], b + 1)
                out(dve, OT, b).then_inc(S["o_read"], 1)
            queries(0)
            keys(0, range(len(units)))
            with dve.Fori(0, LAST) as b:
                s = Steps(dve, S["chain"], b * STEPS + 1)
                shift(b, s)
                keys(b + 1, stretch[0][:4])
                weights(b, s)
                keys(b + 1, stretch[0][4:])
                probs_out(b, s)
                queries(b + 1)
                keys(b + 1, stretch[1])
                o_out(b)
                keys(b + 1, stretch[2])
                finish(b)
                keys(b + 1, stretch[3])
            s = Steps(dve, S["chain"], LAST * STEPS + 1)
            shift(LAST, s)
            weights(LAST, s)
            probs_out(LAST, s)
            o_out(LAST)
            finish(LAST)


def sample_subln(nc, K):
    S = {n: K.sem("subln_" + n) for n in ("squared", "summed", "mean_ok", "rstd_ok", "chain")}
    with ExitStack() as mem:
        square = mem.enter_context(nc.sbuf_tensor("subln_square", [P, DIFF, SAMP], F32))
        ms = mem.enter_context(nc.sbuf_tensor("subln_ms", [P, DIFF, SAMP], F32))
        root, inv, fix = (mem.enter_context(nc.sbuf_tensor(f"subln_{x}", [P, DIFF, SAMP], F32))
                          for x in ("root", "inv", "fix"))
        block = mem.enter_context(nc.Block())
        view = K.feat_s[:, 4:8, :]

        @block.scalar
        def _(act):
            act.activation(square[:, :, :], view, ACT.Square).then_inc(S["squared"], 1)
            act.wait_ge(S["mean_ok"], 1)
            act.activation(root[:, :, :], ms[:, :, :], ACT.Sqrt).then_inc(S["rstd_ok"], 1)

        @block.tensor
        def _(pe):
            pe.wait_ge(S["squared"], 1)
            pe.matmul(K.ps[:, 0, 0:DIFF * SAMP], K.c("ones"), square[:, :, :].rearrange("p h n -> p (h n)"),
                      start=True, stop=True).then_inc(S["summed"], 1)

        @block.vector
        def _(dve):
            s = Steps(dve, S["chain"])
            dve.wait_ge(S["summed"], 1)
            dve.tensor_scalar(ms[:, :, :], K.ps[:, 0, 0:DIFF * SAMP].rearrange("p (h n) -> p h n", h=DIFF),
                              1.0 / P, EPS, ALU.mult, ALU.add).then_inc(S["mean_ok"], 1)
            dve.wait_ge(S["rstd_ok"], 1)
            s.ok(dve.reciprocal(inv[:, :, :], root[:, :, :]))
            s.wait()
            s.ok(dve.tensor_tensor(fix[:, :, :], inv[:, :, :], inv[:, :, :], ALU.mult))
            s.wait()
            dve.wait_ge(S["mean_ok"], 1)
            s.ok(dve.tensor_tensor(fix[:, :, :], fix[:, :, :], ms[:, :, :], ALU.mult))
            s.wait()
            s.ok(dve.tensor_scalar(fix[:, :, :], fix[:, :, :], -0.5, 1.5, ALU.mult, ALU.add))
            s.wait()
            s.ok(dve.tensor_tensor(fix[:, :, :], fix[:, :, :], inv[:, :, :], ALU.mult))
            s.wait()
            s.ok(dve.scalar_tensor_tensor(out=view, in0=view, scalar=K.subln_col8[:, 0:1], in1=fix[:, :, :],
                                          op0=ALU.mult, op1=ALU.mult))
            s.wait()


def add_product(nc, K, tag, lhs_at, tiles):
    W = K.weights
    multiplied, added, passed = (K.sem(f"{tag}_{x}") for x in ("multiplied", "added", "passed"))
    late, last_tile = W.take_late(), tiles[-1][-1][0]
    W.leave(last_tile + 2)
    n_passed = 0
    for half in range(2):
        for tile, _ in tiles[half][:-1]:
            n_passed += 1
            W.used[tile] = (passed, n_passed)
        W.used[tiles[half][-1][0]] = (multiplied, NT * (half + 1))
    with nc.Block() as block:
        @block.sync
        def _(sp):
            W.load_up_to(sp, last_tile + 3)

        @block.tensor
        def _(pe):
            for half in range(2):
                first, last = tiles[half][0][1][0], tiles[half][-1][1][-1]
                for tile, chunks in tiles[half]:
                    W.ready(pe, tile)
                    hi, lo = (x[:, 0:len(chunks) * BANK].rearrange("p (k n) -> p k n", n=BANK)
                              for x in W.parts_of(tile))
                    for t in range(NT):
                        n, item = rows_of(t), half * NT + t
                        if item >= 8 and chunks[0] == first:
                            pe.wait_ge(added, item - 7)
                        for i, c in enumerate(chunks):
                            ins = three_passes(pe, K.ps[0:n, item % 8, :], lhs_at(c, t), (hi[:, i, :], lo[:, i, :]),
                                               c == first, c == last)
                        if chunks[-1] == last:
                            ins.then_inc(multiplied, 1)
                    if chunks[-1] != last:
                        ins.then_inc(passed, 1)

        @block.scalar
        def _(act):
            if late is not None:
                W.hi(act, late)
            for half in range(2):
                for tile, _ in tiles[half]:
                    if tile != last_tile:
                        W.split_after(act, tile, W.hi)

        @block.vector
        def _(dve):
            if late is not None:
                W.lo(dve, late)
            for half in range(2):
                for tile, _ in tiles[half][:-1]:
                    W.split_after(dve, tile, W.lo)
                for t in range(NT):
                    item, n = half * NT + t, rows_of(t)
                    dst = K.resid[0:n, t, half * BANK:(half + 1) * BANK]
                    dve.wait_ge(multiplied, item + 1)
                    if t == NT - 1 and half == 0:
                        W.split_after(dve, tiles[half][-1][0], W.lo)
                    dve.tensor_tensor(dst, dst, K.ps[0:n, item % 8, :], ALU.add).then_inc(added, 1)
            dve.wait_ge(added, 2 * NT)


def gate_up(nc, K, tag, act_hi, act_lo, first, n_chunks):
    S = {n: K.sem(f"{tag}_{n}") for n in ("multiplied", "silu_ok", "up_ok", "hi_ok", "chunk_ok")}
    W = K.weights
    late = W.take_late()
    W.leave(first + n_chunks + 1)
    H = TOK // 2
    LOOPS = (n_chunks - 3) // 2
    assert n_chunks == 2 * LOOPS + 3
    for n in range(n_chunks):
        W.used[first + n] = (S["multiplied"], n + 1)
    with ExitStack() as mem:
        silu = mem.enter_context(nc.sbuf_tensor(f"{tag}_silu", [P, 2, 2, H], F32))
        prod = mem.enter_context(nc.sbuf_tensor(f"{tag}_prod", [P, 2, 2, H], F32))
        block = mem.enter_context(nc.Block())

        def every_chunk(eng, step):
            with eng.Fori(0, LOOPS) as i:
                for x in range(2):
                    step(i * 2 + x, x, i)
            for n in range(2 * LOOPS, n_chunks):
                step(n, n % 2, None)

        def at(buf, n):
            start = ds(n * TOK, TOK) if not isinstance(n, int) else slice(n * TOK, (n + 1) * TOK)
            return buf[:, start].rearrange("p (f n) -> p f n", f=2)

        @block.sync
        def _(sp):
            W.load_up_to(sp, first + n_chunks + 2)

        @block.tensor
        def _(pe):
            def step(n, x, i):
                tile = first + x
                W.ready(pe, first, n)
                hi, lo = (v.rearrange("p (a k n) -> p a k n", a=2, k=KC) for v in W.parts_of(tile))
                pe.wait_ge(S["up_ok"], n + 1)
                for g in range(2):
                    for hf in range(2):
                        for k in range(KC):
                            cols = slice(hf * H, (hf + 1) * H)
                            ins = three_passes(pe, K.ps[:, 4 * x + 2 * g + hf, 0:H],
                                               (hi[:, g, k, :], lo[:, g, k, :]),
                                               (K.feat_hi[:, k, cols], K.feat_lo[:, k, cols]), k == 0, k == KC - 1)
                ins.then_inc(S["multiplied"], 1)
            every_chunk(pe, step)

        @block.scalar
        def _(act):
            def step(n, x, i):
                act.wait_ge(S["multiplied"], n + 1)
                act.wait_ge(S["up_ok"], n + 1)
                act.activation(silu[:, x, :, :], K.ps[:, 4 * x:4 * x + 2, 0:H], ACT.Silu).then_inc(S["silu_ok"], 1)
                if i is None:
                    if n < n_chunks - 1:
                        W.hi(act, first + n + 2)
                else:
                    W.hi(act, first + x + 2, i * 32)
                act.wait_ge(S["up_ok"], n + 3)
                act.activation(at(act_hi, n), prod[:, x, :, :], ACT.Copy).then_inc(S["hi_ok"], 1)
            if late is not None:
                W.hi(act, late)
            every_chunk(act, step)

        @block.vector
        def _(dve):
            dve.sem_inc(S["up_ok"], 2)

            def step(n, x, i):
                dve.wait_ge(S["silu_ok"], n + 1)
                dve.wait_ge(S["chunk_ok"], n + 1)
                dve.tensor_tensor(prod[:, x, :, :], silu[:, x, :, :], K.ps[:, 4 * x + 2:4 * x + 4, 0:H], ALU.mult)\
                   .then_inc(S["up_ok"], 1)
                if i is None:
                    if n < n_chunks - 1:
                        W.lo(dve, first + n + 2)
                else:
                    W.lo(dve, first + x + 2, i * 2)
                dve.wait_ge(S["hi_ok"], n + 1)
                dve.wait_ge(S["up_ok"], n + 3)
                dve.tensor_tensor(at(act_lo, n), prod[:, x, :, :], at(act_hi, n).bitcast(F32), ALU.subtract)\
                   .then_inc(S["chunk_ok"], 1)
            dve.sem_inc(S["chunk_ok"], 2)
            if late is not None:
                W.lo(dve, late)
            every_chunk(dve, step)


def to_mask(dve, dst, view):
    return dve.tensor_scalar(dst, view, TAKEN * 0.5, NEG, ALU.is_gt, ALU.mult)


class SampleTop:

    HALVES = 2 * (K_SAMPLE // 8)

    def __init__(self, nc, K, mem):
        self.K = K
        self.scores = mem.enter_context(nc.sbuf_tensor("sample_scores", [SAMP, KEYS], F32))
        self.best = mem.enter_context(nc.sbuf_tensor("sample_best", [SAMP, 8], F32))
        self.rows_in, self.masked, self.stored = (K.sem("sample_" + n) for n in ("rows_in", "masked", "mask_stored"))

    def half(self, dve, s, i):
        if i == 0:
            dve.wait_ge(self.rows_in, 16)
        s.wait()
        if i % 2 == 0:
            s.ok(dve.max(self.best[:, :], self.scores[:, :]))
        else:
            s.ok(dve.match_replace(self.scores[:, :], self.best[:, :], self.scores[:, :], TAKEN))
        if i == self.HALVES - 1:
            s.wait()
            to_mask(dve, self.scores[:, :], self.scores[:, :]).then_inc(self.masked, 1)

    def store(self, sp):
        sp.wait_ge(self.masked, 1)
        sp.dma_start(self.K.mask_rows.rearrange("b q k -> (b q) k"), self.scores[:, :]).then_inc(self.stored, 16)
        sp.wait_ge(self.stored, 16)


class IndexPages:

    def __init__(self, nc, K, mem):
        self.K = K
        self.rows = mem.enter_context(nc.sbuf_tensor("kidx_pages", [P, DEC_BATCH, N_PAGES, HEAD_DIM], F32))
        self.landed = K.sem("kidx_pages_landed")

    def load(self, sp, b):
        K = self.K
        for j in range(N_PAGES):
            n = b * N_PAGES + j
            pid = sp.value_load(K.pages[0:1, n:n + 1], min_val=0, max_val=K.cache_l1_kidx.shape[0] - 1)
            sp.dma_start(self.rows[:, b, j, :], K.cache_l1_kidx[ds(pid, 1), :, :]
                         .rearrange("a k d -> (a k) d")).then_inc(self.landed, 16)


def select_keys(nc, K, sample_top, kidx_pages):
    names = ("kidx_turned", "kt_ok", "p_scored", "p_relu", "p_ok", "s_scored", "s_relu", "s_mixed", "s_out",
             "row_stored", "chain", "weights_in", "weights_out", "q_ok")
    S = {n: K.sem("select_" + n) for n in names}
    row_stored = [K.sem(f"select_row_stored_{i}") for i in range(2)]
    with ExitStack() as mem:
        sb = lambda name, shape: mem.enter_context(nc.sbuf_tensor("select_" + name, shape, F32))
        relu = sb("relu", [P, 2, SEQ])
        kt = sb("kt", [P, 2, 4, P])
        qs = sb("qs", [P, DEC_BATCH, IDXH, DEC_SEQ])
        wt = sb("wt", [IDXH * DEC_SEQ, DEC_BATCH])
        mix = sb("mix", [IDXH * DEC_SEQ, DEC_BATCH, DEC_SEQ])
        srelu = sb("srelu", [IDXH * DEC_SEQ, 2, KEYS])
        srow = sb("srow", [DEC_SEQ, 2, KEYS])
        prompt = sb("prompt", [P, 3, SEQ])
        best = sb("best", [P, 3, 8])
        block = mem.enter_context(nc.Block())
        NEWS, NEWO = K.ps[0:32, 3, 0:DEC_SEQ], K.ps[0:DEC_SEQ, 6, 0:DEC_SEQ]
        p_units = [(qt, h) for qt in range(1, PT) for h in range(IDXH)]
        B = range(DEC_BATCH)

        @block.sync
        def _(sp):
            for b in B:
                if b >= 2:
                    sp.wait_ge(S["s_out"], b - 1)
                    sp.dma_start(K.idx_rows[b - 2], srow[:, b % 2, :]).then_inc(row_stored[b % 2], 16)
            for b in B[-2:]:
                sp.wait_ge(S["s_out"], b + 1)
                sp.dma_start(K.idx_rows[b], srow[:, b % 2, :]).then_inc(row_stored[b % 2], 16)
            for x in row_stored:
                sp.wait_ge(x, 16 * DEC_BATCH // 2)
            sp.dma_start(sample_top.scores[:, :], K.idx_rows.rearrange("b q k -> (b q) k"))\
              .then_inc(sample_top.rows_in, 16)

        @block.tensor
        def _(pe):
            for u, (qt, h) in enumerate(p_units):
                if u >= 2:
                    pe.wait_ge(S["p_relu"], u - 1)
                lo = (h % 2) * HEAD_DIM
                w = (qt + 1) * P
                pe.matmul(K.ps[:, 6 + u % 2, 0:w], K.qi[lo:lo + HEAD_DIM, h // 2, qt * P:w], K.ki[lo:lo + HEAD_DIM, 0:w],
                          start=True, stop=True).then_inc(S["p_scored"], 1)
            def turn(b):
                pe.wait_ge(kidx_pages.landed, 16 * N_PAGES * DEC_BATCH)
                if b >= 1:
                    pe.wait_ge(S["kt_ok"], b)
                for j in range(0, N_PAGES, 2):
                    ins = pe.transpose(K.ps[:, 0, j // 2 * P:(j // 2 + 1) * P],
                                       kidx_pages.rows[:, b, j:j + 2, :].rearrange("p a d -> p (a d)"), K.c("ident"))
                ins.then_inc(S["kidx_turned"], 1)

            def mix_heads(b):
                pe.wait_ge(S["s_relu"], 2 * b + 2)
                if b >= 1:
                    pe.wait_ge(S["s_out"], b)
                else:
                    pe.wait_ge(S["p_relu"], len(p_units))
                for dst, lo, hi in ((K.ps[0:DEC_SEQ, 4, :], 0, BANK), (K.ps[0:DEC_SEQ, 5, :], BANK, PAST_LEN),
                                    (NEWO, PAST_LEN, KEYS)):
                    ins = pe.matmul(dst, mix[:, b, :], srelu[:, b % 2, lo:hi], start=True, stop=True)
                ins.then_inc(S["s_mixed"], 1)
            turn(0)
            for b in B:
                pe.wait_ge(S["kt_ok"], b + 1)
                pe.wait_ge(S["q_ok"], 1)
                if b >= 1:
                    pe.wait_ge(S["s_relu"], 2 * b)
                for j in range(N_PAGES):
                    lo = (j % 2) * HEAD_DIM
                    pe.matmul(K.ps[0:32, 1 + j % 2, j // 2 * P:(j // 2 + 1) * P],
                              qs[lo:lo + HEAD_DIM, b, :, :].rearrange("p h q -> p (h q)"),
                              kt[lo:lo + HEAD_DIM, b % 2, j // 2, :], start=True, stop=True)
                pe.matmul(NEWS, qs[0:HEAD_DIM, b, :, :].rearrange("p h q -> p (h q)"),
                          K.ki[0:HEAD_DIM, SEQ + b * DEC_SEQ:SEQ + (b + 1) * DEC_SEQ], start=True, stop=True)\
                  .then_inc(S["s_scored"], 1)
                if b + 1 < DEC_BATCH:
                    turn(b + 1)
                if b >= 1:
                    mix_heads(b - 1)
            mix_heads(DEC_BATCH - 1)

        @block.scalar
        def _(act):
            act.dma_start(K.idx_weights, K.wi[0:SAMP, PT, :]).then_inc(S["weights_out"], 16)
            act.wait_ge(S["weights_out"], 16)
            with nc.allow_non_contiguous_dma(reason="256 words"):
                for h in range(IDXH):
                    act.dma_start(wt[h * DEC_SEQ:(h + 1) * DEC_SEQ, :],
                                   K.idx_weights[:, h:h + 1].rearrange("(b q) a -> q (b a)", b=DEC_BATCH))\
                        .then_inc(S["weights_in"], 16)
            for u, (qt, h) in enumerate(p_units):
                w = (qt + 1) * P
                act.wait_ge(S["p_scored"], u + 1)
                if u >= 2:
                    act.wait_ge(S["p_ok"], u - 1)
                act.activation(relu[:, u % 2, 0:w], K.ps[:, 6 + u % 2, 0:w], ACT.Relu).then_inc(S["p_relu"], 1)
            for b in B:
                act.wait_ge(S["kidx_turned"], b + 1)
                if b >= 2:
                    act.wait_ge(S["s_scored"], b - 1)
                act.activation(kt[:, b % 2, :, :], K.ps[:, 0, :].rearrange("p (j n) -> p j n", j=4), ACT.Copy)\
                   .then_inc(S["kt_ok"], 1)
                act.wait_ge(S["s_scored"], b + 1)
                if b >= 2:
                    act.wait_ge(S["s_mixed"], b - 1)
                act.activation(srelu[:, b % 2, 0:PAST_LEN].rearrange("p (j a k) -> p a j k", a=2, k=P),
                               K.ps[0:32, 1:3, :].rearrange("p a (j k) -> p a j k", k=P), ACT.Relu)\
                   .then_inc(S["s_relu"], 1)
                act.activation(srelu[:, b % 2, PAST_LEN:KEYS], NEWS, ACT.Relu).then_inc(S["s_relu"], 1)

        @block.vector
        def _(dve):
            s = Steps(dve, S["chain"])
            for half in range(2):
                for par in range(2):
                    src = K.qi[par * HEAD_DIM:(par + 1) * HEAD_DIM, :, SEQ:TOK].rearrange(
                        "p c (b q) -> p b c q", b=DEC_BATCH)
                    dst = qs[half * HEAD_DIM:(half + 1) * HEAD_DIM, :, par:IDXH:2, :]
                    s.ok(dve.tensor_copy(dst, src))
            dve.wait_ge(S["weights_in"], 16 * IDXH)
            s.ok(dve.tensor_tensor(mix[:, :, :], bc(K.c("idx_sel")[0:32, :], 1, DEC_BATCH),
                                   bc(wt[:, :], 2, DEC_SEQ), ALU.mult))
            s.wait()
            dve.sem_inc(S["q_ok"], 1)
            for u, (qt, h) in enumerate(p_units):
                w = (qt + 1) * P
                dst, src, wh = prompt[:, qt - 1, 0:w], relu[:, u % 2, 0:w], K.wi[:, qt, h:h + 1]
                dve.wait_ge(S["p_relu"], u + 1)
                if h == 0:
                    dve.tensor_scalar(dst, src, wh, None, ALU.mult).then_inc(S["p_ok"], 1)
                else:
                    dve.wait_ge(S["p_ok"], u)
                    dve.scalar_tensor_tensor(out=dst, in0=src, scalar=wh, in1=dst, op0=ALU.mult, op1=ALU.add)\
                       .then_inc(S["p_ok"], 1)
                if h == IDXH - 1:
                    dve.wait_ge(S["p_ok"], u + 1)
                    s.ok(dve.tensor_tensor(dst[:, qt * P:w], dst[:, qt * P:w], K.c("causal"), ALU.add))
            views = [prompt[:, qt - 1, 0:(qt + 1) * P] for qt in range(1, PT)]
            rounds = K_PROMPT // 8
            for b in B:
                dve.wait_ge(S["s_mixed"], b + 1)
                if b >= 2:
                    dve.wait_ge(row_stored[b % 2], 16 * (b // 2))
                s.ok(dve.tensor_copy(srow[:, b % 2, 0:PAST_LEN].rearrange("p (g k) -> p g k", g=2),
                                     K.ps[0:DEC_SEQ, 4:6, :]))
                s.ok(dve.tensor_tensor(srow[:, b % 2, PAST_LEN:KEYS], NEWO, K.c("new_mask")[0:DEC_SEQ, :], ALU.add))
                s.wait()
                dve.sem_inc(S["s_out"], 1)
                for _ in range(rounds * b // DEC_BATCH, rounds * (b + 1) // DEC_BATCH):
                    for i, v in enumerate(views):
                        s.ok(dve.max(best[:, i, :], v))
                    s.wait()
                    for i, v in enumerate(views):
                        s.ok(dve.match_replace(v, best[:, i, :], v, TAKEN))
                    s.wait()
            s.ok(dve.tensor_copy(K.mask[:, 0, 0:P], K.c("causal")))
            for i, v in enumerate(views):
                s.ok(to_mask(dve, K.mask[:, i + 1, 0:(i + 2) * P], v))
            s.wait()


def store_results(nc, K):
    done = K.sem("results_stored")
    with nc.Block() as block:
        @block.sync
        def _(sp):
            sp.dma_start(K.y_prompt[0].rearrange("(t p) d -> p t d", p=P), K.resid[:, 0:PT, :]).then_inc(done, 16)
            sp.dma_start(K.y_sample.rearrange("b t d -> (b t) d"), K.resid[0:SAMP, PT, :]).then_inc(done, 16)
            sp.wait_ge(done, 32)


def two_layers(nc, K):
    W = K.weights = Weights(K, lambda name: nc.alloc_semaphore(name=name))
    cuts0 = dict(qa=0, ka=512, va=1024, qb=1544, kb=2056, vb=2568, fa=1536)

    def by_halves(w, c0, width):
        return [(W.add(column_tile(w, k, 4, c0, width)), range(k, k + 4)) for k in (0, 4)]

    l0 = {n: by_halves(K.w_in0, c, 512) if n != "fa" else [(W.add(column_tile(K.w_in0, 0, KC, c, FOX)), range(KC))]
          for n, c in cuts0.items()}

    FH = FC // 2

    def products(w_out, wg, wu, wd):
        out = [by_halves(w_out, h * BANK, BANK) for h in range(2)]
        halves = []
        for f in range(2):
            gu = [W.add(gate_up_tile(wg, wu, (f * FH + i) * P)) for i in range(FH)]
            down = [[(W.add(column_tile(wd, f * FH + k, min(4, FH - k), h * BANK, BANK)), range(k, min(k + 4, FH)))
                     for k in range(0, FH, 4)] for h in range(2)]
            halves.append((gu[0], down))
        return out, halves

    out0, ffn0 = products(K.w_out0, K.w_gate0, K.w_up0, K.w_down0)
    l1 = {n: by_halves(K.w_in1, c, w) for n, c, w in
          (("idx", 1536, 324), ("kv", 1024, 512), ("q0", 0, 512), ("q1", 512, 512))}
    out1, ffn1 = products(K.w_out1, K.w_gate1, K.w_up1, K.w_down1)

    load_inputs(nc, K)

    def tok_rows(prompt, sample, c0, c1):
        def at(t):
            return prompt[t * P:(t + 1) * P, c0:c1] if t < PT else sample[:, c0:c1]
        return at

    def plain(j):
        return lambda r: r[:, j * P:(j + 1) * P]

    def to(prompt, sample, c):
        return lambda t: prompt[:, c, t * P:(t + 1) * P] if t < PT else sample[:, c, :]

    def ffn(tag, gain, halves):
        norm_to_features(nc, K, gain, tag + "n")
        with ExitStack() as mem:
            act_hi, act_lo = (mem.enter_context(nc.sbuf_tensor(f"{tag}_act_{x}", [P, FH * TOK], F32R)) for x in ("hi", "lo"))

            def lhs(c, t):
                cols = slice(c * TOK + t * P, c * TOK + t * P + rows_of(t))
                return act_hi[:, cols], act_lo[:, cols]
            for f, (gu, down) in enumerate(halves):
                gate_up(nc, K, f"{tag}g{f}", act_hi, act_lo, gu, FH)
                add_product(nc, K, f"{tag}d{f}", lhs, down)

    def feat_lhs(c, t):
        cols = slice(t * P, t * P + rows_of(t))
        return K.feat_hi[:, c, cols], K.feat_lo[:, c, cols]

    norm_to_features(nc, K, 0, "n0")
    with ExitStack() as layer:
        sb = lambda mem, name, shape: mem.enter_context(nc.sbuf_tensor(name, shape, F32))
        qs, ks = sb(layer, "qs0", [P, KC, SAMP]), sb(layer, "ks0", [P, KC, SAMP])
        K.logf = sb(layer, "logf", [P, NT, FOX])
        with ExitStack() as pr:
            qp, kp = sb(pr, "qp0", [P, KC, SEQ]), sb(pr, "kp0", [P, KC, SEQ])
            vp = sb(pr, "vp0", [P, PT, D_MODEL])
            vs = sb(pr, "vs0", [SAMP, D_MODEL])

            def q_part(name, norm, rope, c):
                return Part(l0[name], 512, 512, norm, rope,
                            turns=[(plain(j), to(qp, qs, c + j), SCALE) for j in range(4)])

            def k_part(name, norm, rope, c):
                return Part(l0[name], 512, 512, norm, rope,
                            stores=[(slice(0, 512), tok_rows(K.p_l0_k, K.s_l0_k, c * P, c * P + 512))],
                            turns=[(plain(j), to(kp, ks, c + j), 1.0) for j in range(4)])

            def v_part(name, c0):
                rows = tok_rows(K.p_l0_v, K.s_l0_v, c0, c0 + 512)
                return Part(l0[name], 512, copies=[(
                    slice(0, 512), lambda t: vp[:, t, c0:c0 + 512] if t < PT else vs[:, c0:c0 + 512],
                    rows, rows, None)])

            f_rows = tok_rows(K.p_l0_logf, K.s_l0_logf, 0, FOX)

            parts = [q_part("qa", 0, False, 0), k_part("ka", 1, False, 0), v_part("va", 0),
                     q_part("qb", 2, True, 4), k_part("kb", 3, True, 4), v_part("vb", 512)]
            project(nc, K, parts, "p0")
            forget_gates(nc, K, l0["fa"][0][0], f_rows)
            forget_sums(nc, K)

            def lo(h):
                return slice((h % 2) * HEAD_DIM, (h % 2 + 1) * HEAD_DIM)

            def v_cols(h):
                return slice(h * HEAD_DIM, (h + 1) * HEAD_DIM) if h < FOX else \
                    slice(512 + (h - FOX) // 2 * P, 512 + ((h - FOX) // 2 + 1) * P)
            prompt_attention(
                nc, K, "a0", q_at=lambda h, qt: qp[lo(h), h // 2, qt * P:(qt + 1) * P], k_at=lambda h: kp[lo(h), h // 2, :],
                v_at=lambda h, j: vp[:, j, v_cols(h)],
                bias_at=lambda h, qt: K.minus_c[:, h, 0:(qt + 1) * P] if h < FOX else None, diag=True,
                out_at=lambda h, qt: K.att[:, qt, v_cols(h)], second=lambda h: h >= FOX and h % 2 == 1)

        def fill_q0(dve, qz, b, ok):
            flat = qz[:, :, :].rearrange("p c n -> p (c n)")
            for half in range(2):
                rows = slice(half * HEAD_DIM, (half + 1) * HEAD_DIM)
                for c in range(KC):
                    col = c * P + 16 * c + 8 * half
                    ins = dve.tensor_copy(flat[rows, col:col + DEC_SEQ], qs[rows, c, ds(b * DEC_SEQ, DEC_SEQ)])
            ins.then_inc(ok, 1)

        def out0_fn(dve, OT, b):
            now = ds(b * DEC_SEQ, DEC_SEQ)
            for x in range(2):
                o = OT[:, x, :].rearrange("p (i x a q) -> p i x a q", i=4, x=2, a=2)[:, :, x]
                for half in range(2):
                    rows = slice(half * HEAD_DIM, (half + 1) * HEAD_DIM)
                    dve.tensor_copy(K.feat_s[rows, x:4:2, now], o[rows, 0:2, half, :])
                ins = dve.tensor_reduce(K.feat_s[:, 4 + x:8:2, now], o[:, 2:4].rearrange("p i a q -> p i q a"), AX, ALU.add)
            return ins

        sample_attention(
            nc, K, "s0", K.cache_l0_k, K.cache_l0_v, lambda b: K.s_l0_v[ds(b * DEC_SEQ, DEC_SEQ), :],
            lambda b: K.fox_rows[ds(b, 1), :, :].rearrange("a h k -> (a h) k"), K.c("fox_sel")[0:FOX, :], D_MODEL, KC, fill_q0,
            ks, K.c("new_mask"), K.coef[:, 0:1], out0_fn)
        sample_subln(nc, K)
    turn_attention(nc, K, K.att, "t0", True)
    add_product(nc, K, "o0", feat_lhs, out0)
    ffn("f0", 1, ffn0)

    renew_semaphores(nc, K)

    norm_to_features(nc, K, 2, "n1")
    with ExitStack() as layer:
        sb = lambda mem, name, shape: mem.enter_context(nc.sbuf_tensor(name, shape, F32))
        qs, ks = sb(layer, "qs1", [P, KC, SAMP]), sb(layer, "ks1", [P, 2, SAMP])
        vs = sb(layer, "vs1", [SAMP, 256])
        with ExitStack() as pr:
            qp, kp = sb(pr, "qp1", [P, KC, SEQ]), sb(pr, "kp1", [P, 2, SEQ])
            vp = sb(pr, "vp1", [P, PT, 256])
            K.qi = sb(pr, "qi", [P, 2, TOK])
            K.ki = sb(pr, "ki", [P, TOK])
            K.wi = sb(pr, "wi", [P, NT, IDXH])
            span = lambda t: slice(t * P, t * P + rows_of(t))
            idx_rows = tok_rows(K.p_l1_kidx, K.s_l1_kidx, 0, HEAD_DIM)
            parts = [Part(l1["idx"], 324, 320, None, True,
                          stores=[(slice(256, 320), idx_rows)],
                          turns=[(plain(0), lambda t: K.qi[:, 0, span(t)], 1.0),
                                 (plain(1), lambda t: K.qi[:, 1, span(t)], 1.0),
                                 (plain(2), lambda t: K.ki[:, span(t)], 1.0)],
                          copies=[(slice(320, 324), lambda t: K.wi[0:rows_of(t), t, :], None, None,
                                   lambda dve, dst, src, s: dve.tensor_scalar(dst, src, SCALE * IDXH ** -0.5, None,
                                                                              ALU.mult))]),
                     Part(l1["kv"], 512, 256, 5, True,
                          stores=[(slice(0, 256), tok_rows(K.p_l1_k, K.s_l1_k, 0, 256))],
                          turns=[(plain(j), to(kp, ks, j), 1.0) for j in range(2)],
                          copies=[(slice(256, 512), lambda t: vp[:, t, :] if t < PT else vs[:, :],
                                   tok_rows(K.p_l1_v, K.s_l1_v, 0, 256), tok_rows(K.p_l1_v, K.s_l1_v, 0, 256), None)])]

            for g in range(2):
                parts.append(Part(l1[f"q{g}"], 512, 512, 4, True, paired=True,
                                  turns=[(plain(r), to(qp, qs, 4 * g + r), SCALE) for r in range(4)]))
            sample_top = SampleTop(nc, K, pr)
            with ExitStack() as idx:
                kidx_pages = IndexPages(nc, K, idx)
                project(nc, K, parts, "p1", aside=kidx_pages.load)
                select_keys(nc, K, sample_top, kidx_pages)

            def kv_half(h):
                a = h // 4 % 2
                return slice(a * HEAD_DIM, (a + 1) * HEAD_DIM)
            prompt_attention(
                nc, K, "a1", q_at=lambda h, qt: qp[kv_half(h), 4 * (h // 8) + h % 4, qt * P:(qt + 1) * P],
                k_at=lambda h: kp[kv_half(h), h // 8, :],
                v_at=lambda h, j: vp[:, j, h // 4 * HEAD_DIM:(h // 4 + 1) * HEAD_DIM],
                bias_at=lambda h, qt: K.mask[:, qt, 0:(qt + 1) * P], diag=False,
                out_at=lambda h, qt: K.att[:, qt, h * HEAD_DIM:(h + 1) * HEAD_DIM], second=lambda h: False,
                sample_top=sample_top)

        def fill_q1(dve, qz, b, ok):
            for half in range(2):
                rows = slice(half * HEAD_DIM, (half + 1) * HEAD_DIM)
                for g in range(2):
                    col = (8 * g + 4 * half) * DEC_SEQ
                    dst = qz[rows, g, col:col + 4 * DEC_SEQ].rearrange("p (r q) -> p r q", r=4)
                    ins = dve.tensor_copy(dst, qs[rows, 4 * g:4 * g + 4, ds(b * DEC_SEQ, DEC_SEQ)])
            ins.then_inc(ok, 1)

        def out1_fn(dve, OT, b):
            o = OT[0:HEAD_DIM, 0, :].rearrange("p (c a q) -> p c a q", c=KC, a=2)
            for half in range(2):
                ins = dve.tensor_copy(K.feat_s[half * HEAD_DIM:(half + 1) * HEAD_DIM, :, ds(b * DEC_SEQ, DEC_SEQ)],
                                      o[:, :, half, :])
            return ins

        sample_attention(
            nc, K, "s1", K.cache_l1_k.rearrange("n k g d -> n k (g d)"), K.cache_l1_v.rearrange("n k g d -> n k (g d)"),
            lambda b: K.s_l1_v[ds(b * DEC_SEQ, DEC_SEQ), :],
            lambda b: K.mask_rows[ds(b, 1), :, :].rearrange("a q k -> (a q) k"), K.c("query_sel")[0:DEC_SEQ, :], 256, 2, fill_q1,
            ks, None, None, out1_fn)
    turn_attention(nc, K, K.att, "t1", False)
    add_product(nc, K, "o1", feat_lhs, out1)
    ffn("f1", 3, ffn1)
    store_results(nc, K)


def renew_semaphores(nc, K):
    numbers = sorted(h.num for h in K.phase_sems)
    runs = []
    for n in numbers:
        if runs and runs[-1][1] == n:
            runs[-1][1] = n + 1
        else:
            runs.append([n, n + 1])
    with nc.Block() as block:
        @block.gpsimd
        def _(pool):
            for lo, hi in runs:
                pool.sem_clear(range(lo, hi))
    for h in K.phase_sems:
        nc.release_semaphore(h)
    K.phase_sems = []


def forget_gates(nc, K, tile, rows):
    S = {n: K.sem("logsig_" + n) for n in ("multiplied", "copied", "turned", "added", "act", "dve", "stored")}
    W = K.weights
    W.used[tile] = (S["multiplied"], 1)
    H = TOK // 2
    with ExitStack() as mem:
        by_gate = mem.enter_context(nc.sbuf_tensor("logsig_by_gate", [FOX, TOK], F32))
        low = mem.enter_context(nc.sbuf_tensor("logsig_low", [P, NT, FOX], F32))
        e = mem.enter_context(nc.sbuf_tensor("logsig_e", [P, NT, FOX], F32))
        block = mem.enter_context(nc.Block())
        parts = [lambda x: x[:, 0:PT, :], lambda x: x[0:SAMP, PT, :]]
        TOKENS = K.ps[:, 2, 0:NT * FOX].rearrange("p (t h) -> p t h", h=FOX)

        @block.tensor
        def _(pe):
            W.ready(pe, tile)
            hi, lo = (x[:, 0:KC * FOX].rearrange("p (k n) -> p k n", n=FOX) for x in W.parts_of(tile))
            for half in range(2):
                cols = slice(half * H, (half + 1) * H)
                for k in range(KC):
                    ins = three_passes(pe, K.ps[0:FOX, half, 0:H], (hi[:, k, :], lo[:, k, :]),
                                       (K.feat_hi[:, k, cols], K.feat_lo[:, k, cols]), k == 0, k == KC - 1)
            ins.then_inc(S["multiplied"], 1)
            pe.wait_ge(S["copied"], 1)
            for t in range(NT):
                n = rows_of(t)
                ins = pe.transpose(TOKENS[0:n, t, :], by_gate[:, t * P:t * P + n], K.c("ident")[0:FOX, 0:FOX])
            ins.then_inc(S["turned"], 1)

        @block.scalar
        def _(act):
            W.split_after(act, tile, W.hi)
            act.wait_ge(S["added"], 2)
            for i, (f, src) in enumerate(((ACT.Abs, K.logf), (ACT.Exp, e), (ACT.Ln, e))):
                if i:
                    act.wait_ge(S["act"], 2 * i)
                if i == 2:
                    act.wait_ge(S["dve"], 4)
                for p in parts:
                    act.activation(p(e), p(src), f, scale=-1.0 if f == ACT.Exp else 1.0).then_inc(S["act"], 1)

        @block.vector
        def _(dve):
            dve.wait_ge(S["multiplied"], 1)
            dve.tensor_copy(by_gate[:, :].rearrange("p (a n) -> p a n", a=2), K.ps[0:FOX, 0:2, 0:H])\
               .then_inc(S["copied"], 1)
            W.split_after(dve, tile, W.lo)
            dve.wait_ge(S["turned"], 1)
            dve.tensor_tensor(K.logf[:, 0:PT, :], TOKENS[:, 0:PT, :], bc(K.bias_f[:, :], 1, PT), ALU.add)\
               .then_inc(S["added"], 1)
            dve.tensor_tensor(K.logf[0:SAMP, PT, :], TOKENS[0:SAMP, PT, :], K.bias_f[0:SAMP, :], ALU.add)\
               .then_inc(S["added"], 1)
            dve.wait_ge(S["added"], 2)
            for p in parts:
                dve.tensor_scalar(p(low), p(K.logf), 0.0, None, ALU.min).then_inc(S["dve"], 1)
            dve.wait_ge(S["act"], 4)
            for p in parts:
                dve.tensor_scalar(p(e), p(e), 1.0, None, ALU.add).then_inc(S["dve"], 1)
            dve.wait_ge(S["dve"], 2)
            dve.wait_ge(S["act"], 6)
            for p in parts:
                dve.tensor_tensor(p(K.logf), p(low), p(e), ALU.subtract).then_inc(S["dve"], 1)

        @block.sync
        def _(sp):
            W.load_up_to(sp, tile + 2)
            sp.wait_ge(S["dve"], 6)
            for t in range(NT):
                sp.dma_start(rows(t), K.logf[0:rows_of(t), t, :]).then_inc(S["stored"], 16)
            sp.wait_ge(S["stored"], 16 * NT)


def build(nc, ins, outs, const_in):
    with ExitStack() as ctx:
        sb = lambda name, shape, dt=F32: ctx.enter_context(nc.sbuf_tensor(name, shape, dt))
        K = Kernel()
        K.x_prompt, K.x_sample, K.cache_l0_k = ins["x_prompt"], ins["x_sample"], ins["cache_l0_k"]
        K.cache_l0_v, K.cache_l0_logf, K.cache_l1_k = ins["cache_l0_v"], ins["cache_l0_logf"], ins["cache_l1_k"]
        K.cache_l1_v, K.cache_l1_kidx, K.page_table = ins["cache_l1_v"], ins["cache_l1_kidx"], ins["page_table"]
        K.b_f0, K.subln0, K.w_in0 = ins["b_f0"], ins["subln0"], ins["w_in0"]
        K.w_out0, K.w_gate0, K.w_up0 = ins["w_out0"], ins["w_gate0"], ins["w_up0"]
        K.w_down0, K.w_in1, K.w_out1 = ins["w_down0"], ins["w_in1"], ins["w_out1"]
        K.w_gate1, K.w_up1, K.w_down1 = ins["w_gate1"], ins["w_up1"], ins["w_down1"]
        flat = lambda x: x.rearrange("b t d -> (b t) d")
        heads_flat = lambda x: x.rearrange("b t g d -> (b t) (g d)")
        K.y_prompt, K.y_sample = outs["y_prompt"], outs["y_sample"]
        K.p_l0_k, K.p_l0_v, K.p_l0_logf = flat(outs["p_l0_k"]), flat(outs["p_l0_v"]), flat(outs["p_l0_logf"])
        K.p_l1_kidx, K.s_l0_k, K.s_l0_v = flat(outs["p_l1_kidx"]), flat(outs["s_l0_k"]), flat(outs["s_l0_v"])
        K.s_l0_logf, K.s_l1_kidx = flat(outs["s_l0_logf"]), flat(outs["s_l1_kidx"])
        K.p_l1_k, K.p_l1_v, K.s_l1_k = heads_flat(outs["p_l1_k"]), heads_flat(outs["p_l1_v"]), heads_flat(outs["s_l1_k"])
        K.s_l1_v = heads_flat(outs["s_l1_v"])
        K.phase_sems = []

        def sem(name):
            handle = nc.alloc_semaphore(name=name)
            K.phase_sems.append(handle)
            return handle
        K.sem = sem
        K.const_in = const_in
        K.head_gains = [ins[n] for n in ("qn_fox0", "kn_fox0", "qn_diff0", "kn_diff0", "qn_dsa1", "kn_dsa1")]
        K.norm_gains = [ins[n] for n in ("attn_norm0", "ffn_norm0", "attn_norm1", "ffn_norm1")]
        K.lam_vecs = [ins[n] for n in ("lam_q1_0", "lam_k1_0", "lam_q2_0", "lam_k2_0")]
        scratch = lambda name, shape: nc.dram_tensor(name, shape, F32, kind="Internal").ap()
        K.prompt_rows = scratch("prompt_rows", (FOX, SEQ))
        K.fox_rows = scratch("fox_rows", (DEC_BATCH, FOX, KEYS))
        K.idx_rows = scratch("idx_rows", (DEC_BATCH, DEC_SEQ, KEYS))
        K.mask_rows = scratch("mask_rows", (DEC_BATCH, DEC_SEQ, KEYS))
        K.idx_weights = scratch("idx_weights", (SAMP, IDXH))
        K.ps = ctx.enter_context(nc.psum_tensor("ps", [P, 8, BANK], F32))
        K.resid = sb("resid", [P, NT, D_MODEL])
        feat_hi_at = nc.sbuf_base
        K.feat_hi = sb("feat_hi", [P, KC, TOK], F32R)
        feat_lo_at = nc.sbuf_base
        K.feat_lo = sb("feat_lo", [P, KC, TOK], F32R)
        K.att = nc.alloc_sbuf_tensor_at("att", [P, PT, D_MODEL], F32, offset=feat_lo_at)
        K.minus_c = nc.alloc_sbuf_tensor_at("minus_c", [P, FOX, SEQ], F32, offset=feat_hi_at)
        K.mask = nc.alloc_sbuf_tensor_at("mask", [P, PT, SEQ], F32, offset=feat_hi_at)
        K.kt0 = nc.alloc_sbuf_tensor_at("kt0", [P, 2 * Weights.SIZE], F32, offset=feat_hi_at)
        K.feat_s = sb("feat_s", [P, KC, SAMP])
        K.w_raw = sb("w_raw", [P, 2, Weights.SIZE])
        K.w_hi, K.w_lo = sb("w_hi", [P, 2, Weights.SIZE], F32R), sb("w_lo", [P, 2, Weights.SIZE], F32R)
        K.const = sb("const", [P, const_in.shape[1]])
        K.c = lambda name: K.const[:, CONST_AT[name][0]:CONST_AT[name][0] + CONST_AT[name][1]]
        K.head_gain = sb("head_gain", [P, 6, HEAD_DIM])
        K.subln_row, K.subln_col = sb("subln_row", [P, P]), sb("subln_col", [P, 1])
        K.subln_row8, K.subln_col8 = sb("subln_row8", [P, P]), sb("subln_col8", [P, 1])
        K.bias_f = sb("bias_f", [P, FOX])
        K.pages = sb("pages", [1, DEC_BATCH * N_PAGES], I32)
        K.page_rows = sb("page_rows", [DEC_BATCH * N_PAGES, 1], I32)
        K.lams = sb("lams", [P, 4, HEAD_DIM])
        K.lam, K.minus_lam, K.coef = sb("lam", [P, 1]), sb("minus_lam", [P, 1]), sb("coef", [P, 1])
        two_layers(nc, K)


_INS = ['x_prompt', 'x_sample', 'cache_l0_k', 'cache_l0_v', 'cache_l0_logf', 'cache_l1_k', 'cache_l1_v',
        'cache_l1_kidx', 'page_table', 'attn_norm0', 'w_in0', 'b_f0', 'qn_fox0', 'kn_fox0', 'qn_diff0', 'kn_diff0',
        'lam_q1_0', 'lam_k1_0', 'lam_q2_0', 'lam_k2_0', 'subln0', 'w_out0', 'ffn_norm0', 'w_gate0', 'w_up0', 'w_down0',
        'attn_norm1', 'w_in1', 'qn_dsa1', 'kn_dsa1', 'w_out1', 'ffn_norm1', 'w_gate1', 'w_up1', 'w_down1']
_OUTS = {'y_prompt': (1, SEQ, D_MODEL), 'y_sample': (DEC_BATCH, DEC_SEQ, D_MODEL),
         'p_l0_k': (1, SEQ, 1024), 'p_l0_v': (1, SEQ, 1024), 'p_l0_logf': (1, SEQ, FOX),
         'p_l1_k': (1, SEQ, KVH, HEAD_DIM), 'p_l1_v': (1, SEQ, KVH, HEAD_DIM), 'p_l1_kidx': (1, SEQ, HEAD_DIM),
         's_l0_k': (DEC_BATCH, DEC_SEQ, 1024), 's_l0_v': (DEC_BATCH, DEC_SEQ, 1024),
         's_l0_logf': (DEC_BATCH, DEC_SEQ, FOX), 's_l1_k': (DEC_BATCH, DEC_SEQ, KVH, HEAD_DIM),
         's_l1_v': (DEC_BATCH, DEC_SEQ, KVH, HEAD_DIM), 's_l1_kidx': (DEC_BATCH, DEC_SEQ, HEAD_DIM)}


def kernel(**inputs):
    import numpy as _np
    import concourse.bacc as _bacc
    from concourse import mybir as _mybir
    from concourse.bass_utils import run_bass_kernel_spmd as _run

    nc = _bacc.Bacc("TRN2", target_bir_lowering=False, num_devices=1)
    arrays, ins, outs = {"in_const_dram": CONST}, {}, {}
    for name in _INS:
        a = _np.ascontiguousarray(inputs[name])
        arrays[f"in_{name}_dram"] = a
        ins[name] = nc.dram_tensor(f"in_{name}_dram", a.shape, _mybir.dt.from_np(a.dtype), kind="ExternalInput").ap()
    const_in = nc.dram_tensor("in_const_dram", CONST.shape, _mybir.dt.float32, kind="ExternalInput").ap()
    for name, shape in _OUTS.items():
        outs[name] = nc.dram_tensor(f"out_{name}_dram", shape, _mybir.dt.float32, kind="ExternalOutput").ap()
    build(nc, ins, outs, const_in)
    r = _run(nc, [arrays], core_ids=[0])
    return tuple(r.results[0][f"out_{name}_dram"] for name in _OUTS)
```
